# Optimizing a Trainium2 kernel written in Bass

```python
import math
import jax, jax.numpy as jnp
from jax import lax
import numpy as np

D_MODEL = 1024
BATCH = 1
SEQ = 256
DEPTH = 2

CHUNK = 64
N_MEM = 256
MEM_HEADS = 4
MEM_HEAD_DIM = D_MODEL // MEM_HEADS
D_MIX = D_MODEL
POOL_WINDOWS = (2, 4, 8, 16)
POOL_WIDTH = D_MIX // 4
POOL_GROUP = POOL_WIDTH // len(POOL_WINDOWS)
QK_NOPE = 128
QK_ROPE = 64
V_HEAD = 128
MLA_HEADS = (D_MIX - POOL_WIDTH) // V_HEAD
Q_LORA = 256
KV_LORA = 128
ROPE_BASE = 10000.0
D_FF = 2816
Q_BLOCK = 128
D_IN = POOL_WIDTH + Q_LORA + KV_LORA + QK_ROPE
ALPHA = (2 * DEPTH) ** 0.25
BETA = (8 * DEPTH) ** -0.25
LN_EPS = 1e-5
RMS_EPS = 1e-6
NEG_INF = -1e30

kernel_name = 'hybrid_pool_mla_macaron_deepnorm'

def layer_norm(x, g, b):
    xf = x.astype(jnp.float32)
    mu = jnp.mean(xf, axis=-1, keepdims=True)
    var = jnp.mean(jnp.square(xf - mu), axis=-1, keepdims=True)
    y = (xf - mu) * lax.rsqrt(var + LN_EPS) * g.astype(jnp.float32) + b.astype(jnp.float32)
    return y.astype(x.dtype)

def rms_norm(x, g):
    xf = x.astype(jnp.float32)
    y = xf * lax.rsqrt(jnp.mean(jnp.square(xf), axis=-1, keepdims=True) + RMS_EPS)
    return (y * g.astype(jnp.float32)).astype(x.dtype)

def swiglu(x, w13, w2):
    gate, up = jnp.split(x @ w13, 2, axis=-1)
    return (jax.nn.silu(gate) * up) @ w2

def rope(x, positions):
    half = QK_ROPE // 2
    inv_freq = ROPE_BASE ** (-jnp.arange(half, dtype=jnp.float32) / half)
    ang = positions.astype(jnp.float32)[..., None] * inv_freq
    ang = ang.reshape(ang.shape[:2] + (1,) * (x.ndim - 3) + (half,))
    cos, sin = jnp.cos(ang), jnp.sin(ang)
    xf = x.astype(jnp.float32)
    x1, x2 = xf[..., :half], xf[..., half:]
    out = jnp.concatenate([x1 * cos - x2 * sin, x2 * cos + x1 * sin], axis=-1)
    return out.astype(x.dtype)

def pool_mixer(u, pool_w, pool_scale):
    B, S, _ = u.shape
    uf = u.astype(jnp.float32)
    cs = jnp.cumsum(uf, axis=1)
    t = jnp.arange(S)
    means = []
    for g, w in enumerate(POOL_WINDOWS):
        csg = cs[..., g * POOL_GROUP:(g + 1) * POOL_GROUP]
        prev = jnp.pad(csg[:, :S - w], ((0, 0), (w, 0), (0, 0)))
        cnt = jnp.minimum(t + 1, w).astype(jnp.float32)[None, :, None]
        means.append((csg - prev) / cnt)
    d = (jnp.concatenate(means, axis=-1) - uf).astype(u.dtype)
    d = d.reshape(B, S, len(POOL_WINDOWS), POOL_GROUP)
    y = jnp.einsum('bsgc,gcd->bsgd', d, pool_w).reshape(B, S, POOL_WIDTH)
    return y * pool_scale

def mla_mixer(c_q, c_kv, k_pe, positions, q_norm_g, w_uq, kv_norm_g, w_ukv):
    B, S, _ = c_q.shape
    H = MLA_HEADS
    q = (rms_norm(c_q, q_norm_g) @ w_uq).reshape(B, S, H, QK_NOPE + QK_ROPE)
    q = jnp.concatenate([q[..., :QK_NOPE], rope(q[..., QK_NOPE:], positions)], axis=-1)
    kv = (rms_norm(c_kv, kv_norm_g) @ w_ukv).reshape(B, S, H, QK_NOPE + V_HEAD)
    k_nope, v = kv[..., :QK_NOPE], kv[..., QK_NOPE:]
    k_rot = rope(k_pe, positions)
    k = jnp.concatenate([k_nope, jnp.broadcast_to(k_rot[:, :, None, :], (B, S, H, QK_ROPE))], axis=-1)
    scale = (QK_NOPE + QK_ROPE) ** -0.5
    nb = S // Q_BLOCK
    q_blocks = q.reshape(B, nb, Q_BLOCK, H, QK_NOPE + QK_ROPE).transpose(1, 0, 2, 3, 4)
    q_idx = jnp.arange(S).reshape(nb, Q_BLOCK)
    k_chunk = jnp.arange(S) // CHUNK

    def attend(args):
        qb, qi = args
        s = jnp.einsum('bqhd,bkhd->bhqk', qb, k, preferred_element_type=jnp.float32) * scale
        mask = (qi[:, None] // CHUNK) >= k_chunk[None, :]
        s = jnp.where(mask[None, None], s, NEG_INF)
        p = jax.nn.softmax(s, axis=-1).astype(v.dtype)
        return jnp.einsum('bhqk,bkhd->bqhd', p, v)

    o = lax.map(attend, (q_blocks, q_idx))
    return o.transpose(1, 0, 2, 3, 4).reshape(B, S, H * V_HEAD)

def memory_cross_attention(x, mem, wq, wkv, wo):
    B, S, _ = x.shape
    q = (x @ wq).reshape(B, S, MEM_HEADS, MEM_HEAD_DIM)
    k, v = jnp.split(mem @ wkv, 2, axis=-1)
    k = k.reshape(B, mem.shape[1], MEM_HEADS, MEM_HEAD_DIM)
    v = v.reshape(B, mem.shape[1], MEM_HEADS, MEM_HEAD_DIM)
    s = jnp.einsum('bshd,bmhd->bhsm', q, k, preferred_element_type=jnp.float32) * MEM_HEAD_DIM ** -0.5
    p = jax.nn.softmax(s, axis=-1).astype(v.dtype)
    o = jnp.einsum('bhsm,bmhd->bshd', p, v).reshape(B, S, D_MODEL)
    return o @ wo

def setup_inputs(seed: int = 0) -> dict:
    key = jax.random.key(seed)
    ks = jax.random.split(key, 24)

    def nrm(k, shape, scale):
        return jax.random.normal(k, shape, jnp.float32) * scale

    x = nrm(ks[0], (BATCH, SEQ, D_MODEL), 1.0)
    mem = nrm(ks[1], (BATCH, N_MEM, D_MODEL), 1.0)
    start = jax.random.randint(ks[2], (BATCH, 1), 0, 8192, dtype=jnp.int32)
    positions = (start + jnp.arange(SEQ, dtype=jnp.int32)[None, :]).astype(jnp.int32)
    L = DEPTH
    return {
        'x': x,
        'mem': mem,
        'positions': positions,
        'ln_g': 1.0 + nrm(ks[3], (L, 4, D_MODEL), 0.05),
        'ln_b': nrm(ks[4], (L, 4, D_MODEL), 0.02),
        'ffn1_w13': nrm(ks[5], (L, D_MODEL, 2 * D_FF), D_MODEL ** -0.5),
        'ffn1_w2': nrm(ks[6], (L, D_FF, D_MODEL), BETA * D_FF ** -0.5),
        'w_in': nrm(ks[7], (L, D_MODEL, D_IN), D_MODEL ** -0.5),
        'pool_w': nrm(ks[8], (L, len(POOL_WINDOWS), POOL_GROUP, POOL_GROUP), POOL_GROUP ** -0.5),
        'pool_scale': 1.0 + nrm(ks[9], (L, POOL_WIDTH), 0.1),
        'q_norm_g': 1.0 + nrm(ks[10], (L, Q_LORA), 0.05),
        'w_uq': nrm(ks[11], (L, Q_LORA, MLA_HEADS * (QK_NOPE + QK_ROPE)), Q_LORA ** -0.5),
        'kv_norm_g': 1.0 + nrm(ks[12], (L, KV_LORA), 0.05),
        'w_ukv': nrm(ks[13], (L, KV_LORA, MLA_HEADS * (QK_NOPE + V_HEAD)), KV_LORA ** -0.5),
        'w_out': nrm(ks[14], (L, D_MIX, D_MODEL), BETA * D_MIX ** -0.5),
        'mem_wq': nrm(ks[15], (L, D_MODEL, D_MODEL), D_MODEL ** -0.5),
        'mem_wkv': nrm(ks[16], (L, D_MODEL, 2 * D_MODEL), D_MODEL ** -0.5),
        'mem_wo': nrm(ks[17], (L, D_MODEL, D_MODEL), BETA * D_MODEL ** -0.5),
        'ffn2_w13': nrm(ks[18], (L, D_MODEL, 2 * D_FF), D_MODEL ** -0.5),
        'ffn2_w2': nrm(ks[19], (L, D_FF, D_MODEL), BETA * D_FF ** -0.5),
    }

def reference(x, mem, positions, ln_g, ln_b, ffn1_w13, ffn1_w2, w_in, pool_w, pool_scale,
              q_norm_g, w_uq, kv_norm_g, w_ukv, w_out, mem_wq, mem_wkv, mem_wo,
              ffn2_w13, ffn2_w2):
    for l in range(DEPTH):
        x = layer_norm(ALPHA * x + 0.5 * swiglu(x, ffn1_w13[l], ffn1_w2[l]), ln_g[l, 0], ln_b[l, 0])
        h = x @ w_in[l]
        o0 = POOL_WIDTH
        o1 = o0 + Q_LORA
        o2 = o1 + KV_LORA
        u_pool, c_q, c_kv, k_pe = h[..., :o0], h[..., o0:o1], h[..., o1:o2], h[..., o2:]
        y_pool = pool_mixer(u_pool, pool_w[l], pool_scale[l])
        y_mla = mla_mixer(c_q, c_kv, k_pe, positions, q_norm_g[l], w_uq[l],
                          kv_norm_g[l], w_ukv[l])
        y_mix = jnp.concatenate([y_pool, y_mla], axis=-1) @ w_out[l]
        x = layer_norm(ALPHA * x + y_mix, ln_g[l, 1], ln_b[l, 1])
        y_mem = memory_cross_attention(x, mem, mem_wq[l], mem_wkv[l], mem_wo[l])
        x = layer_norm(ALPHA * x + y_mem, ln_g[l, 2], ln_b[l, 2])
        x = layer_norm(ALPHA * x + 0.5 * swiglu(x, ffn2_w13[l], ffn2_w2[l]), ln_g[l, 3], ln_b[l, 3])
    return x


_drawn_inputs = setup_inputs


def setup_inputs(seed=0):
    import zlib

    import numpy as np

    out = dict(_drawn_inputs(seed))
    spreads = {}
    factors = {'pool_scale': 2.667, 'q_norm_g': 8.0, 'kv_norm_g': 8.0}
    for name, (base, spread) in spreads.items():
        noise = np.random.default_rng([zlib.crc32(name.encode()), seed]).standard_normal(out[name].shape)
        drawn = base * np.exp(spread * noise) if base else spread * noise
        out[name] = __import__('jax').numpy.asarray(drawn.astype(out[name].dtype))
    for name, factor in factors.items():
        out[name] = (out[name] * factor).astype(out[name].dtype)
    return out
```

```python
import math
from contextlib import ExitStack

import numpy as np
import concourse.bass as bass
from concourse import mybir

F32 = mybir.dt.float32
F32R = mybir.dt.float32r
I32 = mybir.dt.int32
ALU = mybir.AluOpType
ACT = mybir.ActivationFunctionType
AX = mybir.AxisListType

P = 128
POOL_WINDOWS = (2, 4, 8, 16)
CHUNK = 64
MEM_HEADS = 4
QK_NOPE, QK_ROPE, V_HEAD = 128, 64, 128
ROPE_BASE = 10000.0
LN_EPS, RMS_EPS, NEG_INF = 1e-5, 1e-6, -1e30

UNIT = 1024
RING = 4
BANKS = 4
STEPS = 4

C_ID, C_ROT, C_ONE, C_CNT, C_FREQ, C_HALF = 0, 128, 256, 384, 896, 897
C_ALL = 898

TURN, _rest = [], 2.0 * math.pi
for _shift in (5, 17, 25):
    TURN.append(math.floor(_rest * 2.0 ** _shift) / 2.0 ** _shift)
    _rest -= TURN[-1]
TURN.append(_rest)
ROUND = 1.5 * 2.0 ** 23
PI_IN = 3.1415925


def constants(seq):
    c = np.zeros((P, C_ALL), np.float32)
    c[:, C_ID:C_ID + P] = np.eye(P)
    half = QK_ROPE // 2
    for p in range(P):
        if p % QK_ROPE < half:
            c[p + half, C_ROT + p] = -1.0
        else:
            c[p - half, C_ROT + p] = 1.0
    c[:, C_ONE:C_ONE + P] = 1.0
    for tile in range(2):
        for p in range(P):
            w = POOL_WINDOWS[2 * tile + p // 64]
            c[p, C_CNT + tile * seq:C_CNT + (tile + 1) * seq] = 1.0 / np.minimum(np.arange(seq) + 1, w)
    c[:, C_FREQ] = (np.float32(ROPE_BASE) ** (-np.arange(half, dtype=np.float32) / half))[np.arange(P) % half]
    c[:, C_HALF] = -0.5
    return c


class Plan:

    def __init__(self):
        self.at, self.done, self.units_by = {}, {}, []
        self.n = dict(units=0, items=0, pairs=0, copies=0, his=0)

    def section(self, name, marks, pairs=0, copies=0, his=0):
        self.at[name] = dict(self.n)
        for mark in marks:
            for what in mark:
                if what == "U":
                    self.done["unit", self.n["units"]] = len(self.units_by) + 1
                    self.n["units"] += 1
                elif what == "I":
                    self.done["item", self.n["items"]] = len(self.units_by) + 1
                    self.n["items"] += 1
                else:
                    self.done[what] = len(self.units_by) + 1
            self.units_by.append(self.n["units"])
        self.n["pairs"] += pairs
        self.n["copies"] += copies
        self.n["his"] += his

    def __getitem__(self, name):
        return self.at[name]


def trunk(nc, a, consts, out):
    L, D, F2 = a["ffn1_w13"].shape
    S = a["x"].shape[1]
    F = F2 // 2
    KT, TB, FT = D // P, S // P, F // P
    H = a["w_ukv"].shape[2] // (QK_NOPE + V_HEAD)
    Q_LORA, KV_LORA = a["w_uq"].shape[1], a["w_ukv"].shape[1]
    POOL_W = len(POOL_WINDOWS) * 64
    assert (S, D, FT, H, Q_LORA, KV_LORA) == (256, 1024, 22, 6, 256, 128)
    ALPHA = (2 * L) ** 0.25
    MLA_SCALE = (QK_NOPE + QK_ROPE) ** -0.5
    MEM_SCALE = (D // MEM_HEADS) ** -0.5
    PAIRS = H // 2
    SMALL = L * (len(POOL_WINDOWS) + 5)
    LOOPS = (FT - 2) // STEPS
    LOOP_UNITS = 3 * STEPS
    assert LOOPS * STEPS == FT - 2 and LOOP_UNITS % RING == 0 and (2 * STEPS) % BANKS == 0

    FILL = {(0, "start"): [(0, 0), (0, 1)], (0, "ln0"): [(0, 2), (0, 3)], (0, "mix"): [(0, 4)],
            (0, "ln1"): [(0, 5)], (0, "ln2"): [(1, 0), (1, 1)], (0, "ln3"): [(1, 2), (1, 3)],
            (1, "ln0"): [(1, 4)], (1, "mix"): [], (1, "ln1"): [(1, 5)], (1, "ln2"): [], (1, "ln3"): []}

    plan = Plan()
    UI, ITEM, UNIT_ = ["U", "I"], ["I"], ["U"]

    def plan_fill(parts):
        for l, i in parts:
            if i < 4:
                plan.section(("kv", l, i), [UI, UI], pairs=1, copies=1)
            else:
                plan.section(("kv", l, i), [UNIT_, UI, UNIT_, UI], his=2)

    def plan_turn(first, second, between):
        plan.section(("turn", first), [[("turned", first)]])
        plan_fill(between)
        plan.section(("turn", second), [[("turned", second)]])

    def plan_rows(name, e, units):
        plan.section(name, [UNIT_] * (units - 1) + [[("y", e, 0)], ["U", ("y", e, 1)]])

    def plan_norm(e, parts):
        plan_fill(parts[0:1])
        plan_turn(4 + 2 * e, 5 + 2 * e, parts[1:])

    plan_turn(0, 1, [])
    plan_fill(FILL[0, "start"])
    plan_turn(2, 3, [])
    for l in range(L):
        for w in range(2):
            if w == 1:
                for s in range(1, 3):
                    if s == 1:
                        plan.section(("win", l), [UI] * 6, copies=3)
                        plan_fill(FILL[l, "mix"])
                        plan.section(("uqA", l), [ITEM] * 3 + [UI], pairs=2, copies=2)
                        plan.section(("uqB", l), [ITEM, UI], pairs=1, copies=1)
                        plan.section(("stat", l), [ITEM] * 2, his=1)
                        plan.section(("uqC", l), [ITEM, ITEM, UI, ITEM], copies=2)
                        plan.section(("kn", l), [ITEM] * 5 + [UI], pairs=3, copies=3)
                        plan.section(("v", l), [ITEM] * 3 + [UI], his=2)
                        plan.section(("rot", l), [ITEM] * 2)
                        for pr in range(PAIRS + 1):
                            if pr < PAIRS:
                                plan.section(("score", l, pr), [[("score", l, pr)]])
                            if pr > 0:
                                plan.section(("pt", l, pr - 1), [ITEM] * 2, his=2)
                                plan.section(("pv", l, pr - 1), [ITEM] * 2, pairs=1, copies=1)
                        plan_rows(("wout", l), 4 * l + 1, KT)
                    else:
                        plan.section(("wq", l), [UI] * KT, pairs=4, copies=4)
                        for b in range(TB):
                            plan.section(("mscore", l, b), [[("mscore", l, b)]])
                        plan.section(("mpt", l), [ITEM] * MEM_HEADS, his=MEM_HEADS)
                        plan.section(("mpv", l), [ITEM] * KT, pairs=4, copies=4)
                        plan_rows(("wo", l), 4 * l + 2, KT)
                    plan_norm(4 * l + s, FILL[l, f"ln{s}"])
            e = 4 * l + 3 * w
            marks = [UI, UI] + ([UI, UI, UNIT_]) * (FT - 1) + [[("y", e, 0)], ["U", ("y", e, 1)]]
            plan.section(("ffn", l, w), marks, pairs=FT, copies=FT)
            if e < 4 * L - 1:
                plan_norm(e, FILL[l, f"ln{3 * w}"])
    done = plan.done
    UNITS = plan.n["units"]

    w13 = [a["ffn1_w13"], a["ffn2_w13"]]
    w2 = [a["ffn1_w2"], a["ffn2_w2"]]

    def columns(w, lo, n):
        return w.rearrange("(k p) f -> p k f", p=P)[:, :, lo:lo + n]

    def ffn_units(base, j):
        g = base if j == 0 else base + 3 * j - 1
        return g, g + 1, base + 3 * j + 4 if j < FT - 1 else base + 3 * FT - 1

    source = {}
    for l in range(L):
        for i in range(4):
            u = plan["kv", l, i]["units"]
            for t in range(2):
                source[u + t] = (UNIT, [(0, columns(a["mem_wkv"][l], (2 * i + t) * P, P))])
        for i in range(2):
            u = plan["kv", l, 4 + i]["units"]
            for t in range(4):
                quarter, half = 2 * i + t // 2, t % 2
                source[u + t] = (UNIT, [(0, columns(a["mem_wkv"][l][half * 512:(half + 1) * 512, :],
                                                    D + quarter * 256, 256))])
        u = plan["win", l]["units"]
        c_q, c_kv, k_pe = POOL_W, POOL_W + Q_LORA, POOL_W + Q_LORA + KV_LORA
        for t, lo in enumerate((c_q, c_q + P, c_kv)):
            source[u + t] = (UNIT, [(0, columns(a["w_in"][l], lo, P))])
        pe_cols = columns(a["w_in"][l], k_pe, QK_ROPE)
        source[u + 3] = (UNIT, [(0, pe_cols), (QK_ROPE, pe_cols)])
        for t in range(2):
            source[u + 4 + t] = (UNIT, [(0, columns(a["w_in"][l], t * P, P))])
        uq = a["w_uq"][l].rearrange("(k p) (h c) -> p k h c", p=P, h=H)
        ukv = a["w_ukv"][l].rearrange("p (h c) -> p h c", h=H)
        for name, heads, cols in (("uqA", slice(0, 4), slice(0, QK_NOPE)), ("uqB", slice(4, 6), slice(0, QK_NOPE)),
                                  ("uqC", slice(0, 6), slice(QK_NOPE, QK_NOPE + QK_ROPE))):
            size = (heads.stop - heads.start) * (cols.stop - cols.start)
            source[plan[name, l]["units"]] = (2 * size, [(k * size, uq[:, k, heads, cols]) for k in range(2)])
        source[plan["kn", l]["units"]] = (H * QK_NOPE, [(0, ukv[:, :, 0:QK_NOPE])])
        source[plan["v", l]["units"]] = (H * V_HEAD, [(0, ukv[:, :, QK_NOPE:QK_NOPE + V_HEAD])])
        for r in range(KT):
            source[plan["wout", l]["units"] + r] = (UNIT, [(0, a["w_out"][l][r * P:(r + 1) * P, :])])
            source[plan["wo", l]["units"] + r] = (UNIT, [(0, a["mem_wo"][l][r * P:(r + 1) * P, :])])
            source[plan["wq", l]["units"] + r] = (UNIT, [(0, columns(a["mem_wq"][l], r * P, P))])
        for w in range(2):
            for j in range(FT):
                g, up, d = ffn_units(plan["ffn", l, w]["units"], j)
                source[g] = (UNIT, [(0, columns(w13[w][l], j * P, P))])
                source[up] = (UNIT, [(0, columns(w13[w][l], F + j * P, P))])
                source[d] = (UNIT, [(0, w2[w][l][j * P:(j + 1) * P, :])])
    assert sorted(source) == list(range(UNITS))

    with ExitStack() as ctx:
        def sb(name, shape, dt=F32):
            return ctx.enter_context(nc.sbuf_tensor(name, shape, dt))

        def sem(name):
            return ctx.enter_context(nc.semaphore(name))

        raw = sb("raw", [P, RING, UNIT])
        w_hi = sb("w_hi", [P, RING, UNIT], F32R)
        w_lo = sb("w_lo", [P, RING, UNIT], F32R)
        x = sb("x", [P, TB, D])
        tmp = sb("tmp", [P, 2 * D])
        gb = sb("gb", [P, 2, D])
        xT = sb("xT", [P, KT, 2, S], F32R)
        memT = sb("memT", [P, KT, 2, S], F32R)
        memK = sb("memK", [P, KT, 2, S], F32R)
        memV = sb("memV", [P, TB, 2, D], F32R)
        qT = sb("qT", [P, 9, 2, S], F32R)
        v = sb("v", [P, TB, 2, H * V_HEAD], F32R)
        mixT = sb("mixT", [P, KT, 2, S], F32R)
        cqp = sb("cqp", [P, 6 * S], F32R)
        ev = sb("ev", [P, 2, 2, S])
        cst = sb("cst", [P, C_ALL])
        cosT = sb("cosT", [P, S])
        sinT = sb("sinT", [P, S])
        rkv_bc = sb("rkv_bc", [P, S])
        pw = sb("pw", [P, L, 2, P])
        pscale = sb("pscale", [P, L, 2])
        gains = sb("gains", [P, L, 3])
        st = sb("st", [P, 96])
        ps = ctx.enter_context(nc.psum_tensor("ps", [P, 8, 512], F32))

        knT, krT = xT[:, 0:6], xT[:, 6:8]
        mpT = xT
        aT = mixT
        cq = cqp[:, :].rearrange("p (t c s) -> p t c s", t=3, c=2)
        pT = cqp[:, :].rearrange("p (e c k) -> p e c k", e=2, c=2)
        ident, rot, ones = cst[:, C_ID:C_ID + P], cst[:, C_ROT:C_ROT + P], cst[:, C_ONE:C_ONE + P]
        inv_count = cst[:, C_CNT:C_CNT + 2 * S].rearrange("p (t s) -> p t s", t=2)

        raw_landed = [sem(f"raw_landed{i}") for i in range(RING)]
        hi_done, lo_done, pe_done = sem("hi_done"), sem("lo_done"), sem("pe_done")
        bank_free, half_copied, pair_done = sem("bank_free"), sem("half_copied"), sem("pair_done")
        silu_done, item_hi = sem("silu_done"), sem("item_hi")
        turned_hi, turned_lo = sem("turned_hi"), sem("turned_lo")
        norm_done, x_scaled, var_ready, rstd_ready = (
            sem("norm_done"), sem("x_scaled"), sem("var_ready"), sem("rstd_ready"))
        gains_landed, consts_landed, mem_landed, x_landed, small_landed, pos_landed, pw_zeroed = (
            sem("gains_landed"), sem("consts_landed"), sem("mem_landed"), sem("x_landed"), sem("small_landed"),
            sem("pos_landed"), sem("pw_zeroed"))
        dve_step, pool_step = sem("dve_step"), sem("pool_step")
        angles_ready, tables_done = sem("angles_ready"), sem("tables_done")
        squares_ready, rms_ready, diag_ready = sem("squares_ready"), sem("rms_ready"), sem("diag_ready")
        cq_hi, cq_ready, pooled, rope_ready = (
            sem("cq_hi"), sem("cq_ready"), sem("pooled"), sem("rope_ready"))
        scores_half, scores_read, max_ready, exp_done, probs_ready = (
            sem("scores_half"), sem("scores_read"), sem("max_ready"), sem("exp_done"), sem("probs_ready"))
        stored = sem("stored")

        def plus(n, it, per):
            return n if it is None else n + it * per

        def bank(m):
            return ps[:, m % BANKS, :]

        def halves(m, n=2):
            return ps[:, m % BANKS:m % BANKS + n, :].rearrange("p b (c s) -> p b c s", c=2)

        def blocks_T(t, c):
            return [t[:, :, c, b * P:(b + 1) * P] for b in range(TB)]

        STATS = [st[:, 16 * b:16 * b + 12] for b in range(2)]
        MEANVAR = [st[:, 32 + 4 * b:34 + 4 * b] for b in range(2)]
        VEPS = [st[:, 34 + 4 * b:35 + 4 * b] for b in range(2)]
        RSTD = [st[:, 35 + 4 * b:36 + 4 * b] for b in range(2)]
        MS, RMS = st[:, 40:44], st[:, 44:48]
        SRQ = st[:, 48:50]
        MX = [st[:, 50 + 4 * i:54 + 4 * i] for i in range(2)]
        NEGM = [st[:, 58 + 4 * i:62 + 4 * i] for i in range(2)]
        SUM = [st[:, 66 + 4 * i:70 + 4 * i] for i in range(2)]
        REC = [st[:, 74 + 4 * i:78 + 4 * i] for i in range(2)]

        def tiles(t, n):
            return t.rearrange("p (t s) -> p t s", t=n)

        cqf = tiles(tmp[:, 0:3 * S], 3)
        diag = tiles(tmp[:, 3 * S:4 * S], 2)
        sq_kv = tmp[:, 3 * S:4 * S]
        ropeX = tiles(tmp[:, 4 * S:8 * S], 4)
        ropeZ = tiles(tmp[:, 0:4 * S], 4)
        kv_pe = tiles(tmp[:, 2 * S:6 * S], 4)[:, 0:3:2]
        poolU, poolA = tiles(gb[:, 0, 0:512], 2), tiles(gb[:, 0, 512:1024], 2)
        poolB, sq_q = tiles(gb[:, 1, 0:512], 2), tiles(gb[:, 1, 512:1024], 2)

        poolM = sb("poolM", [P, 2, S])

        def mla_scores(pr):
            s = tmp[:, 768 * (pr % 2):768 * (pr % 2) + 768]
            return (s[:, 0:512].rearrange("p (e k) -> p e k", e=2),
                    s[:, 512:768].rearrange("p (e k) -> p e k", e=2))

        def mem_scores(b):
            return tmp[:, b * D:(b + 1) * D].rearrange("p (h k) -> p h k", h=MEM_HEADS)

        block = ctx.enter_context(nc.Block())

        @block.sync
        def _(sp):
            sp.dma_start(cst[:, :], consts[:, :]).then_inc(consts_landed, 16)
            sp.dma_start(tmp[:, :].rearrange("p (b d) -> p b d", b=TB),
                         a["mem"][0].rearrange("(b p) d -> p b d", p=P)).then_inc(mem_landed, 16)

            def load(n, parts, it=None):
                if n >= RING:
                    sp.wait_ge(lo_done, plus(n - RING + 1, it, LOOP_UNITS))
                k = n % RING
                for col, src in parts:
                    if len(src.shape) == 2:
                        dst = raw[:, k, :]
                    elif src.shape[2] == QK_ROPE and src.shape[1] == KT:
                        dst = raw[:, k, :].rearrange("p (t c) -> p t c", t=KT)[:, :, col:col + QK_ROPE]
                    else:
                        t, c = src.shape[1:]
                        dst = raw[:, k, col:col + t * c].rearrange("p (t c) -> p t c", t=t)
                    sp.dma_start(dst, src).then_inc(raw_landed[k], 16)

            n = 0
            for l in range(L):
                for w in range(2):
                    u = plan["ffn", l, w]["units"]
                    for n in range(n, u + 5):
                        load(n, source[n][1])
                        if n == RING - 1:
                            sp.dma_start(x[:, :, :], a["x"][0].rearrange("(b p) d -> p b d", p=P))\
                                .then_inc(x_landed, 16)
                    cols13 = w13[w][l].rearrange("(k p) f -> p k f", p=P)
                    with sp.Fori(0, LOOPS) as it:
                        for s in range(STEPS):
                            g = u + 5 + 3 * s
                            col = it * (STEPS * P) + (s + 2) * P
                            load(g, [(0, cols13[:, :, bass.ds(col, P)])], it)
                            load(g + 1, [(0, cols13[:, :, bass.ds(col + F, P)])], it)
                            load(g + 2, [(0, w2[w][l][bass.ds(col - P, P), :])], it)
                    n = u + 5 + LOOP_UNITS * LOOPS
            for n in range(n, UNITS):
                load(n, source[n][1])
            for b in range(TB):
                sp.wait_ge(norm_done, 2 * (4 * L - 1) + b + 1)
                sp.dma_start(out[0, b * P:(b + 1) * P, :], x[:, b, :]).then_inc(stored, 16)
            sp.wait_ge(stored, 16 * TB)

        def landed(n):
            return sum(16 * len(source[k][1]) for k in range(n % RING, n + 1, RING))

        @block.tensor
        def _(pe):
            milestones = [0]

            def reach(ins, *tags):
                milestones[0] += 1
                for tag in tags:
                    assert done[tag] == milestones[0], (tag, done[tag], milestones[0])
                ins.then_inc(pe_done, 1)

            def product(dst, stand, move, start, stop):
                return nc.tensor.matmul(dst, stand, move, start=start, stop=stop, skip_group_check=True)

            def take_bank(m, it=None):
                if m >= BANKS:
                    pe.wait_ge(bank_free, plus(m - BANKS + 1, it, 2 * STEPS))

            def unit_split(n, it=None):
                pe.wait_ge(lo_done, plus(n + 1, it, LOOP_UNITS))

            def column_item(m, n, offsets, acts, it=None):
                take_bank(m, it)
                for i, (o, act) in enumerate(zip(offsets, acts)):
                    product(bank(m), w_hi[:, n % RING, o:o + P], act, i == 0, False)
                    last = product(bank(m)[:, 0:S], w_lo[:, n % RING, o:o + P], act[:, 0, :], False,
                                   i == len(acts) - 1)
                return last

            def column_unit(m, n, acts, it=None):
                unit_split(n, it)
                last = column_item(m, n, [k * P for k in range(KT)], [acts[:, k] for k in range(KT)], it)
                reach(last, ("unit", n), ("item", m))

            def row_unit(n, act, first=False, e=None, it=None):
                unit_split(n, it)
                for b in range(TB):
                    hi, lo = act[:, 0, b * P:(b + 1) * P], act[:, 1, b * P:(b + 1) * P]
                    for stand, ring, start in ((hi, w_hi, first), (hi, w_lo, False), (lo, w_hi, False)):
                        for c in range(2):
                            last = product(ps[:, 4 + 2 * b + c, :], stand, ring[:, n % RING, c * 512:(c + 1) * 512],
                                           start, e is not None and stand is lo)
                    if e is not None and b == 0:
                        reach(last, ("y", e, 0))
                reach(last, ("unit", n), *([("y", e, 1)] if e is not None else []))

            def turn(job, src, b):
                for k in range(KT):
                    dst = ps[:, 4 + 2 * b + k // 4, (k % 4) * P:(k % 4 + 1) * P]
                    last = nc.tensor.transpose(dst, src[:, k * P:(k + 1) * P], ident)
                reach(last, ("turned", job))

            def fill(parts):
                for l, i in parts:
                    u, m = plan["kv", l, i]["units"], plan["kv", l, i]["items"]
                    pe.wait_ge(turned_lo, 2)
                    if i < 4:
                        for t in range(2):
                            column_unit(m + t, u + t, memT)
                        continue
                    for t in range(2):
                        take_bank(m + t)
                        for half in range(2):
                            n = u + 2 * t + half
                            unit_split(n)
                            for b in range(TB):
                                dst = bank(m + t)[:, b * S:(b + 1) * S]
                                for k in range(4):
                                    act = memT[:, 4 * half + k]
                                    hi, lo = act[:, 0, b * P:(b + 1) * P], act[:, 1, b * P:(b + 1) * P]
                                    whi, wlo = (r[:, n % RING, k * 256:(k + 1) * 256] for r in (w_hi, w_lo))
                                    product(dst, hi, whi, half == 0 and b == 0 and k == 0, False)
                                    product(dst, hi, wlo, False, False)
                                    last = product(dst, lo, whi, False, half == 1 and k == 3)
                            reach(last, ("unit", n), *([("item", m + t)] if half else []))

            def ffn(l, w):
                u, m, h = (plan["ffn", l, w][k] for k in ("units", "items", "pairs"))

                def up(j, it=None):
                    g, up_, _ = ffn_units(u, j)
                    column_unit(m + 2 * j, g, xT, it)
                    column_unit(m + 2 * j + 1, up_, xT, it)

                def down(j, it=None, first=False, e=None):
                    pe.wait_ge(pair_done, plus(h + j + 1, it, STEPS))
                    row_unit(ffn_units(u, j)[2], aT[:, j % 2], first, e, it)

                pe.wait_ge(turned_lo, 4 + 2 * (4 * l + 3 * w))
                up(0)
                up(1)
                down(0, first=True)
                with pe.Fori(0, LOOPS) as it:
                    for s in range(STEPS):
                        up(s + 2, it)
                        down(s + 1, it)
                milestones[0] += LOOP_UNITS * (LOOPS - 1)
                down(FT - 1, e=4 * l + 3 * w)

            def norm(e, parts):
                for b in range(TB):
                    fill(parts[0:1] if b == 0 else parts[1:])
                    pe.wait_ge(norm_done, 2 * e + b + 1)
                    turn(4 + 2 * e + b, x[:, b, :], b)

            def mix(l):
                at = {k: plan[k, l] for k in ("win", "uqA", "uqB", "stat", "uqC", "kn", "v", "rot")}
                pe.wait_ge(turned_lo, 4 + 2 * (4 * l + 1))
                for t in range(6):
                    column_unit(at["win"]["items"] + t, at["win"]["units"] + t, xT)
                fill(FILL[l, "mix"])

                def items_of(name, count, offsets, acts, more=0):
                    n, m = at[name]["units"], at[name]["items"]
                    unit_split(n)
                    for i in range(count):
                        last = column_item(m + i, n, offsets(i), acts)
                        reach(last, ("item", m + i), *([("unit", n)] if i == count - 1 else []))

                pe.wait_ge(cq_ready, 3 * l + 2)
                items_of("uqA", 4, lambda i: [(4 * k + i) * P for k in range(2)], [cq[:, k] for k in range(2)])
                items_of("uqB", 2, lambda i: [(2 * k + i) * P for k in range(2)], [cq[:, k] for k in range(2)])

                m = at["stat"]["items"]
                take_bank(m)
                pe.wait_ge(squares_ready, l + 1)
                for b in range(TB):
                    rows = slice(b * P, (b + 1) * P)
                    for t in range(2):
                        nc.tensor.matmul(bank(m)[:, b:b + 1], sq_q[:, t, rows], ones[:, 0:1],
                                         start=b == 0 and t == 0, stop=t == 1, skip_group_check=True)
                    last = nc.tensor.matmul(bank(m)[:, 2 + b:3 + b], sq_kv[:, rows], ones[:, 0:1],
                                            start=False, stop=True, skip_group_check=True)
                reach(last, ("item", m))
                take_bank(m + 1)
                pe.wait_ge(pooled, l + 1)
                pe.wait_ge(small_landed, 16 * SMALL)
                for t in range(2):
                    last = nc.tensor.matmul(bank(m + 1)[:, t * S:(t + 1) * S], pw[:, l, t, :], poolB[:, t, :],
                                            start=t == 0, stop=True, skip_group_check=True)
                reach(last, ("item", m + 1))

                items_of("uqC", 3, lambda i: [k * 6 * QK_ROPE + i * P for k in range(2)], [cq[:, k] for k in range(2)])
                m = at["uqC"]["items"] + 3
                take_bank(m)
                pe.wait_ge(diag_ready, l + 1)
                for b in range(TB):
                    last = nc.tensor.matmul(bank(m)[:, b * P:(b + 1) * P], ones, diag[:, b, :],
                                            start=b == 0, stop=True, skip_group_check=True)
                reach(last, ("item", m))

                pe.wait_ge(cq_ready, 3 * l + 3)
                items_of("kn", 6, lambda i: [i * P], [cq[:, 2]])
                n, m = at["v"]["units"], at["v"]["items"]
                unit_split(n)
                for i in range(4):
                    take_bank(m + i)
                    rows = slice((i // 2) * P, (i // 2 + 1) * P)
                    cols = slice((i % 2) * 384, (i % 2 + 1) * 384)
                    dst = bank(m + i)[:, 0:384]
                    product(dst, cq[:, 2, 0, rows], w_hi[:, n % RING, cols], True, False)
                    product(dst, cq[:, 2, 0, rows], w_lo[:, n % RING, cols], False, False)
                    last = product(dst, cq[:, 2, 1, rows], w_hi[:, n % RING, cols], False, True)
                    reach(last, ("item", m + i), *([("unit", n)] if i == 3 else []))

                m = at["rot"]["items"]
                pe.wait_ge(bank_free, at["uqC"]["items"] + 3)
                for i in range(2):
                    take_bank(m + i)
                    for t in range(2):
                        last = nc.tensor.matmul(bank(m + i)[:, t * S:(t + 1) * S], rot, ropeX[:, 2 * i + t, :],
                                                start=t == 0, stop=True, skip_group_check=True)
                    reach(last, ("item", m + i))

                pe.wait_ge(rope_ready, l + 1)
                for pr in range(PAIRS + 1):
                    if pr < PAIRS:
                        scores(l, pr)
                    if pr > 0:
                        mla_values(l, pr - 1)
                m = plan["stat", l]["items"]
                pe.wait_ge(bank_free, m + 2)
                for r in range(KT):
                    if r >= 2:
                        pe.wait_ge(pair_done, plan["pv", l, (r - 2) // 2]["pairs"] + 1)
                    row_unit(plan["wout", l]["units"] + r, mixT[:, r], r == 0, 4 * l + 1 if r == KT - 1 else None)

            def scores(l, pr):
                j = 5 * l + pr
                pe.wait_ge(pair_done, plan["kn", l]["pairs"] + pr + 1)
                if j:
                    pe.wait_ge(scores_read, j)
                for e in range(2):
                    parts = ((qT[:, 2 * pr + e], knT[:, 2 * pr + e]), (qT[:, 6 + pr], krT[:, e]))
                    for i, (q, k) in enumerate(parts):
                        product(ps[:, 4 + e, :], q[:, 0, P:S], k, i == 0, False)
                        product(ps[:, 4 + e, 0:S], q[:, 1, P:S], k[:, 0, :], False, i == 1)
                    for i, (q, k) in enumerate(parts):
                        product(ps[:, 6, e * S:(e + 1) * S], q[:, 0, 0:P], k[:, :, 0:P], i == 0 and e == 0, False)
                        last = product(ps[:, 6, e * S:e * S + P], q[:, 1, 0:P], k[:, 0, 0:P], False, i == 1)
                reach(last, ("score", l, pr))

            def mla_values(l, pr):
                s1, s0 = mla_scores(pr)
                m = plan["pt", l, pr]["items"]
                pe.wait_ge(probs_ready, 5 * l + pr + 1)
                for e in range(2):
                    take_bank(m + e)
                    nc.tensor.transpose(bank(m + e)[:, 0:P], s0[:, e, :], ident)
                    nc.tensor.transpose(bank(m + e)[:, P:2 * P], s1[:, e, 0:P], ident)
                    last = nc.tensor.transpose(bank(m + e)[:, 2 * P:3 * P], s1[:, e, P:2 * P], ident)
                    reach(last, ("item", m + e))
                m2 = plan["pv", l, pr]["items"]
                for e in range(2):
                    take_bank(m2 + e)
                    pe.wait_ge(bank_free, m + e + 1)
                    cols = slice((2 * pr + e) * P, (2 * pr + e + 1) * P)
                    both = bank(m2 + e).rearrange("p (c s) -> p c s", c=2)
                    product(both, v[:, 0, 0, cols], pT[:, e, :, 0:S], True, False)
                    product(both[:, 0, :], v[:, 0, 1, cols], pT[:, e, 0, 0:S], False, False)
                    product(both[:, :, P:S], v[:, 1, 0, cols], pT[:, e, :, S:S + P], False, False)
                    last = product(both[:, 0, P:S], v[:, 1, 1, cols], pT[:, e, 0, S:S + P], False, True)
                    reach(last, ("item", m2 + e))

            def memory(l):
                u, m, h = (plan["wq", l][k] for k in ("units", "items", "pairs"))
                pe.wait_ge(turned_lo, 4 + 2 * (4 * l + 2))
                for t in range(KT):
                    column_unit(m + t, u + t, xT)
                pe.wait_ge(pair_done, h + 4)
                for b in range(TB):
                    j = 5 * l + PAIRS + b
                    pe.wait_ge(scores_read, j)
                    for hh in range(MEM_HEADS):
                        for t in range(2):
                            q, k = qT[:, 2 * hh + t], memK[:, 2 * hh + t]
                            product(ps[:, 4 + hh, :], q[:, 0, b * P:(b + 1) * P], k, t == 0, False)
                            last = product(ps[:, 4 + hh, 0:S], q[:, 1, b * P:(b + 1) * P], k[:, 0, :], False, t == 1)
                    reach(last, ("mscore", l, b))
                m = plan["mpt", l]["items"]
                pe.wait_ge(probs_ready, 5 * l + PAIRS + 2)
                for hh in range(MEM_HEADS):
                    take_bank(m + hh)
                    for kt in range(2):
                        for b in range(TB):
                            last = nc.tensor.transpose(bank(m + hh)[:, kt * S + b * P:kt * S + (b + 1) * P],
                                                       mem_scores(b)[:, hh, kt * P:(kt + 1) * P], ident)
                    reach(last, ("item", m + hh))
                m2 = plan["mpv", l]["items"]
                for t in range(KT):
                    take_bank(m2 + t)
                    pe.wait_ge(bank_free, m + t // 2 + 1)
                    for kt in range(2):
                        p = mpT[:, 2 * (t // 2) + kt]
                        product(bank(m2 + t), memV[:, kt, 0, t * P:(t + 1) * P], p, kt == 0, False)
                        last = product(bank(m2 + t)[:, 0:S], memV[:, kt, 1, t * P:(t + 1) * P], p[:, 0, :],
                                       False, kt == 1)
                    reach(last, ("item", m2 + t))
                for r in range(KT):
                    pe.wait_ge(pair_done, plan["mpv", l]["pairs"] + r // 2 + 1)
                    row_unit(plan["wo", l]["units"] + r, mixT[:, r], r == 0, 4 * l + 2 if r == KT - 1 else None)

            pe.wait_ge(consts_landed, 16)
            pe.wait_ge(mem_landed, 16)
            for b in range(TB):
                turn(b, tmp[:, b * D:(b + 1) * D], b)
            fill(FILL[0, "start"])
            pe.wait_ge(x_landed, 16)
            pe.wait_ge(turned_lo, 2)
            for b in range(TB):
                turn(2 + b, x[:, b, :], b)
            for l in range(L):
                ffn(l, 0)
                norm(4 * l, FILL[l, "ln0"])
                mix(l)
                norm(4 * l + 1, FILL[l, "ln1"])
                memory(l)
                norm(4 * l + 2, FILL[l, "ln2"])
                ffn(l, 1)
                if l < L - 1:
                    norm(4 * l + 3, FILL[l, "ln3"])
            assert milestones[0] == len(plan.units_by)

        def look_ahead(split, spare=2):
            state = dict(next=0)

            def ahead(tag, more=0):
                while state["next"] < min(UNITS, plan.units_by[done[tag] - 1] + spare + 1 + more):
                    split(state["next"])
                    state["next"] += 1
            return state, ahead

        @block.scalar
        def _(act):
            def split_hi(n, it=None):
                act.wait_ge(raw_landed[n % RING], plus(landed(n), it, 16 * LOOP_UNITS // RING))
                if n >= RING:
                    act.wait_ge(pe_done, plus(done["unit", n - RING], it, LOOP_UNITS))
                size = source[n][0]
                nc.scalar.copy(w_hi[:, n % RING, 0:size], raw[:, n % RING, 0:size]).then_inc(hi_done, 1)

            state, ahead = look_ahead(split_hi)

            def copy_halves(dst, m, copy, h=None, it=None, n=2):
                act.wait_ge(pe_done, plus(done["item", m + n - 1], it, LOOP_UNITS))
                if h is not None and h >= 2:
                    act.wait_ge(pair_done, plus(h - 1, it, STEPS))
                nc.scalar.copy(dst, halves(m, n)[:, :, 1, :]).then_inc(half_copied, 1)

            def pairs(name, count):
                at = plan[name]
                for i in range(count):
                    ahead(("item", at["items"] + 2 * i + 1))
                    copy_halves(ev[:, (at["pairs"] + i) % 2], at["items"] + 2 * i, at["copies"] + i, at["pairs"] + i)

            def fill(parts):
                for l, i in parts:
                    m = plan["kv", l, i]["items"]
                    if i < 4:
                        pairs(("kv", l, i), 1)
                        continue
                    for t in range(2):
                        ahead(("item", m + t))
                        act.wait_ge(pe_done, done["item", m + t])
                        c = (2 * (i - 4) + t) * S
                        nc.scalar.copy(memV[:, :, 0, c:c + S], bank(m + t).rearrange("p (b s) -> p b s", b=TB))\
                            .then_inc(item_hi, 1)

            def turn(job, dst, b):
                ahead(("turned", job))
                act.wait_ge(pe_done, done["turned", job])
                nc.scalar.copy(blocks_T(dst, 0)[b], ps[:, 4 + 2 * b:6 + 2 * b, :].rearrange(
                    "p b (k s) -> p (b k) s", s=P)).then_inc(turned_hi, 1)

            def ffn(l, w):
                at = plan["ffn", l, w]
                u, m, h, f = at["units"], at["items"], at["pairs"], (2 * l + w) * FT

                def gate(j, it=None):
                    copy_halves(ev[:, (h + j) % 2], m + 2 * j, None, h + j, it)
                    act.wait_ge(bank_free, plus(m + 2 * j + 2, it, 2 * STEPS))
                    g = ev[:, (h + j) % 2, 0, :]
                    nc.scalar.activation(g, g, ACT.Silu).then_inc(silu_done, 1)

                for j in range(2):
                    ahead(("item", m + 2 * j + 1), -j)
                    gate(j)
                first = state["next"]
                assert first == u + 6
                with act.Fori(0, LOOPS) as it:
                    for s in range(STEPS):
                        for n in range(first + 3 * s, first + 3 * s + 3):
                            split_hi(n, it)
                        gate(s + 2, it)
                state["next"] = first + LOOP_UNITS * LOOPS

            def norm(e, parts):
                ahead(("y", e, 1), 1)
                for b in range(TB):
                    fill(parts[0:1] if b == 0 else parts[1:])
                    turn(4 + 2 * e + b, xT, b)

            def soft(j, tag, low, views):
                ahead(tag)
                act.wait_ge(pe_done, done[tag])
                for dst, src in low:
                    last = nc.scalar.copy(dst, src)
                last.then_inc(scores_half, 1)
                act.wait_ge(max_ready, j + 1)
                for i, (s, scale) in enumerate(views):
                    last = nc.scalar.activation(s, s, ACT.Exp, bias=NEGM[j % 2][:, i:i + 1], scale=scale,
                                                accum_out=SUM[j % 2][:, i:i + 1])
                last.then_inc(exp_done, 1)

            def round_items(name, dsts, srcs):
                m = plan[name]["items"]
                for i, (dst, src) in enumerate(zip(dsts, srcs)):
                    ahead(("item", m + i))
                    act.wait_ge(pe_done, done["item", m + i])
                    nc.scalar.copy(dst, src(m + i)).then_inc(item_hi, 1)

            def mix(l):
                at = plan["win", l]
                m = at["items"]
                for i, dst in enumerate((cqf[:, 0:2, :], kv_pe, poolU)):
                    ahead(("item", m + 2 * i + 1))
                    copy_halves(dst, m + 2 * i, None)
                    if i < 2:
                        act.wait_ge(bank_free, m + 2 * i + 2)
                        for t in ((0, 1), (2,))[i]:
                            nc.scalar.mul(cq[:, t, 0, :], cqf[:, t, :], gains[:, l, t:t + 1]).then_inc(cq_hi, 1)
                fill(FILL[l, "mix"])
                pairs(("uqA", l), 2)
                pairs(("uqB", l), 1)
                m = plan["stat", l]["items"] + 1
                act.wait_ge(pe_done, done["item", m])
                for t in range(2):
                    last = nc.scalar.mul(mixT[:, t, 0, :], bank(m)[:, t * S:(t + 1) * S], pscale[:, l, t:t + 1])
                last.then_inc(item_hi, 1)
                m = plan["uqC", l]["items"]
                ahead(("item", m + 1))
                copy_halves(ropeX[:, 1:3, :], m, None)
                copy_halves(ropeX[:, 3:4, :], m + 2, None, n=1)
                pairs(("kn", l), 3)
                m = plan["v", l]["items"]
                for b in range(TB):
                    ahead(("item", m + 2 * b + 1))
                    act.wait_ge(pe_done, done["item", m + 2 * b + 1])
                    src = ps[:, (m + 2 * b) % BANKS:(m + 2 * b) % BANKS + 2, 0:384]
                    nc.scalar.mul(v[:, b, 0, :].rearrange("p (i s) -> p i s", i=2), src, RMS[:, 2 + b:3 + b])\
                        .then_inc(item_hi, 1)
                for pr in range(PAIRS + 1):
                    if pr < PAIRS:
                        s1, s0 = mla_scores(pr)
                        views = [(s1[:, 0, :], SRQ[:, 1:2]), (s1[:, 1, :], SRQ[:, 1:2]),
                                 (s0[:, 0, :], SRQ[:, 0:1]), (s0[:, 1, :], SRQ[:, 0:1])]
                        soft(5 * l + pr, ("score", l, pr),
                             [(s1, ps[:, 4:6, S:2 * S]),
                              (s0, ps[:, 6, :].rearrange("p (e c k) -> p e c k", e=2, c=2)[:, :, 1, :])], views)
                    if pr > 0:
                        round_items(("pt", l, pr - 1), [pT[:, e, 0, :] for e in range(2)],
                                    [lambda m: bank(m)[:, 0:384]] * 2)
                        pairs(("pv", l, pr - 1), 1)

            def memory(l):
                pairs(("wq", l), 4)
                for b in range(TB):
                    s = mem_scores(b)
                    soft(5 * l + PAIRS + b, ("mscore", l, b), [(s, ps[:, 4:8, S:2 * S])],
                         [(s[:, hh, :], MEM_SCALE) for hh in range(MEM_HEADS)])
                round_items(("mpt", l), [mpT[:, 2 * hh:2 * hh + 2, 0, :] for hh in range(MEM_HEADS)],
                            [lambda m: bank(m).rearrange("p (k s) -> p k s", k=2)] * MEM_HEADS)
                pairs(("mpv", l), 4)

            for b in range(TB):
                turn(b, memT, b)
            act.wait_ge(angles_ready, 2)
            nc.scalar.activation(cosT[:, :], gb[:, 0, 0:S], ACT.Sin)
            nc.scalar.activation(sinT[:, :], gb[:, 0, S:2 * S], ACT.Sin).then_inc(tables_done, 1)
            fill(FILL[0, "start"])
            for b in range(TB):
                turn(2 + b, xT, b)
            act.wait_ge(small_landed, 16 * SMALL)
            for l in range(L):
                ffn(l, 0)
                norm(4 * l, FILL[l, "ln0"])
                mix(l)
                norm(4 * l + 1, FILL[l, "ln1"])
                memory(l)
                norm(4 * l + 2, FILL[l, "ln2"])
                ffn(l, 1)
                if l < L - 1:
                    norm(4 * l + 3, FILL[l, "ln3"])

        @block.vector
        def _(dve):
            steps = [0]

            def own(ins):
                steps[0] += 1
                ins.then_inc(dve_step, 1)

            def settle(it=None):
                dve.wait_ge(dve_step, plus(steps[0], it, 2 * STEPS))

            def split_lo(n, it=None):
                dve.wait_ge(hi_done, plus(n + 1, it, LOOP_UNITS))
                s = slice(0, source[n][0])
                nc.vector.tensor_tensor(w_lo[:, n % RING, s], raw[:, n % RING, s],
                                        w_hi[:, n % RING, s].bitcast(F32), ALU.subtract).then_inc(lo_done, 1)

            state, ahead = look_ahead(split_lo)

            def add_halves(dst, m, copy, it=None, n=2):
                dve.wait_ge(half_copied, plus(copy + 1, it, STEPS))
                nc.vector.tensor_tensor(dst, halves(m, n)[:, :, 0, :], dst, ALU.add).then_inc(bank_free, n)

            def split_pair(dst, src, it=None):
                own(nc.vector.tensor_copy(dst[:, :, 0, :], src))
                settle(it)
                nc.vector.tensor_tensor(dst[:, :, 1, :], src, dst[:, :, 0, :].bitcast(F32), ALU.subtract)\
                    .then_inc(pair_done, 1)

            def pairs(name, dst, scale=None):
                at = plan[name]
                for i in range(dst.shape[1] // 2):
                    m, h = at["items"] + 2 * i, at["pairs"] + i
                    ahead(("item", m + 1))
                    add_halves(ev[:, h % 2], m, at["copies"] + i)
                    dve.wait_ge(bank_free, m + 2)
                    if scale is not None:
                        own(nc.vector.tensor_tensor(ev[:, h % 2], ev[:, h % 2], scale, ALU.mult))
                        settle()
                    split_pair(dst[:, 2 * i:2 * i + 2], ev[:, h % 2])

            def item_lo(dst, src, hi, count, free=1):
                dve.wait_ge(item_hi, count)
                nc.vector.tensor_tensor(dst, src, hi.bitcast(F32), ALU.subtract).then_inc(bank_free, free)

            def fill(parts):
                for l, i in parts:
                    at = plan["kv", l, i]
                    if i < 4:
                        pairs(("kv", l, i), memK[:, 2 * i:2 * i + 2])
                        continue
                    for t in range(2):
                        m = at["items"] + t
                        ahead(("item", m))
                        c = (2 * (i - 4) + t) * S
                        item_lo(memV[:, :, 1, c:c + S], bank(m).rearrange("p (b s) -> p b s", b=TB),
                                memV[:, :, 0, c:c + S], at["his"] + t + 1)

            def turn(job, dst, b):
                ahead(("turned", job))
                dve.wait_ge(turned_hi, job + 1)
                nc.vector.tensor_tensor(blocks_T(dst, 1)[b], ps[:, 4 + 2 * b:6 + 2 * b, :].rearrange(
                    "p b (k s) -> p (b k) s", s=P), blocks_T(dst, 0)[b].bitcast(F32), ALU.subtract)\
                    .then_inc(turned_lo, 1)

            def ffn(l, w):
                at = plan["ffn", l, w]
                u, m, h, c, f = at["units"], at["items"], at["pairs"], at["copies"], (2 * l + w) * FT

                def hidden(j, it=None):
                    e = ev[:, (h + j) % 2]
                    add_halves(e, m + 2 * j, c + j, it)
                    dve.wait_ge(silu_done, plus(f + j + 1, it, STEPS))
                    own(nc.vector.tensor_tensor(e[:, 0, :], e[:, 0, :], e[:, 1, :], ALU.mult))
                    settle(it)
                    split_pair(aT[:, j % 2:j % 2 + 1], e[:, 0:1, :], it)

                for j in range(2):
                    ahead(("item", m + 2 * j + 1), -j)
                    hidden(j)
                first = state["next"]
                with dve.Fori(0, LOOPS) as it:
                    for s in range(STEPS):
                        for n in range(first + 3 * s, first + 3 * s + 3):
                            split_lo(n, it)
                        hidden(s + 2, it)
                state["next"] = first + LOOP_UNITS * LOOPS
                steps[0] += 2 * STEPS * (LOOPS - 1)

            def norm(e, parts, last=False):
                weight = 0.5 if e % 4 in (0, 3) else 1.0
                for b in range(TB):
                    ahead(("y", e, b))
                    dve.wait_ge(x_scaled, 2 * e + b + 1)
                    dve.wait_ge(pe_done, done["y", e, b])
                    z = x[:, b, :].rearrange("p (c s) -> p c s", c=2)
                    own(nc.vector.scalar_tensor_tensor(out=z, in0=ps[:, 4 + 2 * b:6 + 2 * b, :], scalar=weight,
                                                       in1=z, op0=ALU.mult, op1=ALU.add))
                    settle()
                    for c in range(2):
                        own(nc.vector.bn_stats(STATS[b][:, 6 * c:6 * c + 6], z[:, c, :]))
                    settle()
                    own(nc.vector.bn_aggr(MEANVAR[b], STATS[b]))
                    settle()
                    nc.vector.tensor_scalar(VEPS[b], MEANVAR[b][:, 1:2], LN_EPS, None, ALU.add)\
                        .then_inc(var_ready, 1)
                ahead(("y", e, 1), 1)
                dve.wait_ge(gains_landed, 32 * (e + 1))
                for b in range(TB):
                    own(nc.vector.scalar_tensor_tensor(out=x[:, b, :], in0=x[:, b, :], scalar=MEANVAR[b][:, 0:1],
                                                       in1=gb[:, 0, :], op0=ALU.subtract, op1=ALU.mult))
                    settle()
                    dve.wait_ge(rstd_ready, 2 * e + b + 1)
                    nc.vector.scalar_tensor_tensor(out=x[:, b, :], in0=x[:, b, :], scalar=RSTD[b], in1=gb[:, 1, :],
                                                   op0=ALU.mult, op1=ALU.add).then_inc(norm_done, 1)
                if last:
                    return
                for b in range(TB):
                    fill(parts[0:1] if b == 0 else parts[1:])
                    turn(4 + 2 * e + b, xT, b)

            def soft(j, tag, sums, masked, scales):
                ahead(tag)
                dve.wait_ge(scores_half, j + 1)
                for s, src in sums:
                    last = nc.vector.tensor_tensor(s, src, s, ALU.add)
                last.then_inc(scores_read, 1)
                dve.wait_ge(scores_read, j + 1)
                for s in masked:
                    own(nc.vector.memset(s, NEG_INF))
                settle()
                n = [s.shape[1] for s, _ in sums]
                for i, (s, _) in enumerate(sums):
                    own(nc.vector.tensor_reduce(MX[j % 2][:, 2 * i:2 * i + n[i]], s, AX.X, ALU.max))
                settle()
                for i, scale in enumerate(scales):
                    cols = slice(2 * i, 2 * i + n[i])
                    last = nc.vector.tensor_scalar(NEGM[j % 2][:, cols], MX[j % 2][:, cols], scale, -1.0,
                                                   ALU.mult, ALU.mult)
                last.then_inc(max_ready, 1)
                dve.wait_ge(exp_done, j + 1)
                own(nc.vector.reciprocal(REC[j % 2], SUM[j % 2]))
                settle()
                for i, (s, _) in enumerate(sums):
                    for k in range(n[i]):
                        last = nc.vector.tensor_scalar(s[:, k, :], s[:, k, :], REC[j % 2][:, 2 * i + k:2 * i + k + 1],
                                                       None, ALU.mult)
                last.then_inc(probs_ready, 1)

            def mix(l):
                at = plan["win", l]
                m, c = at["items"], at["copies"]
                ahead(("item", m + 1))
                add_halves(cqf[:, 0:2, :], m, c)
                dve.wait_ge(bank_free, m + 2)
                nc.vector.tensor_tensor(sq_q, cqf[:, 0:2, :], cqf[:, 0:2, :], ALU.mult)
                for t in range(2):
                    dve.wait_ge(cq_hi, 3 * l + t + 1)
                    nc.vector.scalar_tensor_tensor(out=cq[:, t, 1, :], in0=cqf[:, t, :], scalar=gains[:, l, t:t + 1],
                                                   in1=cq[:, t, 0, :].bitcast(F32), op0=ALU.mult, op1=ALU.subtract)\
                        .then_inc(cq_ready, 1)
                ahead(("item", m + 3))
                add_halves(kv_pe, m + 2, c + 1)
                dve.wait_ge(bank_free, m + 4)
                nc.vector.tensor_tensor(sq_kv, cqf[:, 2, :], cqf[:, 2, :], ALU.mult).then_inc(squares_ready, 1)
                dve.wait_ge(cq_hi, 3 * l + 3)
                nc.vector.scalar_tensor_tensor(out=cq[:, 2, 1, :], in0=cqf[:, 2, :], scalar=gains[:, l, 2:3],
                                               in1=cq[:, 2, 0, :].bitcast(F32), op0=ALU.mult, op1=ALU.subtract)\
                    .then_inc(cq_ready, 1)
                ahead(("item", m + 5))
                add_halves(poolU, m + 4, c + 2)
                for e in range(2):
                    own(nc.vector.memset(krT[(1 - e) * 64:(2 - e) * 64, e].bitcast(F32), 0.0))
                fill(FILL[l, "mix"])
                pairs(("uqA", l), qT[:, 0:4])
                pairs(("uqB", l), qT[:, 4:6])

                m = plan["stat", l]["items"]
                dve.wait_ge(pe_done, done["item", m])
                own(nc.vector.tensor_scalar(MS[:, 0:2], bank(m)[:, 0:2], 1.0 / Q_LORA, RMS_EPS, ALU.mult, ALU.add))
                nc.vector.tensor_scalar(MS[:, 2:4], bank(m)[:, 2:4], 1.0 / KV_LORA, RMS_EPS, ALU.mult, ALU.add)\
                    .then_inc(bank_free, 1)
                dve.wait_ge(item_hi, plan["stat", l]["his"] + 1)
                for t in range(2):
                    last = nc.vector.scalar_tensor_tensor(
                        out=mixT[:, t, 1, :], in0=bank(m + 1)[:, t * S:(t + 1) * S], scalar=pscale[:, l, t:t + 1],
                        in1=mixT[:, t, 0, :].bitcast(F32), op0=ALU.mult, op1=ALU.subtract)
                last.then_inc(bank_free, 1)

                m, c = plan["uqC", l]["items"], plan["uqC", l]["copies"]
                dve.wait_ge(rms_ready, l + 1)
                own(nc.vector.tensor_scalar(SRQ, RMS[:, 0:2], MLA_SCALE, None, ALU.mult))
                for b in range(TB):
                    last = nc.vector.tensor_scalar(diag[:, b, :], ident, RMS[:, 2 + b:3 + b], None, ALU.mult)
                last.then_inc(diag_ready, 1)
                ahead(("item", m + 1))
                add_halves(ropeX[:, 1:3, :], m, c)
                dve.wait_ge(half_copied, c + 2)
                nc.vector.tensor_tensor(ropeX[:, 3, :], bank(m + 2)[:, 0:S], ropeX[:, 3, :], ALU.add)\
                    .then_inc(bank_free, 1)
                dve.wait_ge(bank_free, m + 3)
                dve.wait_ge(pe_done, done["item", m + 3])
                nc.vector.tensor_copy(rkv_bc[:, :], bank(m + 3)[:, 0:S]).then_inc(bank_free, 1)
                dve.wait_ge(bank_free, m + 4)
                pairs(("kn", l), knT, rkv_bc[:, :].unsqueeze(1).broadcast_to([P, 2, S]))
                m = plan["v", l]["items"]
                for b in range(TB):
                    ahead(("item", m + 2 * b + 1))
                    dve.wait_ge(item_hi, plan["v", l]["his"] + b + 1)
                    k = (m + 2 * b) % BANKS
                    hi, lo = (v[:, b, i, :].rearrange("p (i s) -> p i s", i=2) for i in range(2))
                    nc.vector.scalar_tensor_tensor(out=lo, in0=ps[:, k:k + 2, 0:384], scalar=RMS[:, 2 + b:3 + b],
                                                   in1=hi.bitcast(F32), op0=ALU.mult, op1=ALU.subtract)\
                        .then_inc(bank_free, 2)

                m = plan["rot", l]["items"]
                for i in range(2):
                    z = ropeZ[:, 2 * i:2 * i + 2, :]
                    dve.wait_ge(pe_done, done["item", m + i])
                    nc.vector.tensor_tensor(z, bank(m + i).rearrange("p (t s) -> p t s", t=2),
                                            sinT[:, :].unsqueeze(1).broadcast_to([P, 2, S]), ALU.mult)\
                        .then_inc(bank_free, 1)
                own(nc.vector.tensor_tensor(ropeX, ropeX, cosT[:, :].unsqueeze(1).broadcast_to([P, 4, S]), ALU.mult))
                dve.wait_ge(bank_free, m + 2)
                settle()
                own(nc.vector.tensor_tensor(ropeZ, ropeZ, ropeX, ALU.add))
                settle()
                own(nc.vector.tensor_copy(qT[:, 6:9, 0, :], ropeZ[:, 1:4, :]))
                for e in range(2):
                    rows = slice(e * 64, e * 64 + 64)
                    own(nc.vector.tensor_copy(krT[rows, e, 0, :], ropeZ[rows, 0, :]))
                settle()
                own(nc.vector.tensor_tensor(qT[:, 6:9, 1, :], ropeZ[:, 1:4, :], qT[:, 6:9, 0, :].bitcast(F32),
                                            ALU.subtract))
                for e in range(2):
                    rows = slice(e * 64, e * 64 + 64)
                    last = nc.vector.tensor_tensor(krT[rows, e, 1, :], ropeZ[rows, 0, :],
                                                   krT[rows, e, 0, :].bitcast(F32), ALU.subtract)
                last.then_inc(rope_ready, 1)
                dve.wait_ge(rope_ready, l + 1)

                for pr in range(PAIRS + 1):
                    if pr < PAIRS:
                        s1, s0 = mla_scores(pr)
                        soft(5 * l + pr, ("score", l, pr),
                             [(s1, ps[:, 4:6, 0:S]),
                              (s0, ps[:, 6, :].rearrange("p (e c k) -> p e c k", e=2, c=2)[:, :, 0, :])],
                             [s1[0:CHUNK, :, P + CHUNK:2 * P], s0[0:CHUNK, :, CHUNK:P]],
                             [SRQ[:, 1:2], SRQ[:, 0:1]])
                    if pr > 0:
                        at = plan["pt", l, pr - 1]
                        for e in range(2):
                            ahead(("item", at["items"] + e))
                            item_lo(pT[:, e, 1, :], bank(at["items"] + e)[:, 0:384], pT[:, e, 0, :],
                                    at["his"] + e + 1)
                        pairs(("pv", l, pr - 1), mixT[:, 2 * pr:2 * pr + 2])

            def memory(l):
                pairs(("wq", l), qT[:, 0:8])
                for b in range(TB):
                    s = mem_scores(b)
                    soft(5 * l + PAIRS + b, ("mscore", l, b), [(s, ps[:, 4:8, 0:S])], [], [MEM_SCALE])
                at = plan["mpt", l]
                for hh in range(MEM_HEADS):
                    ahead(("item", at["items"] + hh))
                    hi, lo = (mpT[:, 2 * hh:2 * hh + 2, i, :] for i in range(2))
                    item_lo(lo, bank(at["items"] + hh).rearrange("p (k s) -> p k s", k=2), hi, at["his"] + hh + 1)
                pairs(("mpv", l), mixT[:, :])

            dve.wait_ge(consts_landed, 16)
            dve.wait_ge(pos_landed, 16)
            ang, turns = gb[:, 0, 2 * S:3 * S], gb[:, 0, 3 * S:4 * S]
            own(nc.vector.tensor_copy(ang, gb[:, 1, 0:S].bitcast(I32)))
            settle()
            own(nc.vector.tensor_scalar(ang, ang, cst[:, C_FREQ:C_FREQ + 1], None, ALU.mult))
            settle()
            for i, quarter in enumerate((0.25, 0.0)):
                r = gb[:, 0, i * S:(i + 1) * S]
                own(nc.vector.tensor_scalar(turns, ang, 1.0 / (2.0 * math.pi), quarter, ALU.mult, ALU.add))
                settle()
                own(nc.vector.tensor_scalar(turns, turns, ROUND, None, ALU.add))
                settle()
                own(nc.vector.tensor_scalar(turns, turns, ROUND, None, ALU.subtract))
                settle()
                for k, part in enumerate(TURN):
                    own(nc.vector.scalar_tensor_tensor(out=r, in0=turns, scalar=-part, in1=ang if k == 0 else r,
                                                       op0=ALU.mult, op1=ALU.add))
                    settle()
                own(nc.vector.tensor_scalar(r, r, quarter * 2.0 * math.pi, PI_IN, ALU.add, ALU.min))
                settle()
                nc.vector.tensor_scalar(r, r, -PI_IN, None, ALU.max).then_inc(angles_ready, 1)

            for b in range(TB):
                turn(b, memT, b)
            fill(FILL[0, "start"])
            for b in range(TB):
                turn(2 + b, xT, b)
            dve.wait_ge(small_landed, 16 * SMALL)
            for l in range(L):
                ffn(l, 0)
                norm(4 * l, FILL[l, "ln0"])
                mix(l)
                norm(4 * l + 1, FILL[l, "ln1"])
                memory(l)
                norm(4 * l + 2, FILL[l, "ln2"])
                ffn(l, 1)
                norm(4 * l + 3, FILL[l, "ln3"], last=l == L - 1)

        @block.gpsimd
        def _(pool):
            steps = [0]

            def own(ins):
                steps[0] += 1
                ins.then_inc(pool_step, 1)
                pool.wait_ge(pool_step, steps[0])

            def load_gains(e):
                for i, w in enumerate(("ln_g", "ln_b")):
                    pool.dma_start(gb[:, i, :], a[w][e // 4, e % 4:e % 4 + 1, :].partition_broadcast(P))\
                        .then_inc(gains_landed, 16)

            def scale_x(job, e):
                for b in range(TB):
                    pool.wait_ge(pe_done, done["turned", job + b])
                    nc.gpsimd.tensor_scalar(x[:, b, :], x[:, b, :], ALPHA, 1.0, ALU.mult, ALU.mult)\
                        .then_inc(x_scaled, 1)

            def norm(e):
                for b in range(TB):
                    pool.wait_ge(var_ready, 2 * e + b + 1)
                    nc.gpsimd.tensor_tensor(RSTD[b], VEPS[b], cst[:, C_HALF:C_HALF + 1], ALU.pow)\
                        .then_inc(rstd_ready, 1)
                if e < 4 * L - 1:
                    if e % 4:
                        pool.wait_ge(norm_done, 2 * e + 2)
                        load_gains(e + 1)
                    scale_x(4 + 2 * e, e)

            def pool_group(l):
                m = plan["win", l]["items"] + 6
                pool.wait_ge(bank_free, m)
                src = poolU
                for i, shift in enumerate((1, 2, 4, 8)):
                    dst = (poolA, poolB)[i % 2]
                    own(nc.gpsimd.tensor_tensor(dst[:, :, shift:S], src[:, :, shift:S], src[:, :, 0:S - shift],
                                                ALU.add))
                    own(nc.gpsimd.tensor_copy(dst[:, :, 0:shift], src[:, :, 0:shift]))
                    keep = ((0, 0), (64, 0), (0, 1), (64, 1))[i]
                    rows = slice(keep[0], keep[0] + 64)
                    own(nc.gpsimd.tensor_copy(poolM[rows, keep[1], :], dst[rows, keep[1], :]))
                    src = dst
                own(nc.gpsimd.tensor_tensor(poolM[:, :, :], poolM[:, :, :], inv_count, ALU.mult))
                nc.gpsimd.tensor_tensor(poolB, poolM[:, :, :], poolU, ALU.subtract).then_inc(pooled, 1)

            own(nc.gpsimd.memset(pw[:, :, :, :], 0.0))
            for l in range(L):
                for g in range(len(POOL_WINDOWS)):
                    rows = slice((g % 2) * 64, (g % 2 + 1) * 64)
                    pool.dma_start(pw[rows, l, g // 2, rows], a["pool_w"][l, g]).then_inc(small_landed, 16)
                for dst, w, t in ((gains[:, l, 0:1], "q_norm_g", 0), (gains[:, l, 1:2], "q_norm_g", 1),
                                  (gains[:, l, 2:3], "kv_norm_g", 0), (pscale[:, l, 0:1], "pool_scale", 0),
                                  (pscale[:, l, 1:2], "pool_scale", 1)):
                    pool.dma_start(dst, a[w][l, t * P:(t + 1) * P].rearrange("(p o) -> p o", o=1))\
                        .then_inc(small_landed, 16)
            pool.dma_start(gb[:, 1, 0:S].bitcast(I32), a["positions"].partition_broadcast(P)).then_inc(pos_landed, 16)
            pool.wait_ge(tables_done, 1)
            load_gains(0)
            scale_x(2, -1)
            for l in range(L):
                norm(4 * l)
                pool_group(l)
                pool.wait_ge(bank_free, plan["stat", l]["items"] + 1)
                nc.gpsimd.tensor_tensor(RMS, MS, cst[:, C_HALF:C_HALF + 1].broadcast_to([P, 4]), ALU.pow)\
                    .then_inc(rms_ready, 1)
                pool.wait_ge(bank_free, plan["stat", l]["items"] + 2)
                load_gains(4 * l + 1)
                for s in range(1, 4):
                    norm(4 * l + s)


_INS = ["x", "mem", "positions", "ln_g", "ln_b", "ffn1_w13", "ffn1_w2", "w_in", "pool_w", "pool_scale",
        "q_norm_g", "w_uq", "kv_norm_g", "w_ukv", "w_out", "mem_wq", "mem_wkv", "mem_wo", "ffn2_w13", "ffn2_w2"]


def kernel(**inputs):
    import concourse.bacc as bacc
    from concourse.bass_utils import run_bass_kernel_spmd

    nc = bacc.Bacc("TRN2", target_bir_lowering=False, num_devices=1)
    arrays = {f"in_{n}": np.ascontiguousarray(inputs[n]) for n in _INS}
    arrays["in_constants"] = constants(inputs["x"].shape[1])
    aps = {n: nc.dram_tensor(n, v.shape, mybir.dt.from_np(v.dtype), kind="ExternalInput").ap()
           for n, v in arrays.items()}
    out = nc.dram_tensor("out_0", inputs["x"].shape, F32, kind="ExternalOutput").ap()
    trunk(nc, {n: aps[f"in_{n}"] for n in _INS}, aps["in_constants"], out)
    r = run_bass_kernel_spmd(nc, [arrays], core_ids=[0])
    return r.results[0]["out_0"]
```

```python
import math
from contextlib import ExitStack

import numpy as np
import concourse.bass as bass
from concourse import mybir

F32 = mybir.dt.float32
F32R = mybir.dt.float32r
I32 = mybir.dt.int32
ALU = mybir.AluOpType
ACT = mybir.ActivationFunctionType
AX = mybir.AxisListType

P = 128
POOL_WINDOWS = (2, 4, 8, 16)
CHUNK = 64
MEM_HEADS = 4
QK_NOPE, QK_ROPE, V_HEAD = 128, 64, 128
ROPE_BASE = 10000.0
LN_EPS, RMS_EPS, NEG_INF = 1e-5, 1e-6, -1e30

UNIT = 1024
RAW = 4
SLOTS = 6
HALVES = 2
BANKS = 4
STEPS = 4

C_ID, C_ROT, C_ONE, C_CNT, C_FREQ, C_HALF = 0, 128, 256, 384, 896, 897
C_ALL = 898

TURN, _rest = [], 2.0 * math.pi
for _shift in (5, 17, 25):
    TURN.append(math.floor(_rest * 2.0 ** _shift) / 2.0 ** _shift)
    _rest -= TURN[-1]
TURN.append(_rest)
ROUND = 1.5 * 2.0 ** 23
PI_IN = 3.1415925


def constants(seq):
    c = np.zeros((P, C_ALL), np.float32)
    c[:, C_ID:C_ID + P] = np.eye(P)
    half = QK_ROPE // 2
    for p in range(P):
        if p % QK_ROPE < half:
            c[p + half, C_ROT + p] = -1.0
        else:
            c[p - half, C_ROT + p] = 1.0
    c[:, C_ONE:C_ONE + P] = 1.0
    for tile in range(2):
        for p in range(P):
            w = POOL_WINDOWS[2 * tile + p // 64]
            c[p, C_CNT + tile * seq:C_CNT + (tile + 1) * seq] = 1.0 / np.minimum(np.arange(seq) + 1, w)
    c[:, C_FREQ] = (np.float32(ROPE_BASE) ** (-np.arange(half, dtype=np.float32) / half))[np.arange(P) % half]
    c[:, C_HALF] = -0.5
    return c


class Plan:

    def __init__(self):
        self.at, self.done, self.units_by = {}, {}, []
        self.n = dict(units=0, items=0)

    def section(self, name, marks):
        self.at[name] = dict(self.n)
        for mark in marks:
            for what in mark:
                if what == "U":
                    self.done["unit", self.n["units"]] = len(self.units_by) + 1
                    self.n["units"] += 1
                elif what == "I":
                    self.done["item", self.n["items"]] = len(self.units_by) + 1
                    self.n["items"] += 1
                else:
                    self.done[what] = len(self.units_by) + 1
            self.units_by.append(self.n["units"])

    def __getitem__(self, name):
        return self.at[name]


def trunk(nc, a, consts, out):
    L, D, F2 = a["ffn1_w13"].shape
    S = a["x"].shape[1]
    F = F2 // 2
    KT, TB, FT = D // P, S // P, F // P
    H = a["w_ukv"].shape[2] // (QK_NOPE + V_HEAD)
    Q_LORA, KV_LORA = a["w_uq"].shape[1], a["w_ukv"].shape[1]
    POOL_W = len(POOL_WINDOWS) * 64
    assert (S, D, FT, H, Q_LORA, KV_LORA) == (256, 1024, 22, 6, 256, 128)
    ALPHA = (2 * L) ** 0.25
    MLA_SCALE = (QK_NOPE + QK_ROPE) ** -0.5
    MEM_SCALE = (D // MEM_HEADS) ** -0.5
    PAIRS = H // 2
    SMALL = L * (len(POOL_WINDOWS) + 5)
    ROWS_TAIL, FFN_TAIL = 4, 3
    LOOPS = (FT - 6) // STEPS
    LOOP_UNITS = 3 * STEPS
    assert LOOPS * STEPS == FT - 6 and LOOP_UNITS % SLOTS == 0 and LOOP_UNITS % RAW == 0 and STEPS % BANKS == 0

    FILL = {
        (0, "ln0"): [(0, 0)], (0, "sums"): [(0, 1)], (0, "rsqrt"): [], (0, "v"): [(0, 2)], (0, "pt0"): [(0, 3)], (0, "pt1"): [(0, 4)],
        (0, "ln1"): [(0, 5)], (0, "soft"): [(1, 0)], (0, "ln2"): [(1, 1)], (0, "ln3"): [],
        (1, "ln0"): [(1, 2)], (1, "sums"): [(1, 3)], (1, "rsqrt"): [], (1, "v"): [], (1, "pt0"): [(1, 4)], (1, "pt1"): [],
        (1, "ln1"): [], (1, "soft"): [(1, 5)], (1, "ln2"): [], (1, "ln3"): []}

    MLA_ORDER = [("score", 0), ("score", 1), ("scale", 0), ("fill", "pt0"), ("pt", 0), ("score", 2), ("scale", 1),
                 ("pv", 0), ("pt", 1), ("scale", 2), ("fill", "pt1"), ("pv", 1), ("pt", 2), ("pv", 2)]
    MEM_ORDER = [("score", 0), ("score", 1), ("scale", 0), ("scale", 1), ("fill", "soft"), ("pt", 0), ("pt", 1),
                 ("pv", 0), ("pt", 2), ("pv", 1), ("pt", 3), ("pv", 2), ("pv", 3)]

    plan = Plan()
    UI, ITEM, UNIT_ = ["U", "I"], ["I"], ["U"]

    def plan_fill(l, place):
        for part in FILL[l, place]:
            plan.section(("kv", *part), [UNIT_, UI] if part[1] < 4 else [UNIT_, UI, UNIT_, UI])

    def plan_rows(name, e):
        plan.section(name, [UNIT_] * (KT - ROWS_TAIL) + [[("y", e, 0)]] + [UNIT_] * (ROWS_TAIL - 1)
                     + [["U", ("y", e, 1)]])

    def plan_turn(job):
        plan.section(("turn", job), turned(job))

    def turned(job):
        return [[("turned", job, c)] for c in range(HALVES)]

    def plan_norm(e, l, place):
        plan_fill(l, place)
        for b in range(TB):
            plan_turn(4 + 2 * e + b)

    def plan_ffn(l, w):
        e = 4 * l + 3 * w
        meanwhile = turned(2) + turned(3) if e == 0 else []
        plan.section(("ffn", l, w), [UNIT_, UI] + meanwhile + [UNIT_, UI, UNIT_] + [UNIT_, UI, UNIT_] * (FT - 4)
                     + [UNIT_, UI] * 2 + [[("y", e, 0)]] + [UNIT_] * (FFN_TAIL - 1) + [["U", ("y", e, 1)]])

    for b in range(TB):
        plan_turn(b)
    for l in range(L):
        plan_ffn(l, 0)
        plan_norm(4 * l, l, "ln0")
        plan.section(("win", l), [UNIT_, UI] * 3)
        plan.section(("sums", l), [ITEM])
        plan_fill(l, "sums")
        plan.section(("rsqrt", l), [ITEM])
        plan_fill(l, "rsqrt")
        plan.section(("uqC", l), [ITEM, UI])
        plan.section(("uqA", l), [ITEM, UI])
        plan.section(("rot", l), [ITEM] * 2)
        plan.section(("pool", l), [ITEM])
        plan.section(("uqB", l), [UI])
        plan.section(("kn", l), [ITEM] * 2 + [UI])
        plan.section(("v", l), [ITEM] * 3 + [UI])
        plan_fill(l, "v")
        for step, i in MLA_ORDER:
            if step == "fill":
                plan_fill(l, i)
            elif step != "scale":
                plan.section((step, l, i), {"score": [[("score", l, i)]], "pt": [ITEM] * 2, "pv": [ITEM]}[step])
        plan_rows(("wout", l), 4 * l + 1)
        plan_norm(4 * l + 1, l, "ln1")
        plan.section(("wq", l), [UNIT_, UI] * (KT // 2))
        for step, i in MEM_ORDER:
            if step == "fill":
                plan_fill(l, i)
            elif step != "scale":
                plan.section(("m" + step, l, i), {"score": [[("mscore", l, i)]], "pt": [ITEM], "pv": [ITEM]}[step])
        plan_rows(("wo", l), 4 * l + 2)
        plan_norm(4 * l + 2, l, "ln2")
        plan_ffn(l, 1)
        if l < L - 1:
            plan_norm(4 * l + 3, l, "ln3")
    done = plan.done
    UNITS = plan.n["units"]

    def first_of_stage(e):
        return plan[(("win", e // 4), ("wq", e // 4), ("ffn", e // 4, 1), ("ffn", e // 4 + 1, 0))[e % 4]]["units"]

    slot, last_user, free_after = [], [], []
    latest = [k - SLOTS for k in range(SLOTS)]
    for n in range(UNITS):
        usable = list(range(SLOTS))
        after = 0
        for l in range(L):
            if plan["v", l]["units"] <= n < plan["wout", l]["units"] + 4:
                usable.remove(4)
            if plan["win", l]["units"] + 2 <= n < plan["wout", l]["units"] + 5:
                usable.remove(5)
        k = min(usable, key=lambda k: latest[k])
        for l in range(L):
            if k >= 4 and latest[k] < plan["wout", l]["units"] <= n:
                after = done["item", plan["pv", l, PAIRS - 1]["items"]]
        slot.append(k)
        last_user.append(latest[k])
        free_after.append(max(after, done["unit", latest[k]] if latest[k] >= 0 else 0))
        latest[k] = n

    w13 = [a["ffn1_w13"], a["ffn2_w13"]]
    w2 = [a["ffn1_w2"], a["ffn2_w2"]]

    def columns(w, lo, n):
        return w.rearrange("(k p) f -> p k f", p=P)[:, :, lo:lo + n]

    def ffn_units(base, j):
        g = base if j == 0 else base + 3 * j - 1 if j < FT - 1 else base + 3 * j - 2
        d = base + 3 * j + 4 if j < FT - FFN_TAIL else base + 3 * FT - FFN_TAIL + (j - (FT - FFN_TAIL))
        return g, g + 1, d

    source = {}
    for l in range(L):
        for i in range(4):
            u = plan["kv", l, i]["units"]
            for t in range(2):
                source[u + t] = (UNIT, [(0, columns(a["mem_wkv"][l], (2 * i + t) * P, P))])
        for i in range(2):
            u = plan["kv", l, 4 + i]["units"]
            for t in range(4):
                quarter, half = 2 * i + t // 2, t % 2
                source[u + t] = (UNIT, [(0, columns(a["mem_wkv"][l][half * 512:(half + 1) * 512, :],
                                                    D + quarter * 256, 256))])
        u = plan["win", l]["units"]
        c_q, c_kv, k_pe = POOL_W, POOL_W + Q_LORA, POOL_W + Q_LORA + KV_LORA
        for t, lo in enumerate((c_q, c_q + P, c_kv)):
            source[u + t] = (UNIT, [(0, columns(a["w_in"][l], lo, P))])
        pe_cols = columns(a["w_in"][l], k_pe, QK_ROPE)
        source[u + 3] = (UNIT, [(0, pe_cols), (QK_ROPE, pe_cols)])
        for t in range(2):
            source[u + 4 + t] = (UNIT, [(0, columns(a["w_in"][l], t * P, P))])
        uq = a["w_uq"][l].rearrange("(k p) (h c) -> p k h c", p=P, h=H)
        ukv = a["w_ukv"][l].rearrange("p (h c) -> p h c", h=H)
        for name, heads, cols in (("uqA", slice(0, 4), slice(0, QK_NOPE)), ("uqB", slice(4, 6), slice(0, QK_NOPE)),
                                  ("uqC", slice(0, 6), slice(QK_NOPE, QK_NOPE + QK_ROPE))):
            size = (heads.stop - heads.start) * (cols.stop - cols.start)
            source[plan[name, l]["units"]] = (2 * size, [(k * size, uq[:, k, heads, cols]) for k in range(2)])
        source[plan["kn", l]["units"]] = (H * QK_NOPE, [(0, ukv[:, :, 0:QK_NOPE])])
        source[plan["v", l]["units"]] = (H * V_HEAD, [(0, ukv[:, :, QK_NOPE:QK_NOPE + V_HEAD])])
        for r in range(KT):
            source[plan["wout", l]["units"] + r] = (UNIT, [(0, a["w_out"][l][r * P:(r + 1) * P, :])])
            source[plan["wo", l]["units"] + r] = (UNIT, [(0, a["mem_wo"][l][r * P:(r + 1) * P, :])])
            source[plan["wq", l]["units"] + r] = (UNIT, [(0, columns(a["mem_wq"][l], r * P, P))])
        for w in range(2):
            for j in range(FT):
                g, up, d = ffn_units(plan["ffn", l, w]["units"], j)
                source[g] = (UNIT, [(0, columns(w13[w][l], j * P, P))])
                source[up] = (UNIT, [(0, columns(w13[w][l], F + j * P, P))])
                source[d] = (UNIT, [(0, w2[w][l][j * P:(j + 1) * P, :])])
    assert sorted(source) == list(range(UNITS))

    with ExitStack() as ctx:
        def sb(name, shape, dt=F32):
            return ctx.enter_context(nc.sbuf_tensor(name, shape, dt))

        def sem(name):
            return ctx.enter_context(nc.semaphore(name))

        raw = sb("raw", [P, RAW, UNIT])
        w_hi = sb("w_hi", [P, 4, UNIT], F32R)
        w_lo = sb("w_lo", [P, 4, UNIT], F32R)
        x = sb("x", [P, TB, D])
        tmp = sb("tmp", [P, 2 * D])
        gb = sb("gb", [P, 2, D])
        xT = sb("xT", [P, KT, 2, S], F32R)
        memT = sb("memT", [P, KT, 2, S], F32R)
        memK = sb("memK", [P, KT, 2, S], F32R)
        memV = sb("memV", [P, TB, 2, D], F32R)
        qT = sb("qT", [P, 9, 2, S], F32R)
        v_flat = sb("v_flat", [P, TB * 2 * H * V_HEAD], F32R)
        mixT = sb("mixT", [P, KT, 2, S], F32R)
        cqp = sb("cqp", [P, 6 * S], F32R)
        ev = sb("ev", [P, 2, S])
        cst = sb("cst", [P, C_ALL])
        cosT = sb("cosT", [P, S])
        sinT = sb("sinT", [P, S])
        diag = sb("diag", [P, 2, S])
        pw = sb("pw", [P, L, 2, P])
        pscale = sb("pscale", [P, L, 2])
        gains = sb("gains", [P, L, 3])
        st = sb("st", [P, 96])
        poolM = sb("poolM", [P, 2, S])
        ps = ctx.enter_context(nc.psum_tensor("ps", [P, 8, 512], F32))

        slot_hi = [w_hi[:, k, :] for k in range(4)] + [v_flat[:, 0:UNIT], v_flat[:, 2 * UNIT:3 * UNIT]]
        slot_lo = [w_lo[:, k, :] for k in range(4)] + [v_flat[:, UNIT:2 * UNIT], cqp[:, 0:UNIT]]

        v = v_flat[:, :].rearrange("p (b c f) -> p b c f", b=TB, c=2)
        knT, krT = xT[:, 0:6], xT[:, 6:8]
        mpT = xT
        aT = mixT
        cq = cqp[:, :].rearrange("p (t c s) -> p t c s", t=3, c=2)
        turned_probs = [
            t.rearrange("p (e c k) -> p e c k", e=2, c=2)
            for t in (cqp[:, :], qT[:, 0:3].rearrange("p t c s -> p (t c s)"), cqp[:, :])]
        ident, rot, ones = cst[:, C_ID:C_ID + P], cst[:, C_ROT:C_ROT + P], cst[:, C_ONE:C_ONE + P]
        inv_count = cst[:, C_CNT:C_CNT + 2 * S].rearrange("p (t s) -> p t s", t=2)

        raw_landed = [sem(f"raw_landed{i}") for i in range(RAW)]
        hi_done, lo_done, pe_done, bank_free = sem("hi_done"), sem("lo_done"), sem("pe_done"), sem("bank_free")
        item_hi, silu_done, hidden_ready = sem("item_hi"), sem("silu_done"), sem("hidden_ready")
        turned_hi, turned_lo = sem("turned_hi"), sem("turned_lo")
        norm_done, x_scaled, var_ready, rstd_ready = (
            sem("norm_done"), sem("x_scaled"), sem("var_ready"), sem("rstd_ready"))
        gains_landed, ident_landed, consts_landed, mem_landed, x_landed, small_landed, pos_landed = (
            sem("gains_landed"), sem("ident_landed"), sem("consts_landed"), sem("mem_landed"), sem("x_landed"),
            sem("small_landed"), sem("pos_landed"))
        dve_step, pool_step = sem("dve_step"), sem("pool_step")
        angles_ready, tables_done = sem("angles_ready"), sem("tables_done")
        squares_ready, rms_ready, diag_ready, cq_scaled, cq_hi, cq_ready = (
            sem("squares_ready"), sem("rms_ready"), sem("diag_ready"), sem("cq_scaled"), sem("cq_hi"), sem("cq_ready"))
        pooled, rope_sum, rope_hi, rope_ready = sem("pooled"), sem("rope_sum"), sem("rope_hi"), sem("rope_ready")
        max_ready, exp_done, probs_ready, stored = (
            sem("max_ready"), sem("exp_done"), sem("probs_ready"), sem("stored"))

        def plus(n, it, per):
            return n if it is None else n + it * per

        def bank(m):
            return ps[:, m % BANKS, :]

        def two(t):
            return t.rearrange("p (t s) -> p t s", t=2)

        def half_T(t, part, b, c):
            return t[:, 4 * c:4 * c + 4, part, b * P:(b + 1) * P]

        def turned_half(b, c):
            return ps[:, 4 + 2 * b + c, :].rearrange("p (k s) -> p k s", s=P)

        STATS = [st[:, 12 * b:12 * b + 12] for b in range(2)]
        MEANVAR = [st[:, 28 + 4 * b:30 + 4 * b] for b in range(2)]
        VEPS = [st[:, 30 + 4 * b:31 + 4 * b] for b in range(2)]
        RSTD = [st[:, 31 + 4 * b:32 + 4 * b] for b in range(2)]
        MS, RMS = st[:, 88:92], st[:, 92:96]
        MX, NEGM, SUM, REC = ([st[:, 36 + 12 * q + 4 * i:40 + 12 * q + 4 * i] for i in range(3)] for q in range(4))

        def tiles(t, n):
            return t.rearrange("p (t s) -> p t s", t=n)

        cqf = tiles(tmp[:, 0:3 * S], 3)
        sq_kv = tmp[:, 3 * S:4 * S]
        ropeX = tiles(tmp[:, 4 * S:8 * S], 4)
        ropeZ = tiles(tmp[:, 0:4 * S], 4)
        kv_pe = tiles(tmp[:, 2 * S:6 * S], 4)[:, 0:3:2]
        poolU, poolA = tiles(gb[:, 0, 0:512], 2), tiles(gb[:, 0, 512:1024], 2)
        poolB, sq_q = tiles(gb[:, 1, 0:512], 2), tiles(gb[:, 1, 512:1024], 2)

        def mla_scores(pr):
            k = 4 + 2 * (pr % 2)
            return two(ps[:, k, :]), ps[:, k + 1, 0:2 * P].rearrange("p (e k) -> p e k", e=2)

        def mla_probs(pr):
            s = tmp[:, 768 * (pr % 2):768 * (pr % 2) + 768]
            return two(s[:, 0:512]), s[:, 512:768].rearrange("p (e k) -> p e k", e=2)

        def mem_scores(b):
            return ps[:, 4 + 2 * b:6 + 2 * b, :].rearrange("p b (h k) -> p (b h) k", h=2)

        def mem_probs(b):
            return tmp[:, b * D:(b + 1) * D].rearrange("p (h k) -> p h k", h=MEM_HEADS)

        def turned_value(job, c):
            return HALVES * job + c + 1

        def normed(e, b, c):
            return HALVES * (2 * e + b) + c + 1

        block = ctx.enter_context(nc.Block())

        @block.sync
        def _(sp):
            sp.dma_start(cst[:, 0:P], consts[:, 0:P]).then_inc(ident_landed, 16)
            for b in range(TB):
                sp.dma_start(x[:, b, :], a["x"][0, b * P:(b + 1) * P, :]).then_inc(x_landed, 16)

            def load(n, parts, it=None):
                if n >= RAW:
                    sp.wait_ge(lo_done, plus(n - RAW + 1, it, LOOP_UNITS))
                k = n % RAW
                for col, src in parts:
                    if len(src.shape) == 2:
                        dst = raw[:, k, :]
                    elif src.shape[2] == QK_ROPE and src.shape[1] == KT:
                        dst = raw[:, k, :].rearrange("p (t c) -> p t c", t=KT)[:, :, col:col + QK_ROPE]
                    else:
                        t, c = src.shape[1:]
                        dst = raw[:, k, col:col + t * c].rearrange("p (t c) -> p t c", t=t)
                    sp.dma_start(dst, src).then_inc(raw_landed[k], 16)

            n = 0
            for l in range(L):
                for w in range(2):
                    u = plan["ffn", l, w]["units"]
                    for n in range(n, u + 5):
                        load(n, source[n][1])
                    cols13 = w13[w][l].rearrange("(k p) f -> p k f", p=P)
                    with sp.Fori(0, LOOPS) as it:
                        for s in range(STEPS):
                            g = u + 5 + 3 * s
                            col = it * (STEPS * P) + (s + 2) * P
                            load(g, [(0, cols13[:, :, bass.ds(col, P)])], it)
                            load(g + 1, [(0, cols13[:, :, bass.ds(col + F, P)])], it)
                            load(g + 2, [(0, w2[w][l][bass.ds(col - P, P), :])], it)
                    n = u + 5 + LOOP_UNITS * LOOPS
            for n in range(n, UNITS):
                load(n, source[n][1])
            for b in range(TB):
                sp.wait_ge(norm_done, normed(4 * L - 1, b, 1))
                sp.dma_start(out[0, b * P:(b + 1) * P, :], x[:, b, :]).then_inc(stored, 16)
            sp.wait_ge(stored, 16 * TB)

        def landed(n):
            return sum(16 * len(source[k][1]) for k in range(n % RAW, n + 1, RAW))

        @block.tensor
        def _(pe):
            milestones = [0]

            def reach(ins, *tags):
                milestones[0] += 1
                for tag in tags:
                    assert done[tag] == milestones[0], (tag, done[tag], milestones[0])
                ins.then_inc(pe_done, 1)

            def product(dst, stand, move, start, stop):
                return nc.tensor.matmul(dst, stand, move, start=start, stop=stop, skip_group_check=True)

            def split_product(dst, stand, move, start, stop):
                product(dst, stand[0], move[0], start, False)
                product(dst, stand[0], move[1], False, False)
                return product(dst, stand[1], move[0], False, stop)

            def take_bank(m, it=None):
                if m >= BANKS:
                    pe.wait_ge(bank_free, plus(m - BANKS + 1, it, STEPS))

            def unit_split(n, it=None):
                pe.wait_ge(lo_done, plus(n + 1, it, LOOP_UNITS))

            def column_tile(m, c, n, offsets, acts, arrival=None):
                hi, lo = slot_hi[slot[n]], slot_lo[slot[n]]
                for i, (o, act) in enumerate(zip(offsets, acts)):
                    if arrival is not None and i in (0, KT // 2):
                        pe.wait_ge(turned_lo, turned_value(arrival, i // (KT // 2)))
                    last = split_product(two(bank(m))[:, c, :], (hi[:, o:o + P], lo[:, o:o + P]),
                                         (act[:, 0, :], act[:, 1, :]), c == 0 and i == 0, i == len(acts) - 1)
                return last

            def column_pair(m, n, acts, it=None, arrival=None):
                take_bank(m, it)
                for c in range(2):
                    unit_split(n + c, it)
                    last = column_tile(m, c, n + c, range(0, D, P), [acts[:, k] for k in range(KT)],
                                       None if c else arrival)
                    reach(last, ("unit", n + c), *([("item", m)] if c else []))

            def row_block(n, act, b, first, last_unit):
                hi, lo = act[:, 0, b * P:(b + 1) * P], act[:, 1, b * P:(b + 1) * P]
                for stand, ring, start in ((hi, slot_hi, first), (hi, slot_lo, False), (lo, slot_hi, False)):
                    for c in range(2):
                        last = product(ps[:, 4 + 2 * b + c, :], stand, ring[slot[n]][:, c * 512:(c + 1) * 512],
                                       start, last_unit and stand is lo)
                return last

            def row_unit(n, act, first=False, it=None):
                unit_split(n, it)
                for b in range(TB):
                    last = row_block(n, act, b, first, False)
                reach(last, ("unit", n))

            def row_tail(e, units, acts, wait_for):
                for b in range(TB):
                    for i, n in enumerate(units):
                        if b == 0:
                            unit_split(n)
                            wait_for(i)
                        last = row_block(n, acts[i], b, False, i == len(units) - 1)
                        if b == 1:
                            reach(last, ("unit", n), *([("y", e, 1)] if i == len(units) - 1 else []))
                    if b == 0:
                        reach(last, ("y", e, 0))

            def turn(job, src, b, e=None):
                for c in range(HALVES):
                    if e is not None:
                        pe.wait_ge(norm_done, normed(e, b, c))
                    for k in range(4 * c, 4 * c + 4):
                        last = nc.tensor.transpose(ps[:, 4 + 2 * b + c, (k % 4) * P:(k % 4 + 1) * P],
                                                   src[:, k * P:(k + 1) * P], ident)
                    reach(last, ("turned", job, c))

            def fill(l, place):
                for l, i in FILL[l, place]:
                    u, m = plan["kv", l, i]["units"], plan["kv", l, i]["items"]
                    pe.wait_ge(turned_lo, turned_value(3, 1))
                    if i < 4:
                        column_pair(m, u, memT)
                        continue
                    for t in range(2):
                        take_bank(m + t)
                        for half in range(2):
                            n = u + 2 * t + half
                            unit_split(n)
                            for b in range(TB):
                                for k in range(4):
                                    act = memT[:, 4 * half + k, :, b * P:(b + 1) * P]
                                    cols = slice(k * 256, (k + 1) * 256)
                                    last = split_product(
                                        bank(m + t)[:, b * S:(b + 1) * S], (act[:, 0, :], act[:, 1, :]),
                                        (slot_hi[slot[n]][:, cols], slot_lo[slot[n]][:, cols]),
                                        half == 0 and b == 0 and k == 0, half == 1 and k == 3)
                            reach(last, ("unit", n), *([("item", m + t)] if half else []))

            def norm(e, l, place):
                fill(l, place)
                for b in range(TB):
                    turn(4 + 2 * e + b, x[:, b, :], b, e)

            def ffn(l, w):
                e, f = 4 * l + 3 * w, (2 * l + w) * FT
                u, m = plan["ffn", l, w]["units"], plan["ffn", l, w]["items"]

                def up(j, it=None, arrival=None):
                    column_pair(m + j, ffn_units(u, j)[0], xT, it, arrival)

                def down(j, it=None, first=False):
                    pe.wait_ge(hidden_ready, plus(f + j + 1, it, STEPS))
                    row_unit(ffn_units(u, j)[2], aT[:, j % 4], first, it)

                up(0, arrival=1 if e == 0 else 3 + 2 * e)
                if e == 0:
                    pe.wait_ge(mem_landed, 16)
                    for b in range(TB):
                        turn(2 + b, tmp[:, b * D:(b + 1) * D], b)
                up(1)
                if e == 0:
                    pe.wait_ge(turned_lo, turned_value(3, 1))
                down(0, first=True)
                with pe.Fori(0, LOOPS) as it:
                    for s in range(STEPS):
                        up(s + 2, it)
                        down(s + 1, it)
                milestones[0] += LOOP_UNITS * (LOOPS - 1)
                for j in (FT - 4, FT - 3):
                    up(j)
                    down(j - 1)
                up(FT - 2)
                up(FT - 1)
                tail = range(FT - FFN_TAIL, FT)
                row_tail(e, [ffn_units(u, j)[2] for j in tail], [aT[:, j % 4] for j in tail],
                         lambda i: pe.wait_ge(hidden_ready, f + tail[i] + 1))

            def mix(l):
                at = {k: plan[k, l] for k in ("win", "sums", "rsqrt", "uqA", "uqB", "uqC", "kn", "v", "rot", "pool")}
                for t in range(3):
                    column_pair(at["win"]["items"] + t, at["win"]["units"] + 2 * t, xT,
                                arrival=None if t else 5 + 2 * (4 * l))

                m = at["sums"]["items"]
                take_bank(m)
                pe.wait_ge(squares_ready, l + 1)
                for b in range(TB):
                    rows = slice(b * P, (b + 1) * P)
                    for t in range(2):
                        nc.tensor.matmul(bank(m)[:, b:b + 1], sq_q[:, t, rows], ones[:, 0:1],
                                         start=b == 0 and t == 0, stop=t == 1, skip_group_check=True)
                    last = nc.tensor.matmul(bank(m)[:, 2 + b:3 + b], sq_kv[:, rows], ones[:, 0:1],
                                            start=False, stop=True, skip_group_check=True)
                reach(last, ("item", m))
                fill(l, "sums")
                m = at["rsqrt"]["items"]
                take_bank(m)
                pe.wait_ge(diag_ready, l + 1)
                for i in range(2):
                    for b in range(TB):
                        last = nc.tensor.matmul(two(bank(m))[:, i, b * P:(b + 1) * P], ones,
                                                diag[:, i, b * P:(b + 1) * P], start=i == 0 and b == 0, stop=True,
                                                skip_group_check=True)
                reach(last, ("item", m))
                fill(l, "rsqrt")

                def items_of(name, tiles_, offsets, acts):
                    n, m = at[name]["units"], at[name]["items"]
                    unit_split(n)
                    for i in range(tiles_):
                        if i % 2 == 0:
                            take_bank(m + i // 2)
                        last = column_tile(m + i // 2, i % 2, n, offsets(i), acts)
                        if i % 2 or i == tiles_ - 1:
                            reach(last, ("item", m + i // 2), *([("unit", n)] if i == tiles_ - 1 else []))

                c_q = [cq[:, k] for k in range(2)]
                pe.wait_ge(cq_ready, 2 * l + 1)
                items_of("uqC", 3, lambda i: [k * 6 * QK_ROPE + i * P for k in range(2)], c_q)
                items_of("uqA", 4, lambda i: [(4 * k + i) * P for k in range(2)], c_q)
                pe.wait_ge(bank_free, at["uqC"]["items"] + 2)
                m = at["rot"]["items"]
                for i in range(2):
                    take_bank(m + i)
                    for t in range(2):
                        last = nc.tensor.matmul(bank(m + i)[:, t * S:(t + 1) * S], rot, ropeX[:, 2 * i + t, :],
                                                start=t == 0, stop=True, skip_group_check=True)
                    reach(last, ("item", m + i))
                m = at["pool"]["items"]
                take_bank(m)
                pe.wait_ge(pooled, l + 1)
                pe.wait_ge(small_landed, 16 * SMALL)
                for t in range(2):
                    last = nc.tensor.matmul(bank(m)[:, t * S:(t + 1) * S], pw[:, l, t, :], poolB[:, t, :],
                                            start=t == 0, stop=True, skip_group_check=True)
                reach(last, ("item", m))
                items_of("uqB", 2, lambda i: [(2 * k + i) * P for k in range(2)], c_q)
                pe.wait_ge(cq_ready, 2 * l + 2)
                items_of("kn", 6, lambda i: [i * P], [cq[:, 2]])
                n, m = at["v"]["units"], at["v"]["items"]
                unit_split(n)
                for i in range(4):
                    take_bank(m + i)
                    rows = slice((i // 2) * P, (i // 2 + 1) * P)
                    cols = slice((i % 2) * 384, (i % 2 + 1) * 384)
                    last = split_product(bank(m + i)[:, 0:384], (cq[:, 2, 0, rows], cq[:, 2, 1, rows]),
                                         (slot_hi[slot[n]][:, cols], slot_lo[slot[n]][:, cols]), True, True)
                    reach(last, ("item", m + i), *([("unit", n)] if i == 3 else []))
                fill(l, "v")

                pe.wait_ge(rope_ready, l + 1)
                for step, i in MLA_ORDER:
                    if step == "score":
                        mla_score(l, i)
                    elif step == "pt":
                        mla_turn(l, i)
                    elif step == "pv":
                        mla_values(l, i)
                    elif step == "fill":
                        fill(l, i)
                n = plan["wout", l]["units"]
                pe.wait_ge(bank_free, at["pool"]["items"] + 1)

                def wait_values(r):
                    if r >= 2 and r % 2 == 0:
                        pe.wait_ge(bank_free, plan["pv", l, (r - 2) // 2]["items"] + 1)
                for r in range(KT - ROWS_TAIL):
                    wait_values(r)
                    row_unit(n + r, mixT[:, r], r == 0)
                tail = range(KT - ROWS_TAIL, KT)
                row_tail(4 * l + 1, [n + r for r in tail], [mixT[:, r] for r in tail], lambda i: wait_values(tail[i]))

            def mla_score(l, pr):
                pe.wait_ge(bank_free, plan["kn", l]["items"] + pr + 1)
                if pr == 2:
                    pe.wait_ge(exp_done, 5 * l + 1)
                s1, s0 = mla_scores(pr)
                for e in range(2):
                    parts = ((qT[:, 2 * pr + e], knT[:, 2 * pr + e]), (qT[:, 6 + pr], krT[:, e]))
                    for i, (q, k) in enumerate(parts):
                        split_product(s1[:, e, :], (q[:, 0, P:S], q[:, 1, P:S]), (k[:, 0, :], k[:, 1, :]),
                                      i == 0 and e == 0, i == 1)
                    for i, (q, k) in enumerate(parts):
                        last = split_product(s0[:, e, :], (q[:, 0, 0:P], q[:, 1, 0:P]), (k[:, 0, 0:P], k[:, 1, 0:P]),
                                             i == 0 and e == 0, i == 1)
                reach(last, ("score", l, pr))

            def mla_turn(l, pr):
                s1, s0 = mla_probs(pr)
                m = plan["pt", l, pr]["items"]
                pe.wait_ge(probs_ready, 5 * l + pr + 1)
                for e in range(2):
                    take_bank(m + e)
                    nc.tensor.transpose(bank(m + e)[:, 0:P], s0[:, e, :], ident)
                    nc.tensor.transpose(bank(m + e)[:, P:2 * P], s1[:, e, 0:P], ident)
                    last = nc.tensor.transpose(bank(m + e)[:, 2 * P:3 * P], s1[:, e, P:2 * P], ident)
                    reach(last, ("item", m + e))

            def mla_values(l, pr):
                pT = turned_probs[pr]
                m = plan["pv", l, pr]["items"]
                take_bank(m)
                for e in range(2):
                    pe.wait_ge(bank_free, plan["pt", l, pr]["items"] + e + 1)
                    cols = slice((2 * pr + e) * P, (2 * pr + e + 1) * P)
                    dst = two(bank(m))[:, e, :]
                    split_product(dst, (v[:, 0, 0, cols], v[:, 0, 1, cols]), (pT[:, e, 0, 0:S], pT[:, e, 1, 0:S]),
                                  e == 0, False)
                    last = split_product(dst[:, P:S], (v[:, 1, 0, cols], v[:, 1, 1, cols]),
                                         (pT[:, e, 0, S:S + P], pT[:, e, 1, S:S + P]), False, True)
                reach(last, ("item", m))

            def memory(l):
                u, m = plan["wq", l]["units"], plan["wq", l]["items"]
                for t in range(KT // 2):
                    column_pair(m + t, u + 2 * t, xT, arrival=None if t else 5 + 2 * (4 * l + 1))
                pe.wait_ge(bank_free, m + KT // 2)
                for step, i in MEM_ORDER:
                    if step == "score":
                        for hh in range(MEM_HEADS):
                            for t in range(2):
                                q, k = qT[:, 2 * hh + t, :, i * P:(i + 1) * P], memK[:, 2 * hh + t]
                                last = split_product(mem_scores(i)[:, hh, :], (q[:, 0, :], q[:, 1, :]),
                                                     (k[:, 0, :], k[:, 1, :]), t == 0 and hh % 2 == 0, t == 1)
                        reach(last, ("mscore", l, i))
                    elif step == "fill":
                        fill(l, i)
                    elif step == "pt":
                        if i == 0:
                            pe.wait_ge(probs_ready, 5 * l + PAIRS + 2)
                        m = plan["mpt", l, i]["items"]
                        take_bank(m)
                        for kt in range(2):
                            for b in range(TB):
                                last = nc.tensor.transpose(bank(m)[:, kt * S + b * P:kt * S + (b + 1) * P],
                                                           mem_probs(b)[:, i, kt * P:(kt + 1) * P], ident)
                        reach(last, ("item", m))
                    elif step == "pv":
                        m = plan["mpv", l, i]["items"]
                        take_bank(m)
                        pe.wait_ge(bank_free, plan["mpt", l, i]["items"] + 1)
                        if i == 0:
                            pe.wait_ge(bank_free, values_split(l))
                        for c in range(2):
                            t = 2 * i + c
                            for kt in range(2):
                                p, cols = mpT[:, 2 * i + kt], slice(t * P, (t + 1) * P)
                                last = split_product(two(bank(m))[:, c, :],
                                                     (memV[:, kt, 0, cols], memV[:, kt, 1, cols]),
                                                     (p[:, 0, :], p[:, 1, :]), c == 0 and kt == 0, kt == 1)
                        reach(last, ("item", m))
                n = plan["wo", l]["units"]

                def wait_values(r):
                    if r % 2 == 0:
                        pe.wait_ge(bank_free, plan["mpv", l, r // 2]["items"] + 1)
                for r in range(KT - ROWS_TAIL):
                    wait_values(r)
                    row_unit(n + r, mixT[:, r], r == 0)
                tail = range(KT - ROWS_TAIL, KT)
                row_tail(4 * l + 2, [n + r for r in tail], [mixT[:, r] for r in tail], lambda i: wait_values(tail[i]))

            def values_split(l):
                return max(plan["kv", l, i]["items"] + 2 for i in (4, 5))

            pe.wait_ge(ident_landed, 16)
            for b in range(TB):
                pe.wait_ge(x_landed, 16 * TB if b else 16 * TB)
                turn(b, x[:, b, :], b)
            pe.wait_ge(consts_landed, 16)
            for l in range(L):
                ffn(l, 0)
                norm(4 * l, l, "ln0")
                mix(l)
                norm(4 * l + 1, l, "ln1")
                memory(l)
                norm(4 * l + 2, l, "ln2")
                ffn(l, 1)
                if l < L - 1:
                    norm(4 * l + 3, l, "ln3")
            assert milestones[0] == len(plan.units_by)

        def look_ahead(split):
            state = dict(next=0)

            def ahead_to(limit):
                while state["next"] < min(UNITS, limit):
                    split(state["next"])
                    state["next"] += 1

            def ahead(tag, more=0):
                limit = state["next"]
                while (limit < UNITS and last_user[limit] <= plan.units_by[done[tag] - 1] - 2 + more
                       and free_after[limit] <= done[tag]):
                    limit += 1
                ahead_to(limit)
            return state, ahead, ahead_to

        def loop_first(l, w):
            first = plan["ffn", l, w]["units"] + 2 + SLOTS
            for n in range(first, first + LOOP_UNITS * (LOOPS - 1)):
                assert slot[n + LOOP_UNITS] == slot[n] and free_after[n + LOOP_UNITS] == free_after[n] + LOOP_UNITS
            return first

        @block.scalar
        def _(act):
            def split_hi(n, it=None):
                act.wait_ge(raw_landed[n % RAW], plus(landed(n), it, 16 * LOOP_UNITS // RAW))
                if free_after[n]:
                    act.wait_ge(pe_done, plus(free_after[n], it, LOOP_UNITS))
                size = source[n][0]
                nc.scalar.copy(slot_hi[slot[n]][:, 0:size], raw[:, n % RAW, 0:size]).then_inc(hi_done, 1)

            state, ahead, ahead_to = look_ahead(split_hi)

            def round_item(m, dst, src, scale=None):
                ahead(("item", m))
                act.wait_ge(pe_done, done["item", m])
                if scale is None:
                    nc.scalar.copy(dst, src).then_inc(item_hi, 1)
                    return
                for t in range(2):
                    last = nc.scalar.mul(dst[:, t, :], src[:, t, :], scale[:, t:t + 1])
                last.then_inc(item_hi, 1)

            def round_tiles(name, dst):
                m = plan[name]["items"]
                for i in range(dst.shape[1] // 2):
                    round_item(m + i, dst[:, 2 * i:2 * i + 2, 0, :], two(bank(m + i)))

            def fill(l, place):
                for l, i in FILL[l, place]:
                    if i < 4:
                        round_tiles(("kv", l, i), memK[:, 2 * i:2 * i + 2])
                        continue
                    m = plan["kv", l, i]["items"]
                    for t in range(2):
                        c = (2 * (i - 4) + t) * S
                        round_item(m + t, memV[:, :, 0, c:c + S], two(bank(m + t)))

            def turn(job, dst, b):
                for c in range(HALVES):
                    act.wait_ge(pe_done, done["turned", job, c])
                    nc.scalar.copy(half_T(dst, 0, b, c), turned_half(b, c)).then_inc(turned_hi, 1)

            def ffn(l, w):
                m, f = plan["ffn", l, w]["items"], (2 * l + w) * FT

                def gate(j, it=None):
                    act.wait_ge(pe_done, plus(done["item", m + j], it, LOOP_UNITS))
                    if f + j >= 2:
                        act.wait_ge(hidden_ready, plus(f + j - 1, it, STEPS))
                    nc.scalar.activation(ev[:, j % 2, :], bank(m + j)[:, 0:S], ACT.Silu).then_inc(silu_done, 1)

                for j in range(2):
                    ahead(("item", m + j), -j)
                    gate(j)
                    if j == 0 and l == 0 and w == 0:
                        for b in range(TB):
                            turn(2 + b, memT, b)
                if l == 0 and w == 0:
                    act.wait_ge(angles_ready, 2)
                    nc.scalar.activation(cosT[:, :], gb[:, 0, 0:S], ACT.Sin)
                    nc.scalar.activation(sinT[:, :], gb[:, 0, S:2 * S], ACT.Sin).then_inc(tables_done, 1)
                first = loop_first(l, w)
                assert state["next"] == first, (state["next"], first)
                with act.Fori(0, LOOPS) as it:
                    for s in range(STEPS):
                        for n in range(first + 3 * s, first + 3 * s + 3):
                            split_hi(n, it)
                        gate(s + 2, it)
                state["next"] = first + LOOP_UNITS * LOOPS
                for j in range(FT - 4, FT):
                    ahead(("item", m + j))
                    gate(j)

            def norm(e, l, place):
                ahead(("y", e, 0), 1)
                fill(l, place)
                ahead_to(first_of_stage(e) + 2)
                for b in range(TB):
                    turn(4 + 2 * e + b, xT, b)

            def exponentials(j, views):
                act.wait_ge(max_ready, j + 1)
                for i, (dst, src, scale) in enumerate(views):
                    last = nc.scalar.activation(dst, src, ACT.Exp, bias=NEGM[j % 3][:, i:i + 1], scale=scale,
                                                accum_out=SUM[j % 3][:, i:i + 1])
                last.then_inc(exp_done, 1)

            def mix(l):
                round_c_q_and_c_kv(l)
                fill(l, "rsqrt")
                round_tiles(("uqA", l), qT[:, 0:4])
                m = plan["pool", l]["items"]
                round_item(m, mixT[:, 0:2, 0, :], two(bank(m)), pscale[:, l, :])
                round_tiles(("uqB", l), qT[:, 4:6])
                act.wait_ge(rope_sum, l + 1)
                nc.scalar.copy(qT[:, 6:9, 0, :], ropeZ[:, 1:4, :])
                for e in range(2):
                    rows = slice(e * 64, e * 64 + 64)
                    last = nc.scalar.copy(krT[rows, e, 0, :], ropeZ[rows, 0, :])
                last.then_inc(rope_hi, 1)
                round_tiles(("kn", l), knT)
                m = plan["v", l]["items"]
                for i in range(4):
                    round_item(m + i, v[:, i // 2, 0, (i % 2) * 384:(i % 2 + 1) * 384], bank(m + i)[:, 0:384])
                fill(l, "v")
                for step, pr in MLA_ORDER:
                    if step == "score":
                        (s1, s0), (p1, p0) = mla_scores(pr), mla_probs(pr)
                        ahead(("score", l, pr))
                        exponentials(5 * l + pr, [(p[:, e, :], s[:, e, :], MLA_SCALE)
                                                  for p, s in ((p1, s1), (p0, s0)) for e in range(2)])
                    elif step == "pt":
                        m = plan["pt", l, pr]["items"]
                        for e in range(2):
                            round_item(m + e, turned_probs[pr][:, e, 0, :], bank(m + e)[:, 0:384])
                    elif step == "pv":
                        round_tiles(("pv", l, pr), mixT[:, 2 + 2 * pr:4 + 2 * pr])
                    elif step == "fill":
                        fill(l, pr)

            def round_c_q_and_c_kv(l):
                ahead(("item", plan["sums", l]["items"]))
                fill(l, "sums")
                ahead(("item", plan["rsqrt", l]["items"]))
                act.wait_ge(cq_scaled, l + 1)
                nc.scalar.copy(cq[:, 0:2, 0, :], cqf[:, 0:2, :]).then_inc(cq_hi, 1)
                act.wait_ge(bank_free, plan["rsqrt", l]["items"] + 1)
                nc.scalar.copy(cq[:, 2, 0, :], cqf[:, 2, :]).then_inc(cq_hi, 1)

            def memory(l):
                round_tiles(("wq", l), qT[:, 0:8])
                for step, i in MEM_ORDER:
                    if step == "score":
                        ahead(("mscore", l, i))
                        exponentials(5 * l + PAIRS + i, [(mem_probs(i)[:, hh, :], mem_scores(i)[:, hh, :], MEM_SCALE)
                                                         for hh in range(MEM_HEADS)])
                    elif step == "pt":
                        round_tiles(("mpt", l, i), mpT[:, 2 * i:2 * i + 2])
                    elif step == "pv":
                        round_tiles(("mpv", l, i), mixT[:, 2 * i:2 * i + 2])
                    elif step == "fill":
                        fill(l, i)

            for b in range(TB):
                turn(b, xT, b)
            for l in range(L):
                ffn(l, 0)
                norm(4 * l, l, "ln0")
                if l == 0:
                    act.wait_ge(small_landed, 16 * SMALL)
                mix(l)
                norm(4 * l + 1, l, "ln1")
                memory(l)
                norm(4 * l + 2, l, "ln2")
                ffn(l, 1)
                if l < L - 1:
                    norm(4 * l + 3, l, "ln3")

        @block.vector
        def _(dve):
            steps, rounded = [0], [0]

            def own(ins):
                steps[0] += 1
                ins.then_inc(dve_step, 1)

            def settle(it=None):
                dve.wait_ge(dve_step, plus(steps[0], it, STEPS))

            def split_lo(n, it=None):
                dve.wait_ge(hi_done, plus(n + 1, it, LOOP_UNITS))
                s = slice(0, source[n][0])
                nc.vector.tensor_tensor(slot_lo[slot[n]][:, s], raw[:, n % RAW, s],
                                        slot_hi[slot[n]][:, s].bitcast(F32), ALU.subtract).then_inc(lo_done, 1)

            state, ahead, ahead_to = look_ahead(split_lo)

            def split_item(m, dst, src, hi, scale=None):
                ahead(("item", m))
                rounded[0] += 1
                dve.wait_ge(item_hi, rounded[0])
                if scale is None:
                    nc.vector.tensor_tensor(dst, src, hi.bitcast(F32), ALU.subtract).then_inc(bank_free, 1)
                    return
                for t in range(2):
                    last = nc.vector.scalar_tensor_tensor(out=dst[:, t, :], in0=src[:, t, :], scalar=scale[:, t:t + 1],
                                                          in1=hi[:, t, :].bitcast(F32), op0=ALU.mult,
                                                          op1=ALU.subtract)
                last.then_inc(bank_free, 1)

            def split_tiles(name, dst):
                m = plan[name]["items"]
                for i in range(dst.shape[1] // 2):
                    pair = dst[:, 2 * i:2 * i + 2]
                    split_item(m + i, pair[:, :, 1, :], two(bank(m + i)), pair[:, :, 0, :])

            def fill(l, place):
                for l, i in FILL[l, place]:
                    if i < 4:
                        split_tiles(("kv", l, i), memK[:, 2 * i:2 * i + 2])
                        continue
                    m = plan["kv", l, i]["items"]
                    for t in range(2):
                        c = (2 * (i - 4) + t) * S
                        split_item(m + t, memV[:, :, 1, c:c + S], two(bank(m + t)), memV[:, :, 0, c:c + S])

            def turn(job, dst, b):
                for c in range(HALVES):
                    dve.wait_ge(turned_hi, turned_value(job, c))
                    nc.vector.tensor_tensor(half_T(dst, 1, b, c), turned_half(b, c),
                                            half_T(dst, 0, b, c).bitcast(F32), ALU.subtract).then_inc(turned_lo, 1)

            def ffn(l, w):
                m, f = plan["ffn", l, w]["items"], (2 * l + w) * FT

                def hidden(j, it=None):
                    h, hid = ev[:, j % 2, :], aT[:, j % 4]
                    dve.wait_ge(silu_done, plus(f + j + 1, it, STEPS))
                    nc.vector.tensor_tensor(h, bank(m + j)[:, S:2 * S], h, ALU.mult).then_inc(bank_free, 1)
                    dve.wait_ge(bank_free, plus(m + j + 1, it, STEPS))
                    own(nc.vector.tensor_copy(hid[:, 0, :], h))
                    settle(it)
                    nc.vector.tensor_tensor(hid[:, 1, :], h, hid[:, 0, :].bitcast(F32), ALU.subtract)\
                        .then_inc(hidden_ready, 1)

                for j in range(2):
                    ahead(("item", m + j), -j)
                    hidden(j)
                    if j == 0 and l == 0 and w == 0:
                        for b in range(TB):
                            turn(2 + b, memT, b)
                first = loop_first(l, w)
                assert state["next"] == first
                with dve.Fori(0, LOOPS) as it:
                    for s in range(STEPS):
                        for n in range(first + 3 * s, first + 3 * s + 3):
                            split_lo(n, it)
                        hidden(s + 2, it)
                state["next"] = first + LOOP_UNITS * LOOPS
                steps[0] += STEPS * (LOOPS - 1)
                for j in range(FT - 4, FT):
                    ahead(("item", m + j))
                    hidden(j)

            def norm(e, l=None, place=None):
                weight = 0.5 if e % 4 in (0, 3) else 1.0

                def statistics(b):
                    dve.wait_ge(x_scaled, 2 * e + b + 1)
                    dve.wait_ge(pe_done, done["y", e, b])
                    z = x[:, b, :].rearrange("p (c s) -> p c s", c=2)
                    own(nc.vector.scalar_tensor_tensor(out=z, in0=ps[:, 4 + 2 * b:6 + 2 * b, :], scalar=weight,
                                                       in1=z, op0=ALU.mult, op1=ALU.add))
                    settle()
                    for c in range(2):
                        own(nc.vector.bn_stats(STATS[b][:, 6 * c:6 * c + 6], z[:, c, :]))
                    settle()
                    own(nc.vector.bn_aggr(MEANVAR[b], STATS[b]))
                    settle()
                    nc.vector.tensor_scalar(VEPS[b], MEANVAR[b][:, 1:2], LN_EPS, None, ALU.add)\
                        .then_inc(var_ready, 1)

                def apply(b):
                    dve.wait_ge(gains_landed, 32 * (e + 1))
                    own(nc.vector.scalar_tensor_tensor(out=x[:, b, :], in0=x[:, b, :], scalar=MEANVAR[b][:, 0:1],
                                                       in1=gb[:, 0, :], op0=ALU.subtract, op1=ALU.mult))
                    settle()
                    dve.wait_ge(rstd_ready, 2 * e + b + 1)
                    for c in range(HALVES):
                        cols = slice(c * D // 2, (c + 1) * D // 2)
                        nc.vector.scalar_tensor_tensor(out=x[:, b, cols], in0=x[:, b, cols], scalar=RSTD[b],
                                                       in1=gb[:, 1, cols], op0=ALU.mult, op1=ALU.add)\
                            .then_inc(norm_done, 1)

                ahead(("y", e, 0), 1)
                statistics(0)
                apply(0)
                statistics(1)
                if place is None:
                    apply(1)
                    return
                fill(l, place)
                ahead_to(first_of_stage(e) + 2)
                turn(4 + 2 * e, xT, 0)
                apply(1)
                turn(5 + 2 * e, xT, 1)

            def maxima(j, scores, masked, scale):
                for s in masked:
                    own(nc.vector.memset(s, NEG_INF))
                settle()
                for i, s in enumerate(scores):
                    n = s.shape[1]
                    own(nc.vector.tensor_reduce(MX[j % 3][:, 2 * i:2 * i + n], s, AX.X, ALU.max))
                settle()
                nc.vector.tensor_scalar(NEGM[j % 3], MX[j % 3], scale, -1.0, ALU.mult, ALU.mult).then_inc(max_ready, 1)

            def scale_probs(j, probs):
                dve.wait_ge(exp_done, j + 1)
                own(nc.vector.reciprocal(REC[j % 3], SUM[j % 3]))
                settle()
                for i, p in enumerate(probs):
                    last = nc.vector.tensor_scalar(p, p, REC[j % 3][:, i:i + 1], None, ALU.mult)
                last.then_inc(probs_ready, 1)

            def mix(l):
                m = plan["win", l]["items"]
                ahead(("item", m))
                dve.wait_ge(pe_done, done["item", m])
                nc.vector.tensor_copy(cqf[:, 0:2, :], two(bank(m))).then_inc(bank_free, 1)
                dve.wait_ge(bank_free, m + 1)
                own(nc.vector.tensor_tensor(sq_q, cqf[:, 0:2, :], cqf[:, 0:2, :], ALU.mult))
                ahead(("item", m + 1))
                dve.wait_ge(pe_done, done["item", m + 1])
                nc.vector.tensor_copy(kv_pe, two(bank(m + 1))).then_inc(bank_free, 1)
                dve.wait_ge(bank_free, m + 2)
                nc.vector.tensor_tensor(sq_kv, cqf[:, 2, :], cqf[:, 2, :], ALU.mult).then_inc(squares_ready, 1)
                ahead(("item", m + 2))
                dve.wait_ge(pe_done, done["item", m + 2])
                nc.vector.tensor_copy(poolU, two(bank(m + 2))).then_inc(bank_free, 1)
                m = plan["sums", l]["items"]
                dve.wait_ge(pe_done, done["item", m])
                own(nc.vector.tensor_scalar(MS[:, 0:2], bank(m)[:, 0:2], 1.0 / Q_LORA, RMS_EPS, ALU.mult, ALU.add))
                nc.vector.tensor_scalar(MS[:, 2:4], bank(m)[:, 2:4], 1.0 / KV_LORA, RMS_EPS, ALU.mult, ALU.add)\
                    .then_inc(bank_free, 1)
                dve.wait_ge(rms_ready, l + 1)
                for i in range(2):
                    for b in range(TB):
                        last = nc.vector.tensor_scalar(diag[:, i, b * P:(b + 1) * P], ident,
                                                       RMS[:, 2 * i + b:2 * i + b + 1], None, ALU.mult)
                last.then_inc(diag_ready, 1)
                for e in range(2):
                    own(nc.vector.memset(krT[(1 - e) * 64:(2 - e) * 64, e].bitcast(F32), 0.0))
                ahead(("item", m))
                fill(l, "sums")
                m = plan["rsqrt", l]["items"]
                ahead(("item", m))
                dve.wait_ge(pe_done, done["item", m])
                for k in range(3):
                    ins = nc.vector.scalar_tensor_tensor(out=cqf[:, k, :], in0=cqf[:, k, :],
                                                         scalar=gains[:, l, k:k + 1], in1=two(bank(m))[:, k // 2, :],
                                                         op0=ALU.mult, op1=ALU.mult)
                    if k:
                        ins.then_inc((cq_scaled, bank_free)[k - 1], 1)
                for i, t in enumerate((slice(0, 2), slice(2, 3))):
                    dve.wait_ge(cq_hi, 2 * l + i + 1)
                    nc.vector.tensor_tensor(cq[:, t, 1, :], cqf[:, t, :], cq[:, t, 0, :].bitcast(F32), ALU.subtract)\
                        .then_inc(cq_ready, 1)
                fill(l, "rsqrt")
                m = plan["uqC", l]["items"]
                ahead(("item", m))
                dve.wait_ge(pe_done, done["item", m])
                nc.vector.tensor_copy(ropeX[:, 1:3, :], two(bank(m))).then_inc(bank_free, 1)
                dve.wait_ge(pe_done, done["item", m + 1])
                nc.vector.tensor_copy(ropeX[:, 3, :], bank(m + 1)[:, 0:S]).then_inc(bank_free, 1)
                split_tiles(("uqA", l), qT[:, 0:4])
                m = plan["rot", l]["items"]
                for i in range(2):
                    z = ropeZ[:, 2 * i:2 * i + 2, :]
                    dve.wait_ge(pe_done, done["item", m + i])
                    nc.vector.tensor_tensor(z, two(bank(m + i)),
                                            sinT[:, :].unsqueeze(1).broadcast_to([P, 2, S]), ALU.mult)\
                        .then_inc(bank_free, 1)
                own(nc.vector.tensor_tensor(ropeX, ropeX, cosT[:, :].unsqueeze(1).broadcast_to([P, 4, S]), ALU.mult))
                dve.wait_ge(bank_free, m + 2)
                settle()
                nc.vector.tensor_tensor(ropeZ, ropeZ, ropeX, ALU.add).then_inc(rope_sum, 1)
                dve.wait_ge(rope_sum, l + 1)
                m = plan["pool", l]["items"]
                split_item(m, mixT[:, 0:2, 1, :], two(bank(m)), mixT[:, 0:2, 0, :], pscale[:, l, :])
                split_tiles(("uqB", l), qT[:, 4:6])
                dve.wait_ge(rope_hi, l + 1)
                own(nc.vector.tensor_tensor(qT[:, 6:9, 1, :], ropeZ[:, 1:4, :], qT[:, 6:9, 0, :].bitcast(F32),
                                            ALU.subtract))
                for e in range(2):
                    rows = slice(e * 64, e * 64 + 64)
                    last = nc.vector.tensor_tensor(krT[rows, e, 1, :], ropeZ[rows, 0, :],
                                                   krT[rows, e, 0, :].bitcast(F32), ALU.subtract)
                last.then_inc(rope_ready, 1)
                split_tiles(("kn", l), knT)
                m = plan["v", l]["items"]
                for i in range(4):
                    hi, lo = (v[:, i // 2, c, (i % 2) * 384:(i % 2 + 1) * 384] for c in range(2))
                    split_item(m + i, lo, bank(m + i)[:, 0:384], hi)
                fill(l, "v")

                for step, pr in MLA_ORDER:
                    if step == "score":
                        s1, s0 = mla_scores(pr)
                        ahead(("score", l, pr))
                        dve.wait_ge(pe_done, done["score", l, pr])
                        maxima(5 * l + pr, [s1, s0], [s1[0:CHUNK, :, P + CHUNK:2 * P], s0[0:CHUNK, :, CHUNK:P]],
                               MLA_SCALE)
                    elif step == "scale":
                        p1, p0 = mla_probs(pr)
                        scale_probs(5 * l + pr, [p1[:, 0, :], p1[:, 1, :], p0[:, 0, :], p0[:, 1, :]])
                    elif step == "pt":
                        m, pT = plan["pt", l, pr]["items"], turned_probs[pr]
                        for e in range(2):
                            split_item(m + e, pT[:, e, 1, :], bank(m + e)[:, 0:384], pT[:, e, 0, :])
                    elif step == "pv":
                        split_tiles(("pv", l, pr), mixT[:, 2 + 2 * pr:4 + 2 * pr])
                    elif step == "fill":
                        fill(l, pr)

            def memory(l):
                split_tiles(("wq", l), qT[:, 0:8])
                for step, i in MEM_ORDER:
                    if step == "score":
                        ahead(("mscore", l, i))
                        dve.wait_ge(pe_done, done["mscore", l, i])
                        maxima(5 * l + PAIRS + i, [mem_scores(i)], [], MEM_SCALE)
                    elif step == "scale":
                        scale_probs(5 * l + PAIRS + i, [mem_probs(i)[:, hh, :] for hh in range(MEM_HEADS)])
                    elif step == "pt":
                        split_tiles(("mpt", l, i), mpT[:, 2 * i:2 * i + 2])
                    elif step == "pv":
                        split_tiles(("mpv", l, i), mixT[:, 2 * i:2 * i + 2])
                    elif step == "fill":
                        fill(l, i)

            for b in range(TB):
                turn(b, xT, b)
            for l in range(L):
                ffn(l, 0)
                norm(4 * l, l, "ln0")
                if l == 0:
                    dve.wait_ge(small_landed, 16 * SMALL)
                mix(l)
                norm(4 * l + 1, l, "ln1")
                memory(l)
                norm(4 * l + 2, l, "ln2")
                ffn(l, 1)
                norm(4 * l + 3, l, "ln3") if l < L - 1 else norm(4 * l + 3)

        @block.gpsimd
        def _(pool):
            steps = [0]

            def own(ins):
                steps[0] += 1
                ins.then_inc(pool_step, 1)
                pool.wait_ge(pool_step, steps[0])

            def load_gains(e):
                for i, w in enumerate(("ln_g", "ln_b")):
                    pool.dma_start(gb[:, i, :], a[w][e // 4, e % 4:e % 4 + 1, :].partition_broadcast(P))\
                        .then_inc(gains_landed, 16)

            def scale_x(job, e):
                for b in range(TB):
                    pool.wait_ge(pe_done, done["turned", job + b, 1])
                    nc.gpsimd.tensor_scalar(x[:, b, :], x[:, b, :], ALPHA, 1.0, ALU.mult, ALU.mult)\
                        .then_inc(x_scaled, 1)

            def norm(e):
                for b in range(TB):
                    pool.wait_ge(var_ready, 2 * e + b + 1)
                    nc.gpsimd.tensor_tensor(RSTD[b], VEPS[b], cst[:, C_HALF:C_HALF + 1], ALU.pow)\
                        .then_inc(rstd_ready, 1)
                if e < 4 * L - 1:
                    if e % 4:
                        pool.wait_ge(norm_done, normed(e, 1, 1))
                        load_gains(e + 1)
                    scale_x(4 + 2 * e, e)

            def rope_angles():
                pool.wait_ge(consts_landed, 16)
                pool.wait_ge(pos_landed, 16)
                ang, turns, part_of = gb[:, 0, 2 * S:3 * S], gb[:, 0, 3 * S:4 * S], gb[:, 1, S:2 * S]
                own(nc.gpsimd.tensor_copy(ang, gb[:, 1, 0:S].bitcast(I32)))
                own(nc.gpsimd.tensor_scalar(ang, ang, cst[:, C_FREQ:C_FREQ + 1], None, ALU.mult))
                for i, quarter in enumerate((0.25, 0.0)):
                    r = gb[:, 0, i * S:(i + 1) * S]
                    own(nc.gpsimd.tensor_scalar(turns, ang, 1.0 / (2.0 * math.pi), quarter, ALU.mult, ALU.add))
                    own(nc.gpsimd.tensor_scalar(turns, turns, ROUND, None, ALU.add))
                    own(nc.gpsimd.tensor_scalar(turns, turns, ROUND, None, ALU.subtract))
                    for k, part in enumerate(TURN):
                        own(nc.gpsimd.tensor_scalar(part_of, turns, part, None, ALU.mult))
                        own(nc.gpsimd.tensor_tensor(r, ang if k == 0 else r, part_of, ALU.subtract))
                    own(nc.gpsimd.tensor_scalar(r, r, quarter * 2.0 * math.pi, PI_IN, ALU.add, ALU.min))
                    nc.gpsimd.tensor_scalar(r, r, -PI_IN, None, ALU.max).then_inc(angles_ready, 1)

            def pool_group(l):
                pool.wait_ge(bank_free, plan["win", l]["items"] + 3)
                src = poolU
                for i, shift in enumerate((1, 2, 4, 8)):
                    dst = (poolA, poolB)[i % 2]
                    own(nc.gpsimd.tensor_tensor(dst[:, :, shift:S], src[:, :, shift:S], src[:, :, 0:S - shift],
                                                ALU.add))
                    own(nc.gpsimd.tensor_copy(dst[:, :, 0:shift], src[:, :, 0:shift]))
                    keep = ((0, 0), (64, 0), (0, 1), (64, 1))[i]
                    rows = slice(keep[0], keep[0] + 64)
                    own(nc.gpsimd.tensor_copy(poolM[rows, keep[1], :], dst[rows, keep[1], :]))
                    src = dst
                own(nc.gpsimd.tensor_tensor(poolM[:, :, :], poolM[:, :, :], inv_count, ALU.mult))
                nc.gpsimd.tensor_tensor(poolB, poolM[:, :, :], poolU, ALU.subtract).then_inc(pooled, 1)

            pool.dma_start(gb[:, 1, 0:S].bitcast(I32), a["positions"].partition_broadcast(P)).then_inc(pos_landed, 16)
            pool.dma_start(cst[:, P:C_ALL], consts[:, P:C_ALL]).then_inc(consts_landed, 16)
            pool.dma_start(tmp[:, :].rearrange("p (b d) -> p b d", b=TB),
                           a["mem"][0].rearrange("(b p) d -> p b d", p=P)).then_inc(mem_landed, 16)
            own(nc.gpsimd.memset(pw[:, :, :, :], 0.0))
            scale_x(0, -1)
            rope_angles()
            for l in range(L):
                for g in range(len(POOL_WINDOWS)):
                    rows = slice((g % 2) * 64, (g % 2 + 1) * 64)
                    pool.dma_start(pw[rows, l, g // 2, rows], a["pool_w"][l, g]).then_inc(small_landed, 16)
                for dst, w, t in ((gains[:, l, 0:1], "q_norm_g", 0), (gains[:, l, 1:2], "q_norm_g", 1),
                                  (gains[:, l, 2:3], "kv_norm_g", 0), (pscale[:, l, 0:1], "pool_scale", 0),
                                  (pscale[:, l, 1:2], "pool_scale", 1)):
                    pool.dma_start(dst, a[w][l, t * P:(t + 1) * P].rearrange("(p o) -> p o", o=1))\
                        .then_inc(small_landed, 16)
            pool.wait_ge(tables_done, 1)
            load_gains(0)
            for l in range(L):
                norm(4 * l)
                pool.wait_ge(bank_free, plan["sums", l]["items"] + 1)
                nc.gpsimd.tensor_tensor(RMS, MS, cst[:, C_HALF:C_HALF + 1].broadcast_to([P, 4]), ALU.pow)\
                    .then_inc(rms_ready, 1)
                pool_group(l)
                pool.wait_ge(bank_free, plan["pool", l]["items"] + 1)
                load_gains(4 * l + 1)
                for s in range(1, 4):
                    norm(4 * l + s)


_INS = ["x", "mem", "positions", "ln_g", "ln_b", "ffn1_w13", "ffn1_w2", "w_in", "pool_w", "pool_scale",
        "q_norm_g", "w_uq", "kv_norm_g", "w_ukv", "w_out", "mem_wq", "mem_wkv", "mem_wo", "ffn2_w13", "ffn2_w2"]


def kernel(**inputs):
    import concourse.bacc as bacc
    from concourse.bass_utils import run_bass_kernel_spmd

    nc = bacc.Bacc("TRN2", target_bir_lowering=False, num_devices=1)
    arrays = {f"in_{n}": np.ascontiguousarray(inputs[n]) for n in _INS}
    arrays["in_constants"] = constants(inputs["x"].shape[1])
    aps = {n: nc.dram_tensor(n, v.shape, mybir.dt.from_np(v.dtype), kind="ExternalInput").ap()
           for n, v in arrays.items()}
    out = nc.dram_tensor("out_0", inputs["x"].shape, F32, kind="ExternalOutput").ap()
    trunk(nc, {n: aps[f"in_{n}"] for n in _INS}, aps["in_constants"], out)
    r = run_bass_kernel_spmd(nc, [arrays], core_ids=[0])
    return r.results[0]["out_0"]
```

```python
import math
from contextlib import ExitStack

import numpy as np
import concourse.bass as bass
from concourse import mybir

F32 = mybir.dt.float32
F32R = mybir.dt.float32r
I32 = mybir.dt.int32
ALU = mybir.AluOpType
ACT = mybir.ActivationFunctionType
AX = mybir.AxisListType

P = 128
POOL_WINDOWS = (2, 4, 8, 16)
CHUNK = 64
MEM_HEADS = 4
QK_NOPE, QK_ROPE, V_HEAD = 128, 64, 128
ROPE_BASE = 10000.0
LN_EPS, RMS_EPS, NEG_INF = 1e-5, 1e-6, -1e30

UNIT = 1024
RAW = 4
SLOTS = 6
HALVES = 2
BANKS = 4
STEPS = 2

C_ID, C_ROT, C_ONE, C_CNT, C_FREQ, C_HALF = 0, 128, 256, 384, 896, 897
C_ALL = 898

TURN, _rest = [], 2.0 * math.pi
for _shift in (5, 17, 25):
    TURN.append(math.floor(_rest * 2.0 ** _shift) / 2.0 ** _shift)
    _rest -= TURN[-1]
TURN.append(_rest)
ROUND = 1.5 * 2.0 ** 23
PI_IN = 3.1415925


def constants(seq):
    c = np.zeros((P, C_ALL), np.float32)
    c[:, C_ID:C_ID + P] = np.eye(P)
    half = QK_ROPE // 2
    for p in range(P):
        if p % QK_ROPE < half:
            c[p + half, C_ROT + p] = -1.0
        else:
            c[p - half, C_ROT + p] = 1.0
    c[:, C_ONE:C_ONE + P] = 1.0
    for tile in range(2):
        for p in range(P):
            w = POOL_WINDOWS[2 * tile + p // 64]
            c[p, C_CNT + tile * seq:C_CNT + (tile + 1) * seq] = 1.0 / np.minimum(np.arange(seq) + 1, w)
    c[:, C_FREQ] = (np.float32(ROPE_BASE) ** (-np.arange(half, dtype=np.float32) / half))[np.arange(P) % half]
    c[:, C_HALF] = -0.5
    return c


class Plan:

    def __init__(self):
        self.at, self.done, self.units_by = {}, {}, []
        self.n = dict(units=0, items=0)

    def section(self, name, marks):
        self.at[name] = dict(self.n)
        for mark in marks:
            for what in mark:
                if what == "U":
                    self.done["unit", self.n["units"]] = len(self.units_by) + 1
                    self.n["units"] += 1
                elif what == "I":
                    self.done["item", self.n["items"]] = len(self.units_by) + 1
                    self.n["items"] += 1
                else:
                    self.done[what] = len(self.units_by) + 1
            self.units_by.append(self.n["units"])

    def __getitem__(self, name):
        return self.at[name]


def trunk(nc, a, consts, out):
    L, D, F2 = a["ffn1_w13"].shape
    S = a["x"].shape[1]
    F = F2 // 2
    KT, TB, FT = D // P, S // P, F // P
    H = a["w_ukv"].shape[2] // (QK_NOPE + V_HEAD)
    Q_LORA, KV_LORA = a["w_uq"].shape[1], a["w_ukv"].shape[1]
    POOL_W = len(POOL_WINDOWS) * 64
    assert (S, D, FT, H, Q_LORA, KV_LORA) == (256, 1024, 22, 6, 256, 128)
    ALPHA = (2 * L) ** 0.25
    MLA_SCALE = (QK_NOPE + QK_ROPE) ** -0.5
    MEM_SCALE = (D // MEM_HEADS) ** -0.5
    PAIRS = H // 2
    SMALL = L * (len(POOL_WINDOWS) + 5)
    ROWS_TAIL, FFN_TAIL = 6, 4
    FS = FT // 2
    LOOPS = (FS - 3) // STEPS
    LOOP_UNITS = 6 * STEPS
    LOOP_ITEMS = 2 * STEPS
    assert LOOPS * STEPS == FS - 3 and LOOP_UNITS % SLOTS == 0 and LOOP_UNITS % RAW == 0
    assert LOOP_ITEMS % BANKS == 0 and FFN_TAIL == 4

    FILL = {
        (0, "ln0"): [(0, 0)], (0, "sums"): [(0, 1)], (0, "rsqrt"): [(0, 2)], (0, "pt0"): [(0, 3)],
        (0, "pt1"): [(0, 4)], (0, "ln1"): [(0, 5)], (0, "soft"): [(0, 6)], (0, "pt"): [(0, 7)], (0, "ln2"): [(1, 0)],
        (0, "ln3"): [(1, 1)],
        (1, "ln0"): [(1, 2)], (1, "sums"): [(1, 3)], (1, "rsqrt"): [(1, 4)], (1, "pt0"): [(1, 5)],
        (1, "pt1"): [], (1, "ln1"): [(1, 6)], (1, "soft"): [(1, 7)], (1, "pt"): [], (1, "ln2"): [], (1, "ln3"): []}

    MLA_ORDER = [("score", 0), ("exp", 0), ("score", 1), ("exp", 1), ("scale", 0), ("scale", 1), ("fill", "pt0"),
                 ("pt", 0), ("score", 2), ("pv", 0), ("pt", 1), ("exp", 2), ("scale", 2), ("fill", "pt1"), ("pv", 1), ("pt", 2), ("rows", 0), ("pv", 2)]
    MEM_ORDER = [("score", 0), ("score", 1), ("scale", 0), ("scale", 1), ("fill", "soft"), ("pt", 0), ("pt", 1),
                 ("fill", "pt"), ("pv", 0), ("pt", 2), ("pv", 1), ("pt", 3), ("pv", 2), ("pv", 3)]

    plan = Plan()
    UI, ITEM, UNIT_ = ["U", "I"], ["I"], ["U"]

    def plan_fill(l, place):
        for part in FILL[l, place]:
            plan.section(("kv", *part), [UNIT_, UI])

    def plan_rows(name, e, begun=0):
        plan.section(name, [UNIT_] * (KT - ROWS_TAIL - begun) + [[("y", e, 0)]] + [UNIT_] * (ROWS_TAIL - 1)
                     + [["U", ("y", e, 1)]])

    def plan_turn(job):
        plan.section(("turn", job), turned(job))

    def turned(job):
        return [[("turned", job, c)] for c in range(HALVES)]

    def plan_norm(e, l, place):
        plan_turn(4 + 2 * e)
        plan_fill(l, place)
        plan_turn(5 + 2 * e)

    def plan_ffn(l, w):
        e = 4 * l + 3 * w
        meanwhile = turned(2) + turned(3) if e == 0 else []
        up, down = [UNIT_, UI] * 2, [UNIT_] * 2
        plan.section(("ffn", l, w), up + meanwhile + up + down + (up + down) * (FS - 3) + up
                     + [[("y", e, 0)]] + [UNIT_] * (FFN_TAIL - 1) + [["U", ("y", e, 1)]])

    for b in range(TB):
        plan_turn(b)
    for l in range(L):
        plan_ffn(l, 0)
        plan_norm(4 * l, l, "ln0")
        plan.section(("win", l), [UNIT_, UI] * 3)
        plan.section(("sums", l), [ITEM])
        plan_fill(l, "sums")
        plan.section(("rsqrt", l), [ITEM])
        plan_fill(l, "rsqrt")
        plan.section(("uqC", l), [ITEM, UI])
        plan.section(("uqA", l), [ITEM, UI])
        plan.section(("rot", l), [ITEM] * 2)
        plan.section(("pool", l), [ITEM])
        plan.section(("uqB", l), [UI])
        plan.section(("kn", l), [ITEM] * 2 + [UI])
        plan.section(("v", l), [ITEM] * 3 + [UI])
        for step, i in MLA_ORDER:
            if step == "fill":
                plan_fill(l, i)
            elif step == "rows":
                plan.section(("wout", l), [UNIT_] * 2)
            elif step not in ("exp", "scale"):
                plan.section((step, l, i), {"score": [[("score", l, i)]], "pt": [ITEM] * 2, "pv": [ITEM]}[step])
        plan_rows(("wout's rest", l), 4 * l + 1, 2)
        plan_norm(4 * l + 1, l, "ln1")
        plan.section(("wq", l), [UNIT_, UI] * (KT // 2))
        for step, i in MEM_ORDER:
            if step == "fill":
                plan_fill(l, i)
            elif step != "scale":
                plan.section(("m" + step, l, i), {"score": [[("mscore", l, i)]], "pt": [ITEM], "pv": [ITEM]}[step])
        plan_rows(("wo", l), 4 * l + 2)
        plan_norm(4 * l + 2, l, "ln2")
        plan_ffn(l, 1)
        if l < L - 1:
            plan_norm(4 * l + 3, l, "ln3")
    done = plan.done
    UNITS = plan.n["units"]

    def first_of_stage(e):
        return plan[(("win", e // 4), ("wq", e // 4), ("ffn", e // 4, 1), ("ffn", e // 4 + 1, 0))[e % 4]]["units"]

    slot, last_user, free_after = [], [], []
    latest = [k - SLOTS for k in range(SLOTS)]
    for n in range(UNITS):
        usable = list(range(SLOTS))
        after = 0
        for l in range(L):
            if plan["v", l]["units"] <= n < plan["wout", l]["units"] + 4:
                usable.remove(4)
            if plan["win", l]["units"] + 2 <= n < plan["wout", l]["units"] + 5:
                usable.remove(5)
        k = min(usable, key=lambda k: latest[k])
        for l in range(L):
            if k >= 4 and latest[k] < plan["wout", l]["units"] <= n:
                after = done["item", plan["pv", l, PAIRS - 1]["items"]]
        slot.append(k)
        last_user.append(latest[k])
        free_after.append(max(after, done["unit", latest[k]] if latest[k] >= 0 else 0))
        latest[k] = n

    w13 = [a["ffn1_w13"], a["ffn2_w13"]]
    w2 = [a["ffn1_w2"], a["ffn2_w2"]]

    def columns(w, half, lo, n):
        return w.rearrange("(k p) f -> p k f", p=P)[:, 4 * half:4 * half + 4, lo:lo + n]

    def ffn_units(base, s):
        g = base if s == 0 else base + 6 * s - 2
        return g, g + 2, base + 6 * s + 8 if s < FS - 1 else base + 6 * s + 4

    source = {}
    for l in range(L):
        c_q, c_kv, k_pe = POOL_W, POOL_W + Q_LORA, POOL_W + Q_LORA + KV_LORA
        for half in range(2):
            for i in range(8):
                source[plan["kv", l, i]["units"] + half] = (UNIT, [(0, columns(a["mem_wkv"][l], half, i * S, S))])
            u = plan["win", l]["units"] + half
            pe_cols = columns(a["w_in"][l], half, k_pe, QK_ROPE)
            source[u] = (UNIT, [(0, columns(a["w_in"][l], half, c_q, S))])
            source[u + 2] = (UNIT, [(0, columns(a["w_in"][l], half, c_kv, P)),
                                    (P, pe_cols), (P + QK_ROPE, pe_cols)])
            source[u + 4] = (UNIT, [(0, columns(a["w_in"][l], half, 0, S))])
            for t in range(KT // 2):
                source[plan["wq", l]["units"] + 2 * t + half] = (UNIT, [(0, columns(a["mem_wq"][l], half, t * S, S))])
            for w in range(2):
                for s in range(FS):
                    g, up, d = ffn_units(plan["ffn", l, w]["units"], s)
                    source[g + half] = (UNIT, [(0, columns(w13[w][l], half, s * S, S))])
                    source[up + half] = (UNIT, [(0, columns(w13[w][l], half, F + s * S, S))])
                    source[d + half] = (UNIT, [(0, w2[w][l][(2 * s + half) * P:(2 * s + half + 1) * P, :])])
        uq = a["w_uq"][l].rearrange("(k p) (h c) -> p k h c", p=P, h=H)
        ukv = a["w_ukv"][l].rearrange("p (h c) -> p h c", h=H)
        for name, heads, cols in (("uqA", slice(0, 4), slice(0, QK_NOPE)), ("uqB", slice(4, 6), slice(0, QK_NOPE)),
                                  ("uqC", slice(0, 6), slice(QK_NOPE, QK_NOPE + QK_ROPE))):
            size = (heads.stop - heads.start) * (cols.stop - cols.start)
            source[plan[name, l]["units"]] = (2 * size, [(k * size, uq[:, k, heads, cols]) for k in range(2)])
        source[plan["kn", l]["units"]] = (H * QK_NOPE, [(0, ukv[:, :, 0:QK_NOPE])])
        source[plan["v", l]["units"]] = (H * V_HEAD, [(0, ukv[:, :, QK_NOPE:QK_NOPE + V_HEAD])])
        for r in range(KT):
            source[plan["wout", l]["units"] + r] = (UNIT, [(0, a["w_out"][l][r * P:(r + 1) * P, :])])
            source[plan["wo", l]["units"] + r] = (UNIT, [(0, a["mem_wo"][l][r * P:(r + 1) * P, :])])
    assert sorted(source) == list(range(UNITS))
    whole = {plan[name, l]["units"] for name in ("uqA", "uqB", "uqC", "kn", "v") for l in range(L)}

    with ExitStack() as ctx:
        def sb(name, shape, dt=F32):
            return ctx.enter_context(nc.sbuf_tensor(name, shape, dt))

        def sem(name):
            return ctx.enter_context(nc.semaphore(name))

        raw = sb("raw", [P, RAW, UNIT])
        w_hi = sb("w_hi", [P, 4, UNIT], F32R)
        w_lo = sb("w_lo", [P, 4, UNIT], F32R)
        x = sb("x", [P, TB, D])
        tmp = sb("tmp", [P, 2 * D])
        gb = sb("gb", [P, 2, D])
        xT = sb("xT", [P, KT, 2, S], F32R)
        memT = sb("memT", [P, KT, 2, S], F32R)
        memK = sb("memK", [P, KT, 2, S], F32R)
        memV = sb("memV", [P, TB, 2, D], F32R)
        qT = sb("qT", [P, 9, 2, S], F32R)
        v_flat = sb("v_flat", [P, TB * 2 * H * V_HEAD], F32R)
        mixT = sb("mixT", [P, KT, 2, S], F32R)
        cqp = sb("cqp", [P, 6 * S], F32R)
        ev = sb("ev", [P, 2, 2 * S])
        cst = sb("cst", [P, C_ALL])
        cosT = sb("cosT", [P, S])
        sinT = sb("sinT", [P, S])
        diag = sb("diag", [P, 2, S])
        pw = sb("pw", [P, L, 2, P])
        pscale = sb("pscale", [P, L, 2])
        gains = sb("gains", [P, L, 3])
        st = sb("st", [P, 96])
        poolM = sb("poolM", [P, 2, S])
        ps = ctx.enter_context(nc.psum_tensor("ps", [P, 8, 512], F32))

        slot_hi = [w_hi[:, k, :] for k in range(4)] + [v_flat[:, 0:UNIT], v_flat[:, 2 * UNIT:3 * UNIT]]
        slot_lo = [w_lo[:, k, :] for k in range(4)] + [v_flat[:, UNIT:2 * UNIT], cqp[:, 0:UNIT]]

        v = v_flat[:, :].rearrange("p (b c f) -> p b c f", b=TB, c=2)
        knT, krT = xT[:, 0:6], xT[:, 6:8]
        mpT = xT
        aT = mixT
        cq = cqp[:, :].rearrange("p (t c s) -> p t c s", t=3, c=2)
        turned_probs = [
            t.rearrange("p (e c k) -> p e c k", e=2, c=2)
            for t in (cqp[:, :], qT[:, 0:3].rearrange("p t c s -> p (t c s)"), cqp[:, :])]
        ident, rot, ones = cst[:, C_ID:C_ID + P], cst[:, C_ROT:C_ROT + P], cst[:, C_ONE:C_ONE + P]
        inv_count = cst[:, C_CNT:C_CNT + 2 * S].rearrange("p (t s) -> p t s", t=2)

        raw_landed = [sem(f"raw_landed{i}") for i in range(RAW)]
        hi_done, lo_done, pe_done, bank_free = sem("hi_done"), sem("lo_done"), sem("pe_done"), sem("bank_free")
        item_hi, silu_done, hidden_ready = sem("item_hi"), sem("silu_done"), sem("hidden_ready")
        turned_hi, turned_lo = sem("turned_hi"), [sem("turned_lo0"), sem("turned_lo1")]
        turned_plain = sem("turned_plain")
        norm_done, x_scaled, var_ready, rstd_ready = (
            sem("norm_done"), sem("x_scaled"), sem("var_ready"), sem("rstd_ready"))
        gains_landed, ident_landed, consts_landed, mem_landed, x_landed, small_landed, pos_landed = (
            sem("gains_landed"), sem("ident_landed"), sem("consts_landed"), sem("mem_landed"), [sem("x_landed0"), sem("x_landed1")],
            sem("small_landed"), sem("pos_landed"))
        dve_step, pool_step = sem("dve_step"), sem("pool_step")
        angles_ready, tables_done = sem("angles_ready"), sem("tables_done")
        squares_ready, rms_ready, diag_ready, cq_scaled, cq_hi, cq_ready = (
            sem("squares_ready"), sem("rms_ready"), sem("diag_ready"), sem("cq_scaled"), sem("cq_hi"), sem("cq_ready"))
        pooled, rope_cos, rope_sum, rope_hi, rope_ready = (
            sem("pooled"), sem("rope_cos"), sem("rope_sum"), sem("rope_hi"), sem("rope_ready"))
        max_ready, exp_done, probs_ready, stored = (
            sem("max_ready"), sem("exp_done"), sem("probs_ready"), sem("stored"))

        def plus(n, it, per):
            return n if it is None else n + it * per

        def bank(m):
            return ps[:, m % BANKS, :]

        def two(t):
            return t.rearrange("p (t s) -> p t s", t=2)

        def half_T(t, part, b, c):
            return t[:, 4 * c:4 * c + 4, part, b * P:(b + 1) * P]

        def plain_half(job, c):
            t = gb[:, 0, :] if job == 0 else tmp[:, 0:D]
            return t[:, c * 512:(c + 1) * 512].rearrange("p (k s) -> p k s", s=P)

        def turned_half(b, c):
            return ps[:, 4 + 2 * b + c, :].rearrange("p (k s) -> p k s", s=P)

        STATS = [st[:, 12 * b:12 * b + 12] for b in range(2)]
        MEANVAR = [st[:, 28 + 4 * b:30 + 4 * b] for b in range(2)]
        VEPS = [st[:, 30 + 4 * b:31 + 4 * b] for b in range(2)]
        RSTD = [st[:, 31 + 4 * b:32 + 4 * b] for b in range(2)]
        MS, RMS = st[:, 88:92], st[:, 92:96]
        MX, NEGM, SUM, REC = ([st[:, 36 + 12 * q + 4 * i:40 + 12 * q + 4 * i] for i in range(3)] for q in range(4))

        def tiles(t, n):
            return t.rearrange("p (t s) -> p t s", t=n)

        cqf = tiles(tmp[:, 0:3 * S], 3)
        sq_kv = tmp[:, 3 * S:4 * S]
        ropeX = tiles(tmp[:, 4 * S:8 * S], 4)
        ropeZ = tiles(tmp[:, 0:4 * S], 4)
        kv_pe = tiles(tmp[:, 2 * S:6 * S], 4)[:, 0:3:2]
        poolU, poolA = tiles(gb[:, 0, 0:512], 2), tiles(gb[:, 0, 512:1024], 2)
        poolB, sq_q = tiles(gb[:, 1, 0:512], 2), tiles(gb[:, 1, 512:1024], 2)

        def mla_scores(pr):
            k = 4 + 2 * (pr % 2)
            return two(ps[:, k, :]), ps[:, k + 1, 0:2 * P].rearrange("p (e k) -> p e k", e=2)

        def mla_probs(pr):
            s = tmp[:, 768 * (pr % 2):768 * (pr % 2) + 768]
            return two(s[:, 0:512]), s[:, 512:768].rearrange("p (e k) -> p e k", e=2)

        def mem_scores(b):
            return ps[:, 4 + 2 * b:6 + 2 * b, :].rearrange("p b (h k) -> p (b h) k", h=2)

        def mem_probs(b):
            return tmp[:, b * D:(b + 1) * D].rearrange("p (h k) -> p h k", h=MEM_HEADS)

        def turned_value(job, c):
            return HALVES * job + c + 1

        def turned_lo_value(job, c):
            return HALVES * (job // TB) + c + 1

        def normed(e, b, c):
            return HALVES * (2 * e + b) + c + 1

        def kv_part(i, part):
            if i < 4:
                return memK[:, 2 * i:2 * i + 2, part, :]
            return memV[:, :, part, (i - 4) * S:(i - 3) * S]

        block = ctx.enter_context(nc.Block())

        @block.sync
        def _(sp):
            sp.dma_start(cst[:, 0:P], consts[:, 0:P]).then_inc(ident_landed, 16)
            for b in range(TB):
                sp.dma_start(x[:, b, :], a["x"][0, b * P:(b + 1) * P, :]).then_inc(x_landed[b], 16)

            def load(n, parts, it=None):
                if n >= RAW:
                    sp.wait_ge(lo_done, plus(n - RAW + 1, it, LOOP_UNITS))
                k = n % RAW
                for col, src in parts:
                    if len(src.shape) == 2:
                        dst = raw[:, k, :]
                    elif n not in whole:
                        dst = raw[:, k, :].rearrange("p (t c) -> p t c", t=4)[:, :, col:col + src.shape[2]]
                    else:
                        t, c = src.shape[1:]
                        dst = raw[:, k, col:col + t * c].rearrange("p (t c) -> p t c", t=t)
                    sp.dma_start(dst, src).then_inc(raw_landed[k], 16)

            n = 0
            for l in range(L):
                for w in range(2):
                    u = plan["ffn", l, w]["units"]
                    for n in range(n, u + 10):
                        load(n, source[n][1])
                        if n == 2:
                            sp.dma_start(cst[:, P:C_ALL], consts[:, P:C_ALL]).then_inc(consts_landed, 16)
                        if n == RAW - 1:
                            sp.dma_start(tmp[:, :].rearrange("p (b d) -> p b d", b=TB),
                                         a["mem"][0].rearrange("(b p) d -> p b d", p=P)).then_inc(mem_landed, 16)
                    tiles13 = w13[w][l].rearrange("(k p) f -> p k f", p=P)
                    with sp.Fori(0, LOOPS) as it:
                        for s in range(STEPS):
                            g, up, d = ffn_units(u, s + 2)[0], ffn_units(u, s + 2)[1], ffn_units(u, s + 1)[2]
                            col = it * (STEPS * S) + (s + 2) * S
                            for first, at in ((g, col), (up, col + F)):
                                for half in range(2):
                                    load(first + half, [(0, tiles13[:, 4 * half:4 * half + 4, bass.ds(at, S)])], it)
                            for half in range(2):
                                load(d + half, [(0, w2[w][l][bass.ds(col - S + half * P, P), :])], it)
                    n = u + 10 + LOOP_UNITS * LOOPS
            for n in range(n, UNITS):
                load(n, source[n][1])
            for b in range(TB):
                for c in range(HALVES):
                    cols = slice(c * D // 2, (c + 1) * D // 2)
                    sp.wait_ge(norm_done, normed(4 * L - 1, b, c))
                    sp.dma_start(out[0, b * P:(b + 1) * P, cols], x[:, b, cols]).then_inc(stored, 16)
            sp.wait_ge(stored, 16 * TB * HALVES)

        def landed(n):
            return sum(16 * len(source[k][1]) for k in range(n % RAW, n + 1, RAW))

        @block.tensor
        def _(pe):
            milestones = [0]

            def reach(ins, *tags):
                milestones[0] += 1
                for tag in tags:
                    assert done[tag] == milestones[0], (tag, done[tag], milestones[0])
                ins.then_inc(pe_done, 1)

            def product(dst, stand, move, start, stop):
                return nc.tensor.matmul(dst, stand, move, start=start, stop=stop, skip_group_check=True)

            def split_product(dst, stand, move, start, stop):
                product(dst, stand[0], move[0], start, False)
                product(dst, stand[0], move[1], False, False)
                return product(dst, stand[1], move[0], False, stop)

            def take_bank(m, it=None):
                if m >= BANKS:
                    pe.wait_ge(bank_free, plus(m - BANKS + 1, it, LOOP_ITEMS))

            def unit_split(n, it=None):
                pe.wait_ge(lo_done, plus(n + 1, it, LOOP_UNITS))

            def column_tile(m, c, n, offsets, acts, first=True, last_unit=True):
                hi, lo = slot_hi[slot[n]], slot_lo[slot[n]]
                for i, (o, act) in enumerate(zip(offsets, acts)):
                    last = split_product(two(bank(m))[:, c, :], (hi[:, o:o + P], lo[:, o:o + P]),
                                         (act[:, 0, :], act[:, 1, :]), first and c == 0 and i == 0,
                                         last_unit and i == len(acts) - 1)
                return last

            def column_pair(m, n, acts, it=None, arrival=None):
                take_bank(m, it)
                for half in range(2):
                    unit_split(n + half, it)
                    if arrival is not None:
                        for b in range(TB):
                            pe.wait_ge(turned_lo[b], turned_lo_value(arrival, half))
                    for c in range(2):
                        last = column_tile(m, c, n + half, range(c * P, UNIT, S),
                                           [acts[:, 4 * half + k] for k in range(4)], half == 0, half == 1)
                    reach(last, ("unit", n + half), *([("item", m)] if half else []))

            def row_block(n, act, b, first, last_unit):
                hi, lo = act[:, 0, b * P:(b + 1) * P], act[:, 1, b * P:(b + 1) * P]
                for stand, ring, start in ((hi, slot_hi, first), (hi, slot_lo, False), (lo, slot_hi, False)):
                    for c in range(2):
                        last = product(ps[:, 4 + 2 * b + c, :], stand, ring[slot[n]][:, c * 512:(c + 1) * 512],
                                       start, last_unit and stand is lo)
                return last

            def row_unit(n, act, first=False, it=None):
                unit_split(n, it)
                for b in range(TB):
                    last = row_block(n, act, b, first, False)
                reach(last, ("unit", n))

            def row_tail(e, units, acts, wait_for):
                for b in range(TB):
                    for i, n in enumerate(units):
                        if b == 0:
                            unit_split(n)
                            wait_for(i)
                        last = row_block(n, acts[i], b, False, i == len(units) - 1)
                        if b == 1:
                            reach(last, ("unit", n), *([("y", e, 1)] if i == len(units) - 1 else []))
                    if b == 0:
                        reach(last, ("y", e, 0))

            def turn(job, src, b, e=None):
                for c in range(HALVES):
                    if e is not None:
                        pe.wait_ge(norm_done, normed(e, b, c))
                    for k in range(4 * c, 4 * c + 4):
                        last = nc.tensor.transpose(ps[:, 4 + 2 * b + c, (k % 4) * P:(k % 4 + 1) * P],
                                                   src[:, k * P:(k + 1) * P], ident)
                    reach(last, ("turned", job, c))

            def fill(l, place):
                for l, i in FILL[l, place]:
                    u, m = plan["kv", l, i]["units"], plan["kv", l, i]["items"]
                    for b in range(TB):
                        pe.wait_ge(turned_lo[b], turned_lo_value(3, 1))
                    if i < 4:
                        column_pair(m, u, memT)
                        continue
                    take_bank(m)
                    for half in range(2):
                        n = u + half
                        unit_split(n)
                        for b in range(TB):
                            for k in range(4):
                                act = memT[:, 4 * half + k, :, b * P:(b + 1) * P]
                                cols = slice(k * 256, (k + 1) * 256)
                                last = split_product(
                                    two(bank(m))[:, b, :], (act[:, 0, :], act[:, 1, :]),
                                    (slot_hi[slot[n]][:, cols], slot_lo[slot[n]][:, cols]),
                                    half == 0 and b == 0 and k == 0, half == 1 and k == 3)
                        reach(last, ("unit", n), *([("item", m)] if half else []))

            def norm(e, l, place):
                turn(4 + 2 * e, x[:, 0, :], 0, e)
                fill(l, place)
                turn(5 + 2 * e, x[:, 1, :], 1, e)

            def ffn(l, w):
                e, f = 4 * l + 3 * w, (2 * l + w) * FS
                u, m = plan["ffn", l, w]["units"], plan["ffn", l, w]["items"]

                def up(s, it=None, arrival=None):
                    g, up_, _ = ffn_units(u, s)
                    column_pair(m + 2 * s, g, xT, it, arrival)
                    column_pair(m + 2 * s + 1, up_, xT, it)

                def down(s, it=None):
                    pe.wait_ge(hidden_ready, plus(f + s + 1, it, STEPS))
                    for t in range(2):
                        row_unit(ffn_units(u, s)[2] + t, aT[:, 2 * (s % 2) + t], s == 0 and t == 0, it)

                up(0, arrival=1 if e == 0 else 3 + 2 * e)
                if e == 0:
                    pe.wait_ge(mem_landed, 16)
                    for b in range(TB):
                        turn(2 + b, tmp[:, b * D:(b + 1) * D], b)
                up(1)
                if e == 0:
                    for b in range(TB):
                        pe.wait_ge(turned_lo[b], turned_lo_value(3, 1))
                down(0)
                with pe.Fori(0, LOOPS) as it:
                    for s in range(STEPS):
                        up(s + 2, it)
                        down(s + 1, it)
                milestones[0] += LOOP_UNITS * (LOOPS - 1)
                up(FS - 1)
                tail = [(s, t) for s in (FS - 2, FS - 1) for t in range(2)]
                row_tail(e, [ffn_units(u, s)[2] + t for s, t in tail], [aT[:, 2 * (s % 2) + t] for s, t in tail],
                         lambda i: pe.wait_ge(hidden_ready, f + tail[i][0] + 1))

            def mix(l):
                at = {k: plan[k, l] for k in ("win", "sums", "rsqrt", "uqA", "uqB", "uqC", "kn", "v", "rot", "pool")}
                for t in range(3):
                    column_pair(at["win"]["items"] + t, at["win"]["units"] + 2 * t, xT,
                                arrival=None if t else 5 + 2 * (4 * l))

                pe.wait_ge(consts_landed, 16)
                m = at["sums"]["items"]
                take_bank(m)
                pe.wait_ge(squares_ready, l + 1)
                for b in range(TB):
                    rows = slice(b * P, (b + 1) * P)
                    for t in range(2):
                        nc.tensor.matmul(bank(m)[:, b:b + 1], sq_q[:, t, rows], ones[:, 0:1],
                                         start=b == 0 and t == 0, stop=t == 1, skip_group_check=True)
                    last = nc.tensor.matmul(bank(m)[:, 2 + b:3 + b], sq_kv[:, rows], ones[:, 0:1],
                                            start=False, stop=True, skip_group_check=True)
                reach(last, ("item", m))
                fill(l, "sums")
                m = at["rsqrt"]["items"]
                take_bank(m)
                pe.wait_ge(diag_ready, l + 1)
                for i in range(2):
                    for b in range(TB):
                        last = nc.tensor.matmul(two(bank(m))[:, i, b * P:(b + 1) * P], ones,
                                                diag[:, i, b * P:(b + 1) * P], start=i == 0 and b == 0, stop=True,
                                                skip_group_check=True)
                reach(last, ("item", m))
                fill(l, "rsqrt")

                def items_of(name, tiles_, offsets, acts):
                    n, m = at[name]["units"], at[name]["items"]
                    unit_split(n)
                    for i in range(tiles_):
                        if i % 2 == 0:
                            take_bank(m + i // 2)
                        last = column_tile(m + i // 2, i % 2, n, offsets(i), acts)
                        if i % 2 or i == tiles_ - 1:
                            reach(last, ("item", m + i // 2), *([("unit", n)] if i == tiles_ - 1 else []))

                c_q = [cq[:, k] for k in range(2)]
                pe.wait_ge(cq_ready, 2 * l + 1)
                items_of("uqC", 3, lambda i: [k * 6 * QK_ROPE + i * P for k in range(2)], c_q)
                items_of("uqA", 4, lambda i: [(4 * k + i) * P for k in range(2)], c_q)
                pe.wait_ge(bank_free, at["uqC"]["items"] + 2)
                m = at["rot"]["items"]
                for i in range(2):
                    take_bank(m + i)
                    for t in range(2):
                        last = nc.tensor.matmul(bank(m + i)[:, t * S:(t + 1) * S], rot, ropeX[:, 2 * i + t, :],
                                                start=t == 0, stop=True, skip_group_check=True)
                    reach(last, ("item", m + i))
                m = at["pool"]["items"]
                take_bank(m)
                pe.wait_ge(pooled, l + 1)
                pe.wait_ge(small_landed, 16 * SMALL)
                for t in range(2):
                    last = nc.tensor.matmul(bank(m)[:, t * S:(t + 1) * S], pw[:, l, t, :], poolB[:, t, :],
                                            start=t == 0, stop=True, skip_group_check=True)
                reach(last, ("item", m))
                items_of("uqB", 2, lambda i: [(2 * k + i) * P for k in range(2)], c_q)
                pe.wait_ge(cq_ready, 2 * l + 2)
                items_of("kn", 6, lambda i: [i * P], [cq[:, 2]])
                n, m = at["v"]["units"], at["v"]["items"]
                unit_split(n)
                for i in range(4):
                    take_bank(m + i)
                    rows = slice((i // 2) * P, (i // 2 + 1) * P)
                    cols = slice((i % 2) * 384, (i % 2 + 1) * 384)
                    last = split_product(bank(m + i)[:, 0:384], (cq[:, 2, 0, rows], cq[:, 2, 1, rows]),
                                         (slot_hi[slot[n]][:, cols], slot_lo[slot[n]][:, cols]), True, True)
                    reach(last, ("item", m + i), *([("unit", n)] if i == 3 else []))

                pe.wait_ge(rope_ready, l + 1)
                for step, i in MLA_ORDER:
                    if step == "score":
                        mla_score(l, i)
                    elif step == "pt":
                        mla_turn(l, i)
                    elif step == "pv":
                        mla_values(l, i)
                    elif step == "fill":
                        fill(l, i)
                    elif step == "rows":
                        pe.wait_ge(bank_free, at["pool"]["items"] + 1)
                        for r in range(2):
                            row_unit(plan["wout", l]["units"] + r, mixT[:, r], r == 0)
                n = plan["wout", l]["units"]

                def wait_values(r):
                    if r % 2 == 0:
                        pe.wait_ge(bank_free, plan["pv", l, (r - 2) // 2]["items"] + 1)
                for r in range(2, KT - ROWS_TAIL):
                    wait_values(r)
                    row_unit(n + r, mixT[:, r])
                tail = range(KT - ROWS_TAIL, KT)
                row_tail(4 * l + 1, [n + r for r in tail], [mixT[:, r] for r in tail], lambda i: wait_values(tail[i]))

            def mla_score(l, pr):
                pe.wait_ge(bank_free, plan["kn", l]["items"] + pr + 1)
                if pr == 2:
                    pe.wait_ge(exp_done, 5 * l + 1)
                s1, s0 = mla_scores(pr)
                for e in range(2):
                    parts = ((qT[:, 2 * pr + e], knT[:, 2 * pr + e]), (qT[:, 6 + pr], krT[:, e]))
                    for i, (q, k) in enumerate(parts):
                        split_product(s1[:, e, :], (q[:, 0, P:S], q[:, 1, P:S]), (k[:, 0, :], k[:, 1, :]),
                                      i == 0 and e == 0, i == 1)
                    for i, (q, k) in enumerate(parts):
                        last = split_product(s0[:, e, :], (q[:, 0, 0:P], q[:, 1, 0:P]), (k[:, 0, 0:P], k[:, 1, 0:P]),
                                             i == 0 and e == 0, i == 1)
                reach(last, ("score", l, pr))

            def mla_turn(l, pr):
                s1, s0 = mla_probs(pr)
                m = plan["pt", l, pr]["items"]
                pe.wait_ge(probs_ready, 5 * l + pr + 1)
                for e in range(2):
                    take_bank(m + e)
                    nc.tensor.transpose(bank(m + e)[:, 0:P], s0[:, e, :], ident)
                    nc.tensor.transpose(bank(m + e)[:, P:2 * P], s1[:, e, 0:P], ident)
                    last = nc.tensor.transpose(bank(m + e)[:, 2 * P:3 * P], s1[:, e, P:2 * P], ident)
                    reach(last, ("item", m + e))

            def mla_values(l, pr):
                pT = turned_probs[pr]
                m = plan["pv", l, pr]["items"]
                take_bank(m)
                for e in range(2):
                    pe.wait_ge(bank_free, plan["pt", l, pr]["items"] + e + 1)
                    cols = slice((2 * pr + e) * P, (2 * pr + e + 1) * P)
                    dst = two(bank(m))[:, e, :]
                    split_product(dst, (v[:, 0, 0, cols], v[:, 0, 1, cols]), (pT[:, e, 0, 0:S], pT[:, e, 1, 0:S]),
                                  e == 0, False)
                    last = split_product(dst[:, P:S], (v[:, 1, 0, cols], v[:, 1, 1, cols]),
                                         (pT[:, e, 0, S:S + P], pT[:, e, 1, S:S + P]), False, True)
                reach(last, ("item", m))

            def memory(l):
                u, m = plan["wq", l]["units"], plan["wq", l]["items"]
                for t in range(KT // 2):
                    column_pair(m + t, u + 2 * t, xT, arrival=None if t else 5 + 2 * (4 * l + 1))
                for step, i in MEM_ORDER:
                    if step == "score":
                        for hh in range(MEM_HEADS):
                            if i == 0:
                                pe.wait_ge(bank_free, m + hh + 1)
                            for t in range(2):
                                q, k = qT[:, 2 * hh + t, :, i * P:(i + 1) * P], memK[:, 2 * hh + t]
                                last = split_product(mem_scores(i)[:, hh, :], (q[:, 0, :], q[:, 1, :]),
                                                     (k[:, 0, :], k[:, 1, :]), t == 0 and hh % 2 == 0, t == 1)
                        reach(last, ("mscore", l, i))
                    elif step == "fill":
                        fill(l, i)
                    elif step == "pt":
                        if i == 0:
                            pe.wait_ge(probs_ready, 5 * l + PAIRS + 2)
                        m = plan["mpt", l, i]["items"]
                        take_bank(m)
                        for kt in range(2):
                            for b in range(TB):
                                last = nc.tensor.transpose(bank(m)[:, kt * S + b * P:kt * S + (b + 1) * P],
                                                           mem_probs(b)[:, i, kt * P:(kt + 1) * P], ident)
                        reach(last, ("item", m))
                    elif step == "pv":
                        m = plan["mpv", l, i]["items"]
                        take_bank(m)
                        pe.wait_ge(bank_free, plan["mpt", l, i]["items"] + 1)
                        pe.wait_ge(bank_free, plan["kv", l, 4 + i]["items"] + 1)
                        for c in range(2):
                            t = 2 * i + c
                            for kt in range(2):
                                p, cols = mpT[:, 2 * i + kt], slice(t * P, (t + 1) * P)
                                last = split_product(two(bank(m))[:, c, :],
                                                     (memV[:, kt, 0, cols], memV[:, kt, 1, cols]),
                                                     (p[:, 0, :], p[:, 1, :]), c == 0 and kt == 0, kt == 1)
                        reach(last, ("item", m))
                n = plan["wo", l]["units"]

                def wait_values(r):
                    if r % 2 == 0:
                        pe.wait_ge(bank_free, plan["mpv", l, r // 2]["items"] + 1)
                for r in range(KT - ROWS_TAIL):
                    wait_values(r)
                    row_unit(n + r, mixT[:, r], r == 0)
                tail = range(KT - ROWS_TAIL, KT)
                row_tail(4 * l + 2, [n + r for r in tail], [mixT[:, r] for r in tail], lambda i: wait_values(tail[i]))

            pe.wait_ge(ident_landed, 16)
            for b in range(TB):
                pe.wait_ge(x_landed[b], 16)
                turn(b, x[:, b, :], b)
            for l in range(L):
                ffn(l, 0)
                norm(4 * l, l, "ln0")
                mix(l)
                norm(4 * l + 1, l, "ln1")
                memory(l)
                norm(4 * l + 2, l, "ln2")
                ffn(l, 1)
                if l < L - 1:
                    norm(4 * l + 3, l, "ln3")
            assert milestones[0] == len(plan.units_by)

        def look_ahead(split):
            state = dict(next=0)

            def ahead_to(limit):
                while state["next"] < min(UNITS, limit):
                    split(state["next"])
                    state["next"] += 1

            def ahead(tag, more=0):
                limit = state["next"]
                while (limit < UNITS and last_user[limit] <= plan.units_by[done[tag] - 1] - 2 + more
                       and free_after[limit] <= done[tag]):
                    limit += 1
                ahead_to(limit)
            return state, ahead, ahead_to

        def loop_first(l, w):
            first = plan["ffn", l, w]["units"] + 7 + SLOTS
            for n in range(first, first + LOOP_UNITS * (LOOPS - 1)):
                assert slot[n + LOOP_UNITS] == slot[n] and free_after[n + LOOP_UNITS] == free_after[n] + LOOP_UNITS
            return first

        @block.scalar
        def _(act):
            def split_hi(n, it=None):
                act.wait_ge(raw_landed[n % RAW], plus(landed(n), it, 16 * LOOP_UNITS // RAW))
                if free_after[n]:
                    act.wait_ge(pe_done, plus(free_after[n], it, LOOP_UNITS))
                size = source[n][0]
                nc.scalar.copy(slot_hi[slot[n]][:, 0:size], raw[:, n % RAW, 0:size]).then_inc(hi_done, 1)

            state, ahead, ahead_to = look_ahead(split_hi)

            def round_item(m, dst, src, scale=None, eager=True):
                if eager:
                    ahead(("item", m))
                act.wait_ge(pe_done, done["item", m])
                if scale is None:
                    nc.scalar.copy(dst, src).then_inc(item_hi, 1)
                    return
                for t in range(2):
                    last = nc.scalar.mul(dst[:, t, :], src[:, t, :], scale[:, t:t + 1])
                last.then_inc(item_hi, 1)

            def round_tiles(name, dst, eager=True):
                m = plan[name]["items"]
                for i in range(dst.shape[1] // 2):
                    round_item(m + i, dst[:, 2 * i:2 * i + 2, 0, :], two(bank(m + i)), eager=eager)

            def fill(l, place, eager=True):
                for l, i in FILL[l, place]:
                    m = plan["kv", l, i]["items"]
                    ahead_to(plan["kv", l, i]["units"] + 2)
                    round_item(m, kv_part(i, 0), two(bank(m)), eager=eager)

            def turn(job, dst, b):
                for c in range(HALVES):
                    act.wait_ge(pe_done, done["turned", job, c])
                    nc.scalar.copy(half_T(dst, 0, b, c), turned_half(b, c)).then_inc(turned_hi, 1)
                    if b == 0:
                        nc.scalar.copy(plain_half(job, c), turned_half(b, c)).then_inc(turned_plain, 1)

            def ffn(l, w):
                m, f = plan["ffn", l, w]["items"], (2 * l + w) * FS

                def gate(s, it=None):
                    act.wait_ge(pe_done, plus(done["item", m + 2 * s], it, LOOP_UNITS))
                    if f + s >= 2:
                        act.wait_ge(hidden_ready, plus(f + s - 1, it, STEPS))
                    nc.scalar.activation(ev[:, (f + s) % 2, :], bank(m + 2 * s), ACT.Silu).then_inc(silu_done, 1)

                for s in range(2):
                    ahead(("item", m + 2 * s))
                    gate(s)
                    ahead(("item", m + 2 * s + 1))
                    if s == 0 and l == 0 and w == 0:
                        for b in range(TB):
                            turn(2 + b, memT, b)
                first = loop_first(l, w)
                assert state["next"] == first, (state["next"], first)
                with act.Fori(0, LOOPS) as it:
                    for s in range(STEPS):
                        for n in range(first + 6 * s, first + 6 * s + 4):
                            split_hi(n, it)
                        gate(s + 2, it)
                        for n in range(first + 6 * s + 4, first + 6 * s + 6):
                            split_hi(n, it)
                state["next"] = first + LOOP_UNITS * LOOPS
                if l == 0 and w == 0:
                    act.wait_ge(angles_ready, 2)
                    nc.scalar.activation(cosT[:, :], gb[:, 0, 0:S], ACT.Sin)
                    nc.scalar.activation(sinT[:, :], gb[:, 0, S:2 * S], ACT.Sin).then_inc(tables_done, 1)
                ahead(("item", m + 2 * (FS - 1)))
                gate(FS - 1)
                ahead(("item", m + 2 * (FS - 1) + 1))

            def norm(e, l, place):
                ahead(("y", e, 0), 1)
                ahead_to(plan.units_by[done["y", e, 1] - 1] + 2)
                turn(4 + 2 * e, xT, 0)
                ahead_to(first_of_stage(e) + 1)
                fill(l, place, eager=False)
                turn(5 + 2 * e, xT, 1)

            def exponentials(j, views):
                act.wait_ge(max_ready, j + 1)
                for i, (dst, src, scale) in enumerate(views):
                    last = nc.scalar.activation(dst, src, ACT.Exp, bias=NEGM[j % 3][:, i:i + 1], scale=scale,
                                                accum_out=SUM[j % 3][:, i:i + 1])
                last.then_inc(exp_done, 1)

            def mix(l):
                round_c_q_and_c_kv(l)
                fill(l, "rsqrt")
                ahead_to(plan["v", l]["units"] + 1)
                round_tiles(("uqA", l), qT[:, 0:4], eager=False)
                m = plan["pool", l]["items"]
                round_item(m, mixT[:, 0:2, 0, :], two(bank(m)), pscale[:, l, :], eager=False)
                round_tiles(("uqB", l), qT[:, 4:6], eager=False)
                act.wait_ge(rope_sum, l + 1)
                nc.scalar.copy(qT[:, 6:9, 0, :], ropeZ[:, 1:4, :])
                for e in range(2):
                    rows = slice(e * 64, e * 64 + 64)
                    last = nc.scalar.copy(krT[rows, e, 0, :], ropeZ[rows, 0, :])
                last.then_inc(rope_hi, 1)
                round_tiles(("kn", l), knT, eager=False)
                m = plan["v", l]["items"]
                for i in range(4):
                    round_item(m + i, v[:, i // 2, 0, (i % 2) * 384:(i % 2 + 1) * 384], bank(m + i)[:, 0:384], eager=False)
                for step, pr in MLA_ORDER:
                    if step == "exp":
                        (s1, s0), (p1, p0) = mla_scores(pr), mla_probs(pr)
                        ahead(("score", l, pr))
                        exponentials(5 * l + pr, [(p[:, e, :], s[:, e, :], MLA_SCALE)
                                                  for p, s in ((p1, s1), (p0, s0)) for e in range(2)])
                    elif step == "pt":
                        m = plan["pt", l, pr]["items"]
                        for e in range(2):
                            round_item(m + e, turned_probs[pr][:, e, 0, :], bank(m + e)[:, 0:384])
                    elif step == "pv":
                        round_tiles(("pv", l, pr), mixT[:, 2 + 2 * pr:4 + 2 * pr])
                    elif step == "fill":
                        fill(l, pr)

            def round_c_q_and_c_kv(l):
                ahead(("item", plan["sums", l]["items"]))
                fill(l, "sums")
                ahead(("item", plan["rsqrt", l]["items"]))
                act.wait_ge(cq_scaled, l + 1)
                nc.scalar.copy(cq[:, 0:2, 0, :], cqf[:, 0:2, :]).then_inc(cq_hi, 1)
                act.wait_ge(bank_free, plan["rsqrt", l]["items"] + 1)
                nc.scalar.copy(cq[:, 2, 0, :], cqf[:, 2, :]).then_inc(cq_hi, 1)

            def memory(l):
                round_tiles(("wq", l), qT[:, 0:8])
                for step, i in MEM_ORDER:
                    if step == "score":
                        ahead(("mscore", l, i))
                        exponentials(5 * l + PAIRS + i, [(mem_probs(i)[:, hh, :], mem_scores(i)[:, hh, :], MEM_SCALE)
                                                         for hh in range(MEM_HEADS)])
                    elif step == "pt":
                        round_tiles(("mpt", l, i), mpT[:, 2 * i:2 * i + 2])
                    elif step == "pv":
                        round_tiles(("mpv", l, i), mixT[:, 2 * i:2 * i + 2])
                    elif step == "fill":
                        fill(l, i)

            for b in range(TB):
                turn(b, xT, b)
            for l in range(L):
                ffn(l, 0)
                norm(4 * l, l, "ln0")
                if l == 0:
                    act.wait_ge(small_landed, 16 * SMALL)
                mix(l)
                norm(4 * l + 1, l, "ln1")
                memory(l)
                norm(4 * l + 2, l, "ln2")
                ffn(l, 1)
                if l < L - 1:
                    norm(4 * l + 3, l, "ln3")

        @block.vector
        def _(dve):
            steps, rounded = [0], [0]

            def own(ins):
                steps[0] += 1
                ins.then_inc(dve_step, 1)

            def settle(it=None):
                dve.wait_ge(dve_step, plus(steps[0], it, STEPS))

            def split_lo(n, it=None):
                dve.wait_ge(hi_done, plus(n + 1, it, LOOP_UNITS))
                s = slice(0, source[n][0])
                nc.vector.tensor_tensor(slot_lo[slot[n]][:, s], raw[:, n % RAW, s],
                                        slot_hi[slot[n]][:, s].bitcast(F32), ALU.subtract).then_inc(lo_done, 1)

            state, ahead, ahead_to = look_ahead(split_lo)

            def split_item(m, dst, src, hi, scale=None, eager=True):
                if eager:
                    ahead(("item", m))
                rounded[0] += 1
                dve.wait_ge(item_hi, rounded[0])
                if scale is None:
                    nc.vector.tensor_tensor(dst, src, hi.bitcast(F32), ALU.subtract).then_inc(bank_free, 1)
                    return
                for t in range(2):
                    last = nc.vector.scalar_tensor_tensor(out=dst[:, t, :], in0=src[:, t, :], scalar=scale[:, t:t + 1],
                                                          in1=hi[:, t, :].bitcast(F32), op0=ALU.mult,
                                                          op1=ALU.subtract)
                last.then_inc(bank_free, 1)

            def split_tiles(name, dst, eager=True):
                m = plan[name]["items"]
                for i in range(dst.shape[1] // 2):
                    pair = dst[:, 2 * i:2 * i + 2]
                    split_item(m + i, pair[:, :, 1, :], two(bank(m + i)), pair[:, :, 0, :], eager=eager)

            def fill(l, place, eager=True):
                for l, i in FILL[l, place]:
                    m = plan["kv", l, i]["items"]
                    ahead_to(plan["kv", l, i]["units"] + 2)
                    split_item(m, kv_part(i, 1), two(bank(m)), kv_part(i, 0), eager=eager)

            def turn(job, dst):
                for c in range(HALVES):
                    dve.wait_ge(turned_hi, turned_value(job, c))
                    nc.vector.tensor_tensor(half_T(dst, 1, 1, c), turned_half(1, c),
                                            half_T(dst, 0, 1, c).bitcast(F32), ALU.subtract).then_inc(turned_lo[1], 1)

            def ffn(l, w):
                m, f = plan["ffn", l, w]["items"], (2 * l + w) * FS

                def hidden(s, it=None):
                    h, hid = ev[:, (f + s) % 2, :], aT[:, 2 * (s % 2):2 * (s % 2) + 2]
                    dve.wait_ge(silu_done, plus(f + s + 1, it, STEPS))
                    dve.wait_ge(pe_done, plus(done["item", m + 2 * s + 1], it, LOOP_UNITS))
                    nc.vector.tensor_tensor(h, bank(m + 2 * s + 1), h, ALU.mult).then_inc(bank_free, 2)
                    dve.wait_ge(bank_free, plus(m + 2 * s + 2, it, LOOP_ITEMS))
                    own(nc.vector.tensor_copy(hid[:, :, 0, :], two(h)))
                    settle(it)
                    nc.vector.tensor_tensor(hid[:, :, 1, :], two(h), hid[:, :, 0, :].bitcast(F32), ALU.subtract)\
                        .then_inc(hidden_ready, 1)

                for s in range(2):
                    ahead(("item", m + 2 * s + 1))
                    hidden(s)
                    if s == 0 and l == 0 and w == 0:
                        turn(3, memT)
                first = loop_first(l, w)
                assert state["next"] == first
                with dve.Fori(0, LOOPS) as it:
                    for s in range(STEPS):
                        for n in range(first + 6 * s, first + 6 * s + 6):
                            split_lo(n, it)
                        hidden(s + 2, it)
                state["next"] = first + LOOP_UNITS * LOOPS
                steps[0] += STEPS * (LOOPS - 1)
                ahead(("item", m + 2 * (FS - 1) + 1))
                hidden(FS - 1)

            def norm(e, l=None, place=None):
                weight = 0.5 if e % 4 in (0, 3) else 1.0

                def statistics(b):
                    dve.wait_ge(x_scaled, 2 * e + b + 1)
                    dve.wait_ge(pe_done, done["y", e, b])
                    z = x[:, b, :].rearrange("p (c s) -> p c s", c=2)
                    own(nc.vector.scalar_tensor_tensor(out=z, in0=ps[:, 4 + 2 * b:6 + 2 * b, :], scalar=weight,
                                                       in1=z, op0=ALU.mult, op1=ALU.add))
                    settle()
                    for c in range(2):
                        own(nc.vector.bn_stats(STATS[b][:, 6 * c:6 * c + 6], z[:, c, :]))
                    settle()
                    own(nc.vector.bn_aggr(MEANVAR[b], STATS[b]))
                    settle()
                    nc.vector.tensor_scalar(VEPS[b], MEANVAR[b][:, 1:2], LN_EPS, None, ALU.add)\
                        .then_inc(var_ready, 1)

                def apply(b):
                    dve.wait_ge(gains_landed, 32 * (e + 1))
                    own(nc.vector.scalar_tensor_tensor(out=x[:, b, :], in0=x[:, b, :], scalar=MEANVAR[b][:, 0:1],
                                                       in1=gb[:, 0, :], op0=ALU.subtract, op1=ALU.mult))
                    settle()
                    dve.wait_ge(rstd_ready, 2 * e + b + 1)
                    for c in range(HALVES):
                        cols = slice(c * D // 2, (c + 1) * D // 2)
                        nc.vector.scalar_tensor_tensor(out=x[:, b, cols], in0=x[:, b, cols], scalar=RSTD[b],
                                                       in1=gb[:, 1, cols], op0=ALU.mult, op1=ALU.add)\
                            .then_inc(norm_done, 1)

                ahead(("y", e, 0), 1)
                statistics(0)
                apply(0)
                ahead_to(plan.units_by[done["y", e, 1] - 1] + 2)
                statistics(1)
                if place is None:
                    apply(1)
                    return
                apply(1)
                ahead_to(first_of_stage(e) + 1)
                fill(l, place, eager=False)
                turn(5 + 2 * e, xT)

            def maxima(j, scores, masked, scale):
                for s in masked:
                    own(nc.vector.memset(s, NEG_INF))
                settle()
                for i, s in enumerate(scores):
                    n = s.shape[1]
                    own(nc.vector.tensor_reduce(MX[j % 3][:, 2 * i:2 * i + n], s, AX.X, ALU.max))
                settle()
                nc.vector.tensor_scalar(NEGM[j % 3], MX[j % 3], scale, -1.0, ALU.mult, ALU.mult).then_inc(max_ready, 1)

            def scale_probs(j, probs):
                dve.wait_ge(exp_done, j + 1)
                own(nc.vector.reciprocal(REC[j % 3], SUM[j % 3]))
                settle()
                for i, p in enumerate(probs):
                    last = nc.vector.tensor_scalar(p, p, REC[j % 3][:, i:i + 1], None, ALU.mult)
                last.then_inc(probs_ready, 1)

            def mix(l):
                m = plan["win", l]["items"]
                ahead(("item", m))
                dve.wait_ge(pe_done, done["item", m])
                nc.vector.tensor_copy(cqf[:, 0:2, :], two(bank(m))).then_inc(bank_free, 1)
                dve.wait_ge(bank_free, m + 1)
                own(nc.vector.tensor_tensor(sq_q, cqf[:, 0:2, :], cqf[:, 0:2, :], ALU.mult))
                ahead(("item", m + 1))
                dve.wait_ge(pe_done, done["item", m + 1])
                nc.vector.tensor_copy(kv_pe, two(bank(m + 1))).then_inc(bank_free, 1)
                dve.wait_ge(bank_free, m + 2)
                nc.vector.tensor_tensor(sq_kv, cqf[:, 2, :], cqf[:, 2, :], ALU.mult).then_inc(squares_ready, 1)
                ahead(("item", m + 2))
                dve.wait_ge(pe_done, done["item", m + 2])
                nc.vector.tensor_copy(poolU, two(bank(m + 2))).then_inc(bank_free, 1)
                m = plan["sums", l]["items"]
                dve.wait_ge(pe_done, done["item", m])
                own(nc.vector.tensor_scalar(MS[:, 0:2], bank(m)[:, 0:2], 1.0 / Q_LORA, RMS_EPS, ALU.mult, ALU.add))
                nc.vector.tensor_scalar(MS[:, 2:4], bank(m)[:, 2:4], 1.0 / KV_LORA, RMS_EPS, ALU.mult, ALU.add)\
                    .then_inc(bank_free, 1)
                dve.wait_ge(rms_ready, l + 1)
                for i in range(2):
                    for b in range(TB):
                        last = nc.vector.tensor_scalar(diag[:, i, b * P:(b + 1) * P], ident,
                                                       RMS[:, 2 * i + b:2 * i + b + 1], None, ALU.mult)
                last.then_inc(diag_ready, 1)
                for e in range(2):
                    own(nc.vector.memset(krT[(1 - e) * 64:(2 - e) * 64, e].bitcast(F32), 0.0))
                ahead(("item", m))
                fill(l, "sums")
                m = plan["rsqrt", l]["items"]
                ahead(("item", m))
                dve.wait_ge(pe_done, done["item", m])
                for k in range(3):
                    ins = nc.vector.scalar_tensor_tensor(out=cqf[:, k, :], in0=cqf[:, k, :],
                                                         scalar=gains[:, l, k:k + 1], in1=two(bank(m))[:, k // 2, :],
                                                         op0=ALU.mult, op1=ALU.mult)
                    if k:
                        ins.then_inc((cq_scaled, bank_free)[k - 1], 1)
                for i, t in enumerate((slice(0, 2), slice(2, 3))):
                    dve.wait_ge(cq_hi, 2 * l + i + 1)
                    nc.vector.tensor_tensor(cq[:, t, 1, :], cqf[:, t, :], cq[:, t, 0, :].bitcast(F32), ALU.subtract)\
                        .then_inc(cq_ready, 1)
                fill(l, "rsqrt")
                m = plan["uqC", l]["items"]
                dve.wait_ge(pe_done, done["item", m])
                nc.vector.tensor_copy(ropeX[:, 1:3, :], two(bank(m))).then_inc(bank_free, 1)
                dve.wait_ge(pe_done, done["item", m + 1])
                nc.vector.tensor_copy(ropeX[:, 3, :], bank(m + 1)[:, 0:S]).then_inc(bank_free, 1)
                ahead_to(plan["v", l]["units"] + 1)
                split_tiles(("uqA", l), qT[:, 0:4], eager=False)
                m = plan["rot", l]["items"]
                for i in range(2):
                    z = ropeZ[:, 2 * i:2 * i + 2, :]
                    dve.wait_ge(pe_done, done["item", m + i])
                    nc.vector.tensor_tensor(z, two(bank(m + i)),
                                            sinT[:, :].unsqueeze(1).broadcast_to([P, 2, S]), ALU.mult)\
                        .then_inc(bank_free, 1)
                dve.wait_ge(bank_free, m + 2)
                dve.wait_ge(rope_cos, l + 1)
                nc.vector.tensor_tensor(ropeZ, ropeZ, ropeX, ALU.add).then_inc(rope_sum, 1)
                dve.wait_ge(rope_sum, l + 1)
                m = plan["pool", l]["items"]
                split_item(m, mixT[:, 0:2, 1, :], two(bank(m)), mixT[:, 0:2, 0, :], pscale[:, l, :], eager=False)
                split_tiles(("uqB", l), qT[:, 4:6], eager=False)
                dve.wait_ge(rope_hi, l + 1)
                own(nc.vector.tensor_tensor(qT[:, 6:9, 1, :], ropeZ[:, 1:4, :], qT[:, 6:9, 0, :].bitcast(F32),
                                            ALU.subtract))
                for e in range(2):
                    rows = slice(e * 64, e * 64 + 64)
                    last = nc.vector.tensor_tensor(krT[rows, e, 1, :], ropeZ[rows, 0, :],
                                                   krT[rows, e, 0, :].bitcast(F32), ALU.subtract)
                last.then_inc(rope_ready, 1)
                split_tiles(("kn", l), knT, eager=False)
                m = plan["v", l]["items"]
                for i in range(4):
                    hi, lo = (v[:, i // 2, c, (i % 2) * 384:(i % 2 + 1) * 384] for c in range(2))
                    split_item(m + i, lo, bank(m + i)[:, 0:384], hi, eager=False)

                for step, pr in MLA_ORDER:
                    if step == "score":
                        s1, s0 = mla_scores(pr)
                        ahead(("score", l, pr))
                        dve.wait_ge(pe_done, done["score", l, pr])
                        maxima(5 * l + pr, [s1, s0], [s1[0:CHUNK, :, P + CHUNK:2 * P], s0[0:CHUNK, :, CHUNK:P]],
                               MLA_SCALE)
                    elif step == "scale":
                        p1, p0 = mla_probs(pr)
                        scale_probs(5 * l + pr, [p1[:, 0, :], p1[:, 1, :], p0[:, 0, :], p0[:, 1, :]])
                    elif step == "pt":
                        m, pT = plan["pt", l, pr]["items"], turned_probs[pr]
                        for e in range(2):
                            split_item(m + e, pT[:, e, 1, :], bank(m + e)[:, 0:384], pT[:, e, 0, :])
                    elif step == "pv":
                        split_tiles(("pv", l, pr), mixT[:, 2 + 2 * pr:4 + 2 * pr])
                    elif step == "fill":
                        fill(l, pr)

            def memory(l):
                split_tiles(("wq", l), qT[:, 0:8])
                for step, i in MEM_ORDER:
                    if step == "score":
                        ahead(("mscore", l, i))
                        dve.wait_ge(pe_done, done["mscore", l, i])
                        maxima(5 * l + PAIRS + i, [mem_scores(i)], [], MEM_SCALE)
                    elif step == "scale":
                        scale_probs(5 * l + PAIRS + i, [mem_probs(i)[:, hh, :] for hh in range(MEM_HEADS)])
                    elif step == "pt":
                        split_tiles(("mpt", l, i), mpT[:, 2 * i:2 * i + 2])
                    elif step == "pv":
                        split_tiles(("mpv", l, i), mixT[:, 2 * i:2 * i + 2])
                    elif step == "fill":
                        fill(l, i)

            turn(1, xT)
            for l in range(L):
                ffn(l, 0)
                norm(4 * l, l, "ln0")
                if l == 0:
                    dve.wait_ge(small_landed, 16 * SMALL)
                mix(l)
                norm(4 * l + 1, l, "ln1")
                memory(l)
                norm(4 * l + 2, l, "ln2")
                ffn(l, 1)
                norm(4 * l + 3, l, "ln3") if l < L - 1 else norm(4 * l + 3)

        @block.gpsimd
        def _(pool):
            steps = [0]

            def own(ins):
                steps[0] += 1
                ins.then_inc(pool_step, 1)
                pool.wait_ge(pool_step, steps[0])

            def load_gains(e):
                for i, w in enumerate(("ln_g", "ln_b")):
                    pool.dma_start(gb[:, i, :], a[w][e // 4, e % 4:e % 4 + 1, :].partition_broadcast(P))\
                        .then_inc(gains_landed, 16)

            def scale_x(job, e):
                for b in range(TB):
                    pool.wait_ge(pe_done, done["turned", job + b, 1])
                    nc.gpsimd.tensor_scalar(x[:, b, :], x[:, b, :], ALPHA, 1.0, ALU.mult, ALU.mult)\
                        .then_inc(x_scaled, 1)

            def turn(job, dst):
                for c in range(HALVES):
                    pool.wait_ge(turned_plain, turned_lo_value(job, c))
                    nc.gpsimd.tensor_tensor(half_T(dst, 1, 0, c), plain_half(job, c),
                                            half_T(dst, 0, 0, c).bitcast(F32), ALU.subtract).then_inc(turned_lo[0], 1)

            def norm(e):
                for b in range(TB):
                    pool.wait_ge(var_ready, 2 * e + b + 1)
                    nc.gpsimd.tensor_tensor(RSTD[b], VEPS[b], cst[:, C_HALF:C_HALF + 1], ALU.pow)\
                        .then_inc(rstd_ready, 1)
                if e < 4 * L - 1:
                    turn(4 + 2 * e, xT)
                    if e % 4:
                        pool.wait_ge(norm_done, normed(e, 1, 1))
                        load_gains(e + 1)
                    scale_x(4 + 2 * e, e)

            def rope_angles():
                pool.wait_ge(consts_landed, 16)
                pool.wait_ge(pos_landed, 16)
                ang, turns, part_of = gb[:, 0, 2 * S:3 * S], gb[:, 0, 3 * S:4 * S], gb[:, 1, S:2 * S]
                own(nc.gpsimd.tensor_copy(ang, gb[:, 1, 0:S].bitcast(I32)))
                own(nc.gpsimd.tensor_scalar(ang, ang, cst[:, C_FREQ:C_FREQ + 1], None, ALU.mult))
                for i, quarter in enumerate((0.25, 0.0)):
                    r = gb[:, 0, i * S:(i + 1) * S]
                    own(nc.gpsimd.tensor_scalar(turns, ang, 1.0 / (2.0 * math.pi), quarter, ALU.mult, ALU.add))
                    own(nc.gpsimd.tensor_scalar(turns, turns, ROUND, None, ALU.add))
                    own(nc.gpsimd.tensor_scalar(turns, turns, ROUND, None, ALU.subtract))
                    for k, part in enumerate(TURN):
                        own(nc.gpsimd.tensor_scalar(part_of, turns, part, None, ALU.mult))
                        own(nc.gpsimd.tensor_tensor(r, ang if k == 0 else r, part_of, ALU.subtract))
                    own(nc.gpsimd.tensor_scalar(r, r, quarter * 2.0 * math.pi, PI_IN, ALU.add, ALU.min))
                    nc.gpsimd.tensor_scalar(r, r, -PI_IN, None, ALU.max).then_inc(angles_ready, 1)

            def pool_group(l):
                pool.wait_ge(bank_free, plan["win", l]["items"] + 3)
                src = poolU
                for i, shift in enumerate((1, 2, 4, 8)):
                    dst = (poolA, poolB)[i % 2]
                    own(nc.gpsimd.tensor_tensor(dst[:, :, shift:S], src[:, :, shift:S], src[:, :, 0:S - shift],
                                                ALU.add))
                    own(nc.gpsimd.tensor_copy(dst[:, :, 0:shift], src[:, :, 0:shift]))
                    keep = ((0, 0), (64, 0), (0, 1), (64, 1))[i]
                    rows = slice(keep[0], keep[0] + 64)
                    own(nc.gpsimd.tensor_copy(poolM[rows, keep[1], :], dst[rows, keep[1], :]))
                    src = dst
                own(nc.gpsimd.tensor_tensor(poolM[:, :, :], poolM[:, :, :], inv_count, ALU.mult))
                nc.gpsimd.tensor_tensor(poolB, poolM[:, :, :], poolU, ALU.subtract).then_inc(pooled, 1)

            pool.dma_start(gb[:, 1, 0:S].bitcast(I32), a["positions"].partition_broadcast(P)).then_inc(pos_landed, 16)
            turn(0, xT)
            own(nc.gpsimd.memset(pw[:, :, :, :], 0.0))
            scale_x(0, -1)
            turn(2, memT)
            rope_angles()
            for l in range(L):
                for g in range(len(POOL_WINDOWS)):
                    rows = slice((g % 2) * 64, (g % 2 + 1) * 64)
                    pool.dma_start(pw[rows, l, g // 2, rows], a["pool_w"][l, g]).then_inc(small_landed, 16)
                for dst, w, t in ((gains[:, l, 0:1], "q_norm_g", 0), (gains[:, l, 1:2], "q_norm_g", 1),
                                  (gains[:, l, 2:3], "kv_norm_g", 0), (pscale[:, l, 0:1], "pool_scale", 0),
                                  (pscale[:, l, 1:2], "pool_scale", 1)):
                    pool.dma_start(dst, a[w][l, t * P:(t + 1) * P].rearrange("(p o) -> p o", o=1))\
                        .then_inc(small_landed, 16)
            pool.wait_ge(tables_done, 1)
            load_gains(0)
            for l in range(L):
                norm(4 * l)
                pool.wait_ge(bank_free, plan["sums", l]["items"] + 1)
                nc.gpsimd.tensor_tensor(RMS, MS, cst[:, C_HALF:C_HALF + 1].broadcast_to([P, 4]), ALU.pow)\
                    .then_inc(rms_ready, 1)
                pool_group(l)
                pool.wait_ge(pe_done, done["item", plan["rot", l]["items"] + 1])
                nc.gpsimd.tensor_tensor(ropeX, ropeX, cosT[:, :].unsqueeze(1).broadcast_to([P, 4, S]), ALU.mult)\
                    .then_inc(rope_cos, 1)
                pool.wait_ge(bank_free, plan["pool", l]["items"] + 1)
                load_gains(4 * l + 1)
                for s in range(1, 4):
                    norm(4 * l + s)


_INS = ["x", "mem", "positions", "ln_g", "ln_b", "ffn1_w13", "ffn1_w2", "w_in", "pool_w", "pool_scale",
        "q_norm_g", "w_uq", "kv_norm_g", "w_ukv", "w_out", "mem_wq", "mem_wkv", "mem_wo", "ffn2_w13", "ffn2_w2"]


def kernel(**inputs):
    import concourse.bacc as bacc
    from concourse.bass_utils import run_bass_kernel_spmd

    nc = bacc.Bacc("TRN2", target_bir_lowering=False, num_devices=1)
    arrays = {f"in_{n}": np.ascontiguousarray(inputs[n]) for n in _INS}
    arrays["in_constants"] = constants(inputs["x"].shape[1])
    aps = {n: nc.dram_tensor(n, v.shape, mybir.dt.from_np(v.dtype), kind="ExternalInput").ap()
           for n, v in arrays.items()}
    out = nc.dram_tensor("out_0", inputs["x"].shape, F32, kind="ExternalOutput").ap()
    trunk(nc, {n: aps[f"in_{n}"] for n in _INS}, aps["in_constants"], out)
    r = run_bass_kernel_spmd(nc, [arrays], core_ids=[0])
    return r.results[0]["out_0"]
```
